# Optimizing a Trainium2 kernel written in Bass

```python
import jax, jax.numpy as jnp
from jax import lax
import numpy as np

D_MODEL = 2048
BATCH = 1
SEQ = 512
DEPTH = 2
DEC_BATCH = 8
DEC_SEQ = 8
PAST_LEN = 2048
PAGE_SIZE = 128

A_HEADS = 16
A_KV_HEADS = 2
A_GROUP = A_HEADS // A_KV_HEADS
A_HEAD_DIM = 64
A_WIDTH = A_HEADS * A_HEAD_DIM
A_KV_WIDTH = A_KV_HEADS * A_HEAD_DIM
WINDOW = 128
CHUNK = 128
B_GROUPS = 4
B_WIDTH = D_MODEL - A_WIDTH
B_GROUP_DIM = B_WIDTH // B_GROUPS
EVEN_IN = 2 * A_WIDTH + 2 * A_KV_WIDTH + 3 * B_WIDTH
EVEN_OUT = A_WIDTH + B_WIDTH
R_HEADS = 8
R_KEY_DIM = D_MODEL // R_HEADS
R_VAL_DIM = 2 * R_KEY_DIM
R_K_WIDTH = R_HEADS * R_KEY_DIM
R_V_WIDTH = R_HEADS * R_VAL_DIM
R_CHUNK = 128
RET_IN = 2 * R_K_WIDTH + 2 * R_V_WIDTH
MEM_LEN = 256
X_HEADS = 4
X_HEAD_DIM = 128
X_WIDTH = X_HEADS * X_HEAD_DIM

N_ATTN_LAYERS = (DEPTH + 1) // 2
N_RET_LAYERS = DEPTH // 2
EPS = 1e-6
NEG_INF = -1e30
F32 = jnp.float32

kernel_name = 'hybrid_swa_gmlp_retention_step'

def rmsnorm(x, g):
    x32 = x.astype(F32)
    y = x32 * lax.rsqrt(jnp.mean(x32 * x32, axis=-1, keepdims=True) + EPS)
    return (y * g.astype(F32)).astype(x.dtype)

def standardize(x):
    x32 = x.astype(F32)
    xc = x32 - jnp.mean(x32, axis=-1, keepdims=True)
    return xc * lax.rsqrt(jnp.mean(xc * xc, axis=-1, keepdims=True) + EPS)

def alibi_slopes():
    return jnp.exp2(-8.0 * (jnp.arange(A_HEADS, dtype=F32) + 1.0) / A_HEADS)

def retention_log_decay():
    return jnp.log1p(-jnp.exp2(-5.0 - jnp.arange(R_HEADS, dtype=F32)))

def sink_window_attention(q, k, v, q_pos, k_pos, sinks):
    s = jnp.einsum('bnqkgd,bnskd->bnkgqs', q.astype(F32), k.astype(F32)) * (A_HEAD_DIM ** -0.5)
    dist = q_pos[:, :, None] - k_pos[:, None, :]
    valid = (dist >= 0) & (dist < WINDOW) & (k_pos[:, None, :] >= 0)
    slopes = alibi_slopes().reshape(A_KV_HEADS, A_GROUP)[None, None, :, :, None, None]
    s = jnp.where(valid[None, :, None, None], s - slopes * dist.astype(F32)[None, :, None, None], NEG_INF)
    sink = sinks.astype(F32).reshape(A_KV_HEADS, A_GROUP)[None, None, :, :, None, None]
    m = jnp.maximum(jnp.max(s, axis=-1, keepdims=True), sink)
    p = jnp.exp(s - m)
    denom = jnp.sum(p, axis=-1, keepdims=True) + jnp.exp(sink - m)
    return jnp.einsum('bnkgqs,bnskd->bnqkgd', p / denom, v.astype(F32))

def spatial_gate(u, v, w_s, b_s):
    tc = v.shape[2]
    causal = jnp.tril(jnp.ones((tc, tc), dtype=bool))
    ws = jnp.where(causal[None], w_s[:, :tc, :tc].astype(F32), 0.0)
    mixed = jnp.einsum('gij,bnjgc->bnigc', ws, v.astype(F32)) + b_s[:, :tc].astype(F32).T[:, :, None]
    return u.astype(F32) * mixed

def split_even(z):
    sizes = (A_WIDTH, A_KV_WIDTH, A_KV_WIDTH, A_WIDTH, B_WIDTH, B_WIDTH, B_WIDTH)
    idx = [int(i) for i in np.cumsum(sizes)[:-1]]
    return jnp.split(z, idx, axis=-1)

def even_output(x, a, ga, bo, gb, w_out):
    mixed = jnp.concatenate([jax.nn.silu(ga.astype(F32)) * a, jax.nn.silu(gb.astype(F32)) * bo], axis=-1)
    return x + mixed.astype(x.dtype) @ w_out

def shift_band(t):
    prev = jnp.concatenate([jnp.zeros_like(t[:, :1]), t[:, :-1]], axis=1)
    return jnp.concatenate([prev, t], axis=2)

def even_layer_prompt(x, g_mix, w_in, sinks, w_s, b_s, lnv_g, lnv_b, w_out):
    bsz, seq, _ = x.shape
    q, k, v, ga, u, vb, gb = split_even(rmsnorm(x, g_mix) @ w_in)
    nb = seq // WINDOW
    k = k.reshape(bsz, seq, A_KV_HEADS, A_HEAD_DIM)
    v = v.reshape(bsz, seq, A_KV_HEADS, A_HEAD_DIM)
    kb = shift_band(k.reshape(bsz, nb, WINDOW, A_KV_HEADS, A_HEAD_DIM))
    vbk = shift_band(v.reshape(bsz, nb, WINDOW, A_KV_HEADS, A_HEAD_DIM))
    pos = jnp.arange(seq, dtype=jnp.int32).reshape(nb, WINDOW)
    k_pos = jnp.concatenate([pos - WINDOW, pos], axis=1)
    qb = q.reshape(bsz, nb, WINDOW, A_KV_HEADS, A_GROUP, A_HEAD_DIM)
    a = sink_window_attention(qb, kb, vbk, pos, k_pos, sinks).reshape(bsz, seq, A_WIDTH)
    vn = standardize(vb) * lnv_g.astype(F32) + lnv_b.astype(F32)
    gshape = (bsz, seq // CHUNK, CHUNK, B_GROUPS, B_GROUP_DIM)
    bo = spatial_gate(u.reshape(gshape), vn.reshape(gshape), w_s, b_s).reshape(bsz, seq, B_WIDTH)
    return even_output(x, a, ga, bo, gb, w_out), k[:, -WINDOW:], v[:, -WINDOW:]

def even_layer_sample(x, win_k, win_v, g_mix, w_in, sinks, w_s, b_s, lnv_g, lnv_b, w_out):
    bsz, t, _ = x.shape
    q, k, v, ga, u, vb, gb = split_even(rmsnorm(x, g_mix) @ w_in)
    kk = jnp.concatenate([win_k.astype(x.dtype), k.reshape(bsz, t, A_KV_HEADS, A_HEAD_DIM)], axis=1)
    vv = jnp.concatenate([win_v.astype(x.dtype), v.reshape(bsz, t, A_KV_HEADS, A_HEAD_DIM)], axis=1)
    q_pos = (PAST_LEN + jnp.arange(t, dtype=jnp.int32))[None]
    k_pos = (PAST_LEN - WINDOW + jnp.arange(WINDOW + t, dtype=jnp.int32))[None]
    qb = q.reshape(bsz, 1, t, A_KV_HEADS, A_GROUP, A_HEAD_DIM)
    a = sink_window_attention(qb, kk[:, None], vv[:, None], q_pos, k_pos, sinks).reshape(bsz, t, A_WIDTH)
    vn = standardize(vb) * lnv_g.astype(F32) + lnv_b.astype(F32)
    gshape = (bsz, 1, t, B_GROUPS, B_GROUP_DIM)
    bo = spatial_gate(u.reshape(gshape), vn.reshape(gshape), w_s, b_s).reshape(bsz, t, B_WIDTH)
    y = even_output(x, a, ga, bo, gb, w_out)
    return y, kk[:, -WINDOW:], vv[:, -WINDOW:], vn.astype(x.dtype)

def retention_chunk(state, q, k, v, log_g):
    t = q.shape[1]
    i = jnp.arange(t, dtype=F32)
    rel = i[:, None] - i[None, :]
    decay = jnp.where(rel[None] >= 0, jnp.exp(jnp.maximum(rel, 0.0)[None] * log_g[:, None, None]), 0.0)
    scores = jnp.einsum('bthd,bshd->bhts', q, k) * decay[None]
    inner = jnp.einsum('bhts,bshe->bthe', scores, v)
    q_decay = jnp.exp((i[:, None] + 1.0) * log_g[None, :])
    cross = jnp.einsum('bthd,bhde->bthe', q * q_decay[None, :, :, None], state)
    k_decay = jnp.exp((t - 1.0 - i)[:, None] * log_g[None, :])
    new_state = jnp.exp(t * log_g)[None, :, None, None] * state + jnp.einsum('bshd,bshe->bhde', k * k_decay[None, :, :, None], v)
    return new_state, inner + cross

def split_ret(z, bsz, t):
    q, k, v, g = jnp.split(z, [R_K_WIDTH, 2 * R_K_WIDTH, 2 * R_K_WIDTH + R_V_WIDTH], axis=-1)
    q = q.reshape(bsz, t, R_HEADS, R_KEY_DIM).astype(F32)
    k = k.reshape(bsz, t, R_HEADS, R_KEY_DIM).astype(F32) * (R_KEY_DIM ** -0.5)
    v = v.reshape(bsz, t, R_HEADS, R_VAL_DIM).astype(F32)
    return q, k, v, g

def ret_output(x, o, g, w_out):
    bsz, t = x.shape[0], x.shape[1]
    on = standardize(o).reshape(bsz, t, R_V_WIDTH)
    return x + (jax.nn.silu(g.astype(F32)) * on).astype(x.dtype) @ w_out

def odd_layer_prompt(x, g_mix, w_in, w_out):
    bsz, seq, _ = x.shape
    q, k, v, g = split_ret(rmsnorm(x, g_mix) @ w_in, bsz, seq)
    log_g = retention_log_decay()
    nc = seq // R_CHUNK

    def to_chunks(a):
        return a.reshape(bsz, nc, R_CHUNK, a.shape[2], a.shape[3]).swapaxes(0, 1)

    def step(state, qkv):
        qc, kc, vc = qkv
        return retention_chunk(state, qc, kc, vc, log_g)

    state0 = jnp.zeros((bsz, R_HEADS, R_KEY_DIM, R_VAL_DIM), F32)
    state, o = lax.scan(step, state0, (to_chunks(q), to_chunks(k), to_chunks(v)))
    o = o.swapaxes(0, 1).reshape(bsz, seq, R_HEADS, R_VAL_DIM)
    return ret_output(x, o, g, w_out), state.astype(x.dtype)

def odd_layer_sample(x, state, g_mix, w_in, w_out):
    bsz, t, _ = x.shape
    q, k, v, g = split_ret(rmsnorm(x, g_mix) @ w_in, bsz, t)
    new_state, o = retention_chunk(state.astype(F32), q, k, v, retention_log_decay())
    return ret_output(x, o, g, w_out), new_state.astype(state.dtype)

def memory_kv(mem, g_mem, w_k, w_v):
    bsz, m, _ = mem.shape
    h = rmsnorm(mem, g_mem)
    return (h @ w_k).reshape(bsz, m, X_HEADS, X_HEAD_DIM), (h @ w_v).reshape(bsz, m, X_HEADS, X_HEAD_DIM)

def cross_attend(x, g, w_q, w_o, mem_k, mem_v):
    bsz, t, _ = x.shape
    q = (rmsnorm(x, g) @ w_q).reshape(bsz, t, X_HEADS, X_HEAD_DIM)
    s = jnp.einsum('bthd,bmhd->bhtm', q.astype(F32), mem_k.astype(F32)) * (X_HEAD_DIM ** -0.5)
    p = jax.nn.softmax(s, axis=-1)
    o = jnp.einsum('bhtm,bmhd->bthd', p, mem_v.astype(F32)).reshape(bsz, t, X_WIDTH)
    return x + o.astype(x.dtype) @ w_o

def setup_inputs(seed: int = 0) -> dict:
    key = jax.random.key(seed)
    ks = iter(jax.random.split(key, 32))

    def nrm(shape, scale):
        return scale * jax.random.normal(next(ks), shape, F32)

    na, nr = N_ATTN_LAYERS, N_RET_LAYERS
    return {
        'x_prompt': nrm((BATCH, SEQ, D_MODEL), 1.0),
        'x_sample': nrm((DEC_BATCH, DEC_SEQ, D_MODEL), 1.0),
        'cache_win_k': nrm((na, DEC_BATCH, WINDOW, A_KV_HEADS, A_HEAD_DIM), 1.0),
        'cache_win_v': nrm((na, DEC_BATCH, WINDOW, A_KV_HEADS, A_HEAD_DIM), 1.0),
        'state_ret': nrm((nr, DEC_BATCH, R_HEADS, R_KEY_DIM, R_VAL_DIM), 0.3),
        'cache_mem_k': nrm((DEPTH, DEC_BATCH, MEM_LEN, X_HEADS, X_HEAD_DIM), 1.0),
        'cache_mem_v': nrm((DEPTH, DEC_BATCH, MEM_LEN, X_HEADS, X_HEAD_DIM), 1.0),
        'mem_prompt': nrm((BATCH, MEM_LEN, D_MODEL), 1.0),
        'norm_mix': 1.0 + nrm((DEPTH, D_MODEL), 0.02),
        'w_in_even': nrm((na, D_MODEL, EVEN_IN), D_MODEL ** -0.5),
        'attn_sinks': nrm((na, A_HEADS), 1.0),
        'w_spatial': nrm((na, B_GROUPS, CHUNK, CHUNK), CHUNK ** -0.5),
        'b_spatial': 1.0 + nrm((na, B_GROUPS, CHUNK), 0.1),
        'norm_v_g': 1.0 + nrm((na, B_WIDTH), 0.02),
        'norm_v_b': nrm((na, B_WIDTH), 0.02),
        'w_out_even': nrm((na, EVEN_OUT, D_MODEL), EVEN_OUT ** -0.5),
        'w_in_ret': nrm((nr, D_MODEL, RET_IN), D_MODEL ** -0.5),
        'w_out_ret': nrm((nr, R_V_WIDTH, D_MODEL), R_V_WIDTH ** -0.5),
        'norm_cross': 1.0 + nrm((DEPTH, D_MODEL), 0.02),
        'norm_mem': 1.0 + nrm((DEPTH, D_MODEL), 0.02),
        'w_xq': nrm((DEPTH, D_MODEL, X_WIDTH), D_MODEL ** -0.5),
        'w_xk': nrm((DEPTH, D_MODEL, X_WIDTH), D_MODEL ** -0.5),
        'w_xv': nrm((DEPTH, D_MODEL, X_WIDTH), D_MODEL ** -0.5),
        'w_xo': nrm((DEPTH, X_WIDTH, D_MODEL), X_WIDTH ** -0.5),
        'norm_final': 1.0 + nrm((D_MODEL,), 0.02),
    }

def reference(x_prompt, x_sample, cache_win_k, cache_win_v, state_ret, cache_mem_k, cache_mem_v, mem_prompt,
              norm_mix, w_in_even, attn_sinks, w_spatial, b_spatial, norm_v_g, norm_v_b, w_out_even,
              w_in_ret, w_out_ret, norm_cross, norm_mem, w_xq, w_xk, w_xv, w_xo, norm_final):
    xp, xs = x_prompt, x_sample
    wkp, wvp, rsp, mkp, mvp = [], [], [], [], []
    wks, wvs, rss, cvs = [], [], [], []
    for layer in range(DEPTH):
        i = layer // 2
        if layer % 2 == 0:
            params = (norm_mix[layer], w_in_even[i], attn_sinks[i], w_spatial[i], b_spatial[i],
                      norm_v_g[i], norm_v_b[i], w_out_even[i])
            xp, kp, vp = even_layer_prompt(xp, *params)
            xs, ksn, vsn, cv = even_layer_sample(xs, cache_win_k[i], cache_win_v[i], *params)
            wkp.append(kp)
            wvp.append(vp)
            wks.append(ksn)
            wvs.append(vsn)
            cvs.append(cv)
        else:
            xp, sp = odd_layer_prompt(xp, norm_mix[layer], w_in_ret[i], w_out_ret[i])
            xs, ss = odd_layer_sample(xs, state_ret[i], norm_mix[layer], w_in_ret[i], w_out_ret[i])
            rsp.append(sp)
            rss.append(ss)
        mk, mv = memory_kv(mem_prompt, norm_mem[layer], w_xk[layer], w_xv[layer])
        mkp.append(mk)
        mvp.append(mv)
        xp = cross_attend(xp, norm_cross[layer], w_xq[layer], w_xo[layer], mk, mv)
        xs = cross_attend(xs, norm_cross[layer], w_xq[layer], w_xo[layer], cache_mem_k[layer], cache_mem_v[layer])
    y_prompt = rmsnorm(xp, norm_final)
    y_sample = rmsnorm(xs, norm_final)
    return (y_prompt, y_sample,
            jnp.stack(wkp), jnp.stack(wvp), jnp.stack(rsp), jnp.stack(mkp), jnp.stack(mvp),
            jnp.stack(wks), jnp.stack(wvs), jnp.stack(rss), jnp.stack(cvs))


_drawn_inputs = setup_inputs


def setup_inputs(seed=0):
    import zlib

    import numpy as np

    out = dict(_drawn_inputs(seed))
    spreads = {}
    factors = {'norm_v_g': 2.741,
     'norm_v_b': 2.874,
     'norm_cross': 8.0,
     'norm_mem': 2.803,
     'norm_final': 2.838}
    for name, (base, spread) in spreads.items():
        noise = np.random.default_rng([zlib.crc32(name.encode()), seed]).standard_normal(out[name].shape)
        drawn = base * np.exp(spread * noise) if base else spread * noise
        out[name] = __import__('jax').numpy.asarray(drawn.astype(out[name].dtype))
    for name, factor in factors.items():
        out[name] = (out[name] * factor).astype(out[name].dtype)
    return out
```

```python
from contextlib import ExitStack

import numpy as np

import concourse.bass as bass
from concourse import mybir

F32 = mybir.dt.float32
F32R = mybir.dt.float32r
ALU = mybir.AluOpType
ACT = mybir.ActivationFunctionType
AXX = mybir.AxisListType.X

P = 128
D = 2048
KT = D // P
SEQ = 512
DEC_B, DEC_T = 8, 8
NS = DEC_B * DEC_T
NT = SEQ // P
AH, AD, AG = 16, 64, 8
AW = AH * AD
WIN = 128
BW = D - AW
BG = 4
EVEN_IN = 2 * AW + 2 * 128 + 3 * BW
RH, RK, RV = 8, 256, 512
XH, XD, MEM = 4, 128, 256
XW = XH * XD
EPS = 1e-6
CW = 512
GK = 2
GPC = KT // GK
RING = 4
PT = NT + 1
MASKED = -1e33

CONSTS = dict(ident=128, dist=256, slope=16, sbias=128, strip=120, tril=128, smask=64, qd=16, qd2=16, kd=8, kz=64, gp=16)
COFF = {}
_o = 0
for _n, _w in CONSTS.items():
    COFF[_n] = (_o, _w)
    _o += _w
NCONST = _o


def shape_constants():
    c = np.zeros((P, NCONST), np.float32)

    def put(name, a):
        o, w = COFF[name]
        c[:a.shape[0], o:o + w] = a.reshape(a.shape[0], w)

    i = np.arange(P)
    put("ident", np.eye(P))
    dist = i[:, None] + WIN - np.arange(2 * WIN)[None]
    put("dist", np.where((dist >= 0) & (dist < WIN), -dist.astype(np.float64), MASKED))
    slopes = np.exp2(-8.0 * (np.arange(AH) + 1.0) / AH)
    put("slope", np.tile(slopes, (P, 1)))
    row_t = i % DEC_T
    row_slope = slopes[(i // 64) * AG + (i % 64) // DEC_T][:, None]
    d = WIN + row_t[:, None] - np.arange(WIN)[None]
    put("sbias", np.where(d < WIN, -d * row_slope, MASKED))
    x = np.arange(120)[None] - 56
    dn = row_t[:, None] - x
    put("strip", np.where((x >= 0) & (x < DEC_T) & (dn >= 0), -dn * row_slope, MASKED))
    put("tril", (i[None] <= i[:, None]).astype(np.float64))
    s = np.arange(NS)
    same = (s[:, None] // DEC_T) == (s[None] // DEC_T)
    put("smask", (same & (s[:, None] % DEC_T <= s[None] % DEC_T)).astype(np.float64))
    g = 1.0 - np.exp2(-5.0 - np.arange(RH))
    qd = np.zeros((P, 16))
    qd[:, :8] = g[None] ** (i[:, None] + 1)
    qd[:, 8:] = g[None] ** (row_t[:, None] + 1)
    put("qd", qd)
    put("qd2", qd ** 2)
    put("kd", g[None] ** (P - 1 - i[:, None]) * RK ** -0.5)
    kz = np.zeros((NS, RH, DEC_B))
    kz[s, :, s // DEC_T] = g[None] ** (DEC_T - 1 - s[:, None] % DEC_T) * RK ** -0.5
    put("kz", kz)
    put("gp", np.tile(np.concatenate([g ** P, g ** DEC_T]), (P, 1)))
    rdec = np.zeros((RH, P, P + NS), np.float32)
    rdec[:, :, :P] = np.where(i[None, :, None] <= i[None, None], g[:, None, None] ** (-i[None, :, None] - 1.0), 0) * RK ** -0.5
    rdec[:, :NS, P:] = np.where((same & (s[:, None] % DEC_T <= s[None] % DEC_T))[None],
                                g[:, None, None] ** (-(s % DEC_T)[None, :, None] - 1.0), 0) * RK ** -0.5
    zmask = np.zeros((P, DEC_B, NS), np.float32)
    for b in range(DEC_B):
        zmask[:, b, b * DEC_T:(b + 1) * DEC_T] = 1.0
    return c, rdec, zmask.reshape(P, DEC_B * NS)


class Bag:
    pass


class Lin:

    def __init__(self, c, k=0, i=0):
        self.c, self.k, self.i = c, k, i

    def at(self, d=0):
        return self.c + d + (self.k * self.i if self.k else 0)

    def quarter(self, d=0):
        return (self.c + d) // RING + ((self.k // RING) * self.i if self.k else 0)


class BankPlan:

    def __init__(self):
        self.uses, self.fulls, self.where = [0] * 8, [0] * 8, {}

    def add(self, stage, names, trips=1):
        u, f = [0] * 8, [0] * 8
        mine = []
        for name, bank, signals in names:
            mine.append((name, bank, self.uses[bank] + u[bank], self.fulls[bank] + f[bank]))
            u[bank] += 1
            f[bank] += signals
        for name, bank, n, m in mine:
            self.where[stage, name] = (bank, n, u[bank], m, f[bank])
        for b in range(8):
            self.uses[b] += trips * u[b]
            self.fulls[b] += trips * f[b]


def acc_uses(tag, tiles):
    return [((tag, t), t, t != tiles[-1]) for t in tiles]


ALL = list(range(NT + 1))

E_POINTS = [(2, "qT"), (6, "Kb"), (10, "Ss"), (17, "pTs"), (25, "PVs")] + \
    [(7 + 8 * b, f"QK{b}") for b in range(NT)] + [(11 + 8 * b, f"pT{b}") for b in range(NT)] + \
    [(13 + 8 * b, f"PV{b}") for b in range(NT)]
E_POINTS.sort()
E_BANK = dict(qT=5, Kb=7, Ss=7, pTs=7, PVs=7, QK=5, pT=6, PV=7)
RB_POINTS = [(2 + 4 * c, f"T{c}") for c in range(NT)] + [(5 + 4 * c, f"ST{c}") for c in range(NT)] + [(18, "T4"), (22, "ST4")]
RC_POINTS = [(2, "OI")] + [(4 + 9 * c, f"O{c}") for c in range(NT)] + \
    [(5 + 9 * c, f"U{c}0") for c in range(NT)] + [(7 + 9 * c, f"U{c}1") for c in range(NT)] + \
    [(p, f"W{b}0") for b, p in enumerate((3, 8, 12, 17, 21, 26, 30, 35))] + \
    [(p + 1, f"W{b}1") for b, p in enumerate((3, 8, 12, 17, 21, 26, 30, 35))]
RC_DRAINS = [(p + 3 if n[0] == "O" else p, n) for p, n in RC_POINTS]
RA_POINTS = [(4, "M00"), (8, "M01"), (12, "M02"), (18, "M10"), (22, "M11"), (26, "M12")]
RZ_POINTS = [(2 + 3 * n, name) for n, (_, name) in enumerate(RA_POINTS)]
for _l in (RB_POINTS, RC_POINTS, RC_DRAINS, RA_POINTS):
    _l.sort()


def r_bank(name):
    return {"T": 5, "S": 6, "O": 6, "U": 7, "W": 7, "M": 5 + (name[-1] == "1")}[name[0]]


def make_plan():
    plan = BankPlan()
    plan.groups = {}
    plan.xt, plan.st = {}, {}
    state = Bag()
    state.g, state.xt, state.st, state.hi = 0, 0, 0, 0

    def weights(stage, chunks):
        plan.groups[stage] = state.g
        state.g += GPC * chunks

    def xt(stage, batches):
        plan.xt[stage] = state.xt
        for n in range(batches):
            plan.add(stage, [(("xt", n), 5 + (state.xt + n) % 2, True)])
        highs(stage, batches)
        state.xt += batches

    plan.hi = {}

    def highs(stage, n):
        plan.hi[stage] = state.hi
        state.hi += n

    def sqrt(stage, n):
        plan.st[stage] = state.st
        state.st += n

    sqrt("mem", 1)
    xt("mem", 16)
    weights("mem", 4)
    for c in range(4):
        plan.add("mem", acc_uses(c, [2 * (c // 2), 2 * (c // 2) + 1]))
    sqrt("n0", 1)
    xt("n0", 18)
    weights("even", 11)
    plan.add("kvq", [(n, b, s) for c in range(3) for n, b, s in acc_uses(c, ALL)])
    plan.add("epre", [("kT", 5, True), ("kTs", 6, True), ("qTs", 7, True), ("wsT", 5, True)])
    for pair in range(4):
        plan.add(f"pair{pair}", [(n, E_BANK[n.rstrip("0123")], True) for _, n in E_POINTS] + acc_uses("acc", ALL), trips=2)
        if pair == 0:
            sqrt("ln", 1)
            plan.add("mixv", [((t, q), 5 + q, True) for t in ALL for q in range(2)])
    plan.add("epost", [("o0", 5, True), ("o1", 6, True)])
    xt("zt", 18)
    weights("eout", 4)
    plan.add("eout", acc_uses("acc", ALL), trips=4)
    for layer in range(2):
        s = f"x{layer}"
        sqrt(s, 1)
        xt(s, 18)
        weights(s + "q", 1)
        plan.add(s, acc_uses("acc", ALL))
        plan.add(s, [("kT0", 5, True), ("kT1", 6, True)] + [(f"qT{t}", 5 + t % 2, True) for t in ALL])
        order = [(f"S0{q}", q, True) for q in range(2)]
        for t in range(NT):
            if t + 1 < NT:
                order += [(f"S{t + 1}{q}", 2 * ((t + 1) % 2) + q, True) for q in range(2)]
            order += [(f"pT{t}0", 5, True), (f"pT{t}1", 6, True), (f"PV{t}", 7, True), (f"oT{t}", 4, True)]
        plan.add(s, order)
        plan.add(s, [(f"K{b}{m}", 5 + m, True) for b in range(DEC_B) for m in range(2)] + [("SS", 7, True)])
        plan.add(s, [("SR", 5, True), ("PR", 6, True), ("OS", 7, True)])
        highs(s + "o", 5)
        weights(s + "o", 1)
        for c in range(4):
            plan.add(s + "o", acc_uses(c, ALL))
        if layer == 0:
            sqrt("n1", 1)
            xt("n1", 18)
            weights("ret", 3 * RH)
            plan.add("retA", acc_uses("acc", ALL))
            body = [(n, r_bank(n), True) for _, n in RB_POINTS] + acc_uses("B", ALL) + \
                [("OI", 5, True)] + [(n, r_bank(n), True) for _, n in RC_POINTS if n != "OI"] + acc_uses("C", ALL) + \
                [(n, r_bank(n), True) for _, n in RA_POINTS]
            plan.add("ret", body + acc_uses("A", ALL), trips=RH - 1)
            plan.add("retZ", body)
            sqrt("gn", RH * 5)
            weights("rout", 8)
            plan.add("rout", acc_uses("acc", ALL), trips=8)
    sqrt("fin", 1)
    plan.total = state.g
    return plan


PLAN = make_plan()


def build(nc, I, O, consts, rdec_d, zmask_d, x_scratch, mix_scratch):
    plan = PLAN
    with ExitStack() as ctx:
        def sb(name, shape, dt=F32):
            return ctx.enter_context(nc.sbuf_tensor(name, shape, dt))

        def sem(name):
            return ctx.enter_context(nc.semaphore(name))

        xh = sb("xT_hi", [P, KT, SEQ], F32R)
        xl = sb("xT_lo", [P, KT, SEQ], F32R)
        xs = sb("xT_sample", [P, KT, 2 * NS], F32R)
        raw = sb("w_raw", [P, RING, GK, CW])
        whi = sb("w_hi", [P, RING, GK, CW], F32R)
        wlo = sb("w_lo", [P, RING, GK, CW], F32R)
        cst = sb("cst", [P, NCONST])
        stat = sb("stat", [P, 96])
        bn = sb("bn", [P, 12])
        R1 = sb("R1", [P, 10240])
        R2 = sb("R2", [P, 14336])
        bank = [ctx.enter_context(nc.psum_tensor(f"bank{b}", [P, 512], F32)) for b in range(8)]

        def C(name, rows=P):
            o, w = COFF[name]
            return cst[0:rows, o:o + w]

        ident = C("ident")

        class Carve:
            def __init__(self, tensor, at=0, size=None):
                self.t, self.at = tensor, at

            def take(self, *shape):
                n = int(np.prod(shape))
                a = self.t[:, self.at:self.at + n]
                self.at += n
                assert self.at <= self.t.shape[1], (self.at, self.t.shape)
                if len(shape) == 2:
                    a = a.rearrange("p (a b) -> p a b", b=shape[1])
                elif len(shape) == 3:
                    a = a.rearrange("p (a b c) -> p a b c", b=shape[1], c=shape[2])
                return a

        X = R2[:, 0:5 * D].rearrange("p (t n) -> p t n", n=D)
        Z = R1[:, 0:5 * D].rearrange("p (t n) -> p t n", n=D)
        c = Carve(R1)
        xn, gbc, junk = c.take(2, D), c.take(D), c.take(D)
        memX = R2[:, 5 * D:7 * D].rearrange("p (t n) -> p t n", n=D)
        memKV = R1[:, 4 * D:5 * D].rearrange("p (c m n) -> p c m n", c=2, m=2)
        c = Carve(R2)
        KV, SG = c.take(5, 256), c.take(5, AW)
        qst, qT, kT = c.take(NT, P), c.take(SEQ), c.take(SEQ + NS)
        S = c.take(2, 260)
        pT, qTs, oTs = c.take(4, P), c.take(DEC_B, 64), c.take(AG, NS)
        qs, kTs, Kraw, Vraw = c.take(64), c.take(WIN + NS), c.take(P), c.take(P)
        Ss, pTs = c.take(196), c.take(2 * P)
        wsT, wsTs = c.take(BG, P), c.take(BG, NS)
        bs, bss, sinkb, sinkr = c.take(BG), c.take(BG), c.take(AH), c.take(1)
        rden = c.take(2, 2)
        shared = c.at
        lng, lnb = c.take(BW), c.take(BW)
        wraw = lng[:, 0:BG * P].rearrange("p (g n) -> p g n", n=P)
        sil = R2[:, shared:shared + 2 * CW].rearrange("p (a n) -> p a n", n=CW)
        sils = R2[:, shared + 2 * CW:shared + 3 * CW]
        c = Carve(R1)
        qc, cqT, ckT, Vm = c.take(5, XW), c.take(XH, SEQ + NS), c.take(XH, MEM), c.take(2, XW)
        Px, cpT, Ox, Sb = c.take(XH, MEM), c.take(8, P), c.take(XW), c.take(CW)
        c = Carve(R2, 5 * D)
        KVb = c.take(4, 2, XW)
        c = Carve(R1)
        QK, V, ON, sg = c.take(5, CW), c.take(5, CW), c.take(5, CW), c.take(2, CW)
        sgs = c.take(CW)
        c = Carve(R2)
        mt, qkT, STm = c.take(GK, SEQ + NS), c.take(4, SEQ + NS), c.take(5, P)
        kdec, rstate, Wst = c.take(2, RK), c.take(2, RV), c.take(4, 2, RV)
        kzb, qz, zm, rdec = c.take(2, RK), c.take(2, DEC_B, NS), c.take(DEC_B, NS), c.take(P + NS)

        raw_loaded = [sem(f"raw_loaded{s}") for s in range(RING)]
        keys_loaded = [sem(f"keys_loaded{s}") for s in range(RING)]
        hi_ready, lo_ready, w_used = sem("hi_ready"), sem("lo_ready"), sem("w_used")
        full = [sem(f"full{b}") for b in range(8)]
        free = [sem(f"free{b}") for b in range(8)]
        waited = sem("waited")
        consts_in, mem_in, x_in, g_in = sem("consts_in"), sem("mem_in"), sem("x_in"), sem("gain_in")
        squares_done, var_ready, std_ready = sem("squares_done"), sem("var_ready"), sem("std_ready")
        xn_ready, xt_hi_ready, stat_zero = sem("xn_ready"), sem("xt_hi_ready"), sem("stat_zero")
        outs_done, x_saved = sem("outs_done"), sem("x_saved")
        mem_stored = [sem(f"mem_stored{n}") for n in range(2)]
        y_out = [sem(f"y_out{n}") for n in range(2)]
        x_done = sem("x_done")
        q_staged, neg_ready, p_ready = sem("q_staged"), sem("neg_ready"), sem("p_ready")
        sneg_ready, sexp_done, sp_ready = sem("sneg_ready"), sem("sexp_done"), sem("sp_ready")
        kb_in, vn_ready, small_in, ln_in = sem("kb_in"), sem("vn_ready"), sem("small_in"), sem("ln_in")
        ws_zeroed, ws_ready, sg_ready = sem("ws_zeroed"), sem("ws_ready"), sem("sg_ready")
        vn_out, z_ready = sem("vn_out"), sem("z_ready")
        sil_ready, gated = sem("sil_ready"), sem("gated")
        cneg, cross_in, cross_sp, vb_used = sem("cross_neg"), sem("cross_in"), sem("cross_sample_p"), sem("vb_used")
        kvb_in = [sem(f"kvb_in{s}") for s in range(4)]
        rd_in, zm_in, kdec_ready, kz_ready, qz_ready = sem("rd_in"), sem("zm_in"), sem("kdec_ready"), sem("kz_ready"), sem("qz_ready")
        state_in = [sem(f"state_in{s}") for s in range(4)]
        state_out = [sem(f"state_out{s}") for s in range(4)]
        mt_out, rstate_out = sem("mt_out"), sem("rstate_out")
        mix_in = [sem(f"mix_in{g}") for g in range(GPC)]
        mix_hi, mix_ready = sem("mix_hi"), sem("mix_ready")

        def is_free(stage, name, i=0):
            b, n, _ = use(stage, name, i)
            return free[b], n + 1

        def is_full(stage, name, i=0):
            b, _, m = use(stage, name, i)
            return full[b], m + 1

        def is_drained(stage, name, i=0):
            b, n, _ = use(stage, name, i)
            return free[b], n + 2

        def was_full(stage, name, i=0):
            b, _, m = use(stage, name, i)
            return full[b], m

        def use(stage, name, i):
            b, n, per, m, fper = plan.where[stage, name]
            if isinstance(i, int):
                return b, n + per * i, m + fper * i
            return b, Lin(n, per, i).at(), Lin(m, fper, i).at()

        def bank_of(stage, name):
            return bank[plan.where[stage, name][0]]

        def FULL(stage, name):
            return full[plan.where[stage, name][0]]

        def FREE(stage, name):
            return free[plan.where[stage, name][0]]

        def rows(t):
            return P if t < NT else NS

        block = ctx.enter_context(nc.Block())

        @block.sync
        def _(sp):
            def group(L, g, w, k0, col, width=CW):
                if not (L.k == 0 and L.c + g < RING):
                    sp.wait_ge(lo_ready, L.at(g - RING + 1))
                src = w.rearrange("(k p) n -> p k n", p=P)[:, k0:k0 + GK, bass.ds(col, width)]
                sp.dma_start(raw[:, g % RING, :, 0:width], src).then_inc(raw_loaded[g % RING], 16)

            def chunk(L, w, col, width=CW, k0=0):
                for g in range(GPC):
                    group(L, g, w, k0 + GK * g, col, width)

            for l in range(2):
                for n, w in enumerate((I.w_xk, I.w_xv)):
                    chunk(Lin(plan.groups["mem"] + GPC * (2 * l + n)), w[l], 0)
            base = plan.groups["even"]
            w = I.w_in_even[0]
            chunk(Lin(base), w, AW, 256)
            with sp.Fori(0, 2) as i:
                chunk(Lin(base + GPC, GPC, i), w, CW * i)
            for pair, col in enumerate((2304 + BW, 1280, 2304, 2304 + 2 * BW)):
                with sp.Fori(0, 2) as i:
                    chunk(Lin(base + GPC * (3 + 2 * pair), GPC, i), w, col + CW * i)
            with sp.Fori(0, 4) as i:
                chunk(Lin(plan.groups["eout"], GPC, i), I.w_out_even[0], CW * i)

            def cross(l):
                chunk(Lin(plan.groups[f"x{l}q"]), I.w_xq[l], 0)
                for n in range(4):
                    for g in range(2):
                        group(Lin(plan.groups[f"x{l}o"]), 2 * n + g, I.w_xo[l], GK * g, CW * n)

            cross(0)
            wr = I.w_in_ret[0]
            base = plan.groups["ret"]

            def chunk_a(L, h):
                for g in range(GPC):
                    sp.wait_ge(lo_ready, L.at(g - RING + 1))
                    for n, loaded in enumerate((raw_loaded, keys_loaded)):
                        src = wr.rearrange("(k p) n -> p k n", p=P)[:, GK * g:GK * g + GK, bass.ds(n * RH * RK + RK * h, RK)]
                        sp.dma_start(raw[:, g % RING, :, n * RK:(n + 1) * RK], src).then_inc(loaded[g % RING], 16)

            def head(h, L):
                chunk(L, wr, 2 * RH * RK + RV * h)
                chunk(Lin(L.c + GPC, L.k, L.i), wr, 2 * RH * RK + RH * RV + RV * h)

            chunk_a(Lin(base), 0)
            with sp.Fori(0, RH - 1) as h:
                head(h, Lin(base + GPC, 3 * GPC, h))
                chunk_a(Lin(base + 3 * GPC, 3 * GPC, h), h + 1)
            head(RH - 1, Lin(base + GPC + 3 * GPC * (RH - 1)))
            for half in range(2):
                with sp.Fori(0, 4) as i:
                    chunk(Lin(plan.groups["rout"] + 4 * GPC * half, GPC, i), I.w_out_ret[0], CW * i, k0=KT * half)
            cross(1)
            for n, t in enumerate(ALL):
                sp.wait_ge(xn_ready, 24 + n + 1)
                dst = O.y_prompt[0, t * P:(t + 1) * P, :] if t < NT else O.y_sample.rearrange("b t d -> (b t) d")
                sp.dma_start(dst, xn[0:rows(t), n % 2]).then_inc(y_out[n % 2], 16)
            for s, n in ((mem_stored[0], 4), (mem_stored[1], 4), (outs_done, 20), (vn_out, 1), (x_saved, 5), (rstate_out, RH), (mt_out, 2 * RH), (y_out[0], 3), (y_out[1], 2)):
                sp.wait_ge(s, 16 * n)
            for s in state_out:
                sp.wait_ge(s, 16 * 2 * RH)

        @block.gpsimd
        def _(pool):
            with pool.Fori(0, plan.total // RING) as i:
                for s in range(RING):
                    pool.wait_ge(hi_ready, RING * i + (s + 1))
                    pool.tensor_tensor(wlo[:, s], raw[:, s], whi[:, s].bitcast(F32), ALU.subtract).then_inc(lo_ready, 1)

        @block.tensor
        def _(pe):
            def gemm(L, stage, tag, i=0, tiles=ALL, width=CW, groups=GPC, g0=0, between=None, parts=(xh, xl)):
                th, tl = parts
                for g in range(groups):
                    slot = (g0 + g) % RING
                    pe.wait_ge(lo_ready, L.at(g0 + g + 1))
                    hi, lo = whi[:, slot], wlo[:, slot]
                    for n, t in enumerate(tiles):
                        if between:
                            between(PT * g + n)
                        if g == 0:
                            pe.wait_ge(*is_free(stage, (tag, t), i))
                        acc = bank[t][:, 0:width]
                        for kk in range(GK):
                            k = GK * g + kk
                            first, last = g == 0 and kk == 0, g == groups - 1 and kk == GK - 1
                            if t < NT:
                                tok = slice(t * P, (t + 1) * P)
                                pe.matmul(acc, th[:, k, tok], hi[:, kk, 0:width], start=first, stop=False)
                                pe.matmul(acc, th[:, k, tok], lo[:, kk, 0:width], start=False, stop=False)
                                mm = pe.matmul(acc, tl[:, k, tok], hi[:, kk, 0:width], start=False, stop=last)
                            else:
                                pe.matmul(acc, xs[:, k, :], hi[:, kk, 0:width], start=first, stop=False)
                                mm = pe.matmul(acc, xs[:, k, :], lo[:, kk, 0:width], start=False, stop=last)
                        if t == tiles[-1]:
                            mm.then_inc(w_used, 1)
                        elif g == groups - 1:
                            mm.then_inc(full[t], 1)

            def wait_apart():
                pe.nop().then_inc(waited, 1)

            def tp(out, in_, n=P):
                return pe.transpose(out, in_, cst[0:n, 0:n])

            def xt_tile(stage, t, at, src):
                per, m = (4, P) if t < NT else (8, NS)
                for q in range(KT // per):
                    pe.wait_ge(*is_free(stage, ("xt", at + q)))
                    bk = bank_of(stage, ("xt", at + q))
                    for k in range(per):
                        mm = tp(bk[:, k * m:(k + 1) * m], src[0:m, (q * per + k) * P:(q * per + k + 1) * P], m)
                    mm.then_inc(FULL(stage, ("xt", at + q)), 1)

            def norm(stage, tile_list, first_xn):
                for n, t in enumerate(tile_list):
                    pe.wait_ge(xn_ready, first_xn + n + 1)
                    xt_tile(stage, t, 4 * n, xn[:, n % 2])

            def xt_done(stage, batches):
                for n in (batches - 2, batches - 1):
                    pe.wait_ge(*is_drained(stage, ("xt", n)))

            pe.wait_ge(consts_in, 16)
            norm("mem", [0, 1, 2, 3], 0)
            xt_done("mem", 16)
            for ch in range(4):
                l = ch // 2
                gemm(Lin(plan.groups["mem"] + GPC * ch), "mem", ch, tiles=[2 * l, 2 * l + 1])
            norm("n0", ALL, 4)
            xt_done("n0", 18)
            base = plan.groups["even"]
            for ch in range(3):
                gemm(Lin(base + GPC * ch), "kvq", ch, width=256 if ch == 0 else CW)

            for t in ALL:
                pe.wait_ge(*is_drained("kvq", (0, t)))
            pe.wait_ge(*is_free("epre", "kT"))
            bk = bank_of("epre", "kT")
            for b in range(NT):
                mm = tp(bk[:, b * P:(b + 1) * P], KV[:, b, 0:P])
            mm.then_inc(FULL("epre", "kT"), 1)
            pe.wait_ge(*is_free("epre", "kTs"))
            bk = bank_of("epre", "kTs")
            tp(bk[:, 0:NS], KV[0:NS, NT, 0:P], NS).then_inc(FULL("epre", "kTs"), 1)
            pe.wait_ge(*is_free("epre", "qTs"))
            bk = bank_of("epre", "qTs")
            for ch in (1, 2):
                pe.wait_ge(*is_drained("kvq", (ch, NT)))
            for g in range(AG):
                mm = tp(bk[:, g * NS:(g + 1) * NS], Z[0:NS, NT, g * P:(g + 1) * P], NS)
            mm.then_inc(FULL("epre", "qTs"), 1)
            pe.wait_ge(ws_ready, 1)
            pe.wait_ge(*is_free("epre", "wsT"))
            bk = bank_of("epre", "wsT")
            for g in range(BG):
                mm = tp(bk[:, g * P:(g + 1) * P], wraw[:, g])
            mm.then_inc(FULL("epre", "wsT"), 1)

            def window_step(stage, j, i, name):
                pe.wait_ge(*is_free(stage, name, i))
                bk = bank_of(stage, name)
                kind = name.rstrip("0123")
                b = int(name[-1]) if kind in ("QK", "pT", "PV") else 0
                if kind == "qT":
                    pe.wait_ge(q_staged, j + 1)
                    for n in range(NT):
                        mm = tp(bk[:, n * P:(n + 1) * P], qst[:, n])
                elif kind == "Kb":
                    pe.wait_ge(kb_in, 32 * j + 32)
                    mm = tp(bk[:, 0:P], Kraw)
                elif kind == "Ss":
                    wait_apart()
                    for kv in range(2):
                        h = slice(64 * kv, 64 * kv + 64)
                        mm = pe.matmul(bk[h, 0:WIN + NS], qs[h, :], kTs[h, :], start=True, stop=True)
                elif kind == "QK":
                    ks = 0 if b else P
                    for kv in range(2):
                        if kv:
                            pe.drain()
                        h = slice(64 * kv, 64 * kv + 64)
                        mm = pe.matmul(bk[:, kv * 256 + ks:kv * 256 + 256], qT[h, b * P:(b + 1) * P],
                                       kT[h, (b - 1) * P + ks:(b + 1) * P], start=True, stop=True)
                elif kind == "pT":
                    pe.wait_ge(p_ready, 4 * j + (b + 1))
                    for kv in range(2):
                        for kb in range(0 if b else 1, 2):
                            mm = tp(bk[:, (2 * kv + kb) * P:(2 * kv + kb + 1) * P], S[:, kv, kb * P:(kb + 1) * P])
                elif kind == "PV":
                    pe.wait_ge(*is_drained(stage, f"pT{b}", i))
                    for kv in range(2):
                        for kb in range(0 if b else 1, 2):
                            mm = pe.matmul(bk[:, kv * 64:kv * 64 + 64], pT[:, 2 * kv + kb],
                                           KV[:, b - 1 + kb, P + kv * 64:P + kv * 64 + 64],
                                           start=(kb == (0 if b else 1)), stop=(kb == 1))
                elif kind == "pTs":
                    pe.wait_ge(sp_ready, j + 1)
                    tp(bk[:, 0:P], Ss[:, 0:P])
                    mm = tp(bk[0:NS, P:2 * P], Ss[:, P:P + NS])
                else:
                    for kv in range(2):
                        h = slice(64 * kv, 64 * kv + 64)
                        pe.matmul(bk[h, 0:64], Vraw[:, h], pTs[:, h], start=True, stop=False)
                        mm = pe.matmul(bk[h, 0:64], KV[0:NS, NT, P + 64 * kv:P + 64 * kv + 64],
                                       pTs[0:NS, P + 64 * kv:P + 64 * kv + 64], start=False, stop=True)
                mm.then_inc(FULL(stage, name), 1)

            def window_steps(stage, j, i, step):
                for point, name in E_POINTS:
                    if point == step:
                        window_step(stage, j, i, name)

            for pair in range(4):
                stage = f"pair{pair}"
                with pe.Fori(0, 2) as i:
                    gemm(Lin(base + GPC * (3 + 2 * pair), GPC, i), stage, "acc", i,
                         between=lambda step: window_steps(stage, 2 * pair + i, i, step))
                if pair == 0:
                    for t in ALL:
                        pe.wait_ge(vn_ready, t + 1)
                        for q in range(2):
                            pe.wait_ge(*is_free("mixv", (t, q)))
                            bk = bank_of("mixv", (t, q))
                            for g in (2 * q, 2 * q + 1):
                                lhs = wsT[:, g] if t < NT else wsTs[0:NS, g]
                                mm = pe.matmul(bk[0:rows(t), (g % 2) * 256:(g % 2) * 256 + 256], lhs,
                                               Z[0:rows(t), t, AW + 256 * g:AW + 256 * g + 256], start=True, stop=True)
                            mm.then_inc(FULL("mixv", (t, q)), 1)
            for n in range(2):
                pe.wait_ge(*is_free("epost", f"o{n}"))
                bk = bank_of("epost", f"o{n}")
                if n == 0:
                    pe.wait_ge(*is_drained("pair3", "PVs", 1))
                for g in range(4):
                    mm = tp(bk[0:NS, g * P:(g + 1) * P], oTs[:, 4 * n + g])
                mm.then_inc(FULL("epost", f"o{n}"), 1)
            for t in ALL:
                pe.wait_ge(z_ready, t + 1)
                xt_tile("zt", t, 4 * t, Z[:, t])
            xt_done("zt", 18)
            with pe.Fori(0, 4) as i:
                gemm(Lin(plan.groups["eout"], GPC, i), "eout", "acc", i)

            def cross(l):
                st = f"x{l}"
                norm(st, ALL, 9 + 5 * l + 5 * l)
                xt_done(st, 18)
                gemm(Lin(plan.groups[st + "q"]), st, "acc")
                pe.wait_ge(cross_in, 32 * (l + 1))
                for m in range(2):
                    pe.wait_ge(*is_free(st, f"kT{m}"))
                    bk = bank_of(st, f"kT{m}")
                    for h in range(XH):
                        mm = tp(bk[:, h * P:(h + 1) * P], KVb[:, 0, m, h * P:(h + 1) * P])
                    mm.then_inc(FULL(st, f"kT{m}"), 1)
                for t in ALL:
                    r = rows(t)
                    pe.wait_ge(*is_free(st, f"qT{t}"))
                    bk = bank_of(st, f"qT{t}")
                    if t < NT:
                        pe.wait_ge(*is_drained(st, ("acc", t)))
                    else:
                        pe.wait_ge(*is_drained(st, ("acc", NT)))
                    for h in range(XH):
                        mm = tp(bk[:, h * r:(h + 1) * r], qc[0:r, t, h * P:(h + 1) * P], r)
                    mm.then_inc(FULL(st, f"qT{t}"), 1)
                for t in ALL:
                    pe.wait_ge(*is_drained(st, f"qT{t}"))

                def scores(t):
                    for q in range(2):
                        pe.wait_ge(*is_free(st, f"S{t}{q}"))
                        bk = bank_of(st, f"S{t}{q}")
                        for h in (2 * q, 2 * q + 1):
                            mm = pe.matmul(bk[:, (h % 2) * MEM:(h % 2 + 1) * MEM], cqT[:, h, t * P:(t + 1) * P],
                                           ckT[:, h], start=True, stop=True)
                        mm.then_inc(FULL(st, f"S{t}{q}"), 1)

                scores(0)
                for t in range(NT):
                    if t + 1 < NT:
                        scores(t + 1)
                    for q in range(2):
                        pe.wait_ge(*is_free(st, f"pT{t}{q}"))
                        bk = bank_of(st, f"pT{t}{q}")
                        pe.wait_ge(*is_drained(st, f"S{t}{q}"))
                        for h in (2 * q, 2 * q + 1):
                            for m in range(2):
                                mm = tp(bk[:, (2 * (h % 2) + m) * P:(2 * (h % 2) + m + 1) * P], Px[:, h, m * P:(m + 1) * P])
                        mm.then_inc(FULL(st, f"pT{t}{q}"), 1)
                    pe.wait_ge(*is_free(st, f"PV{t}"))
                    bk = bank_of(st, f"PV{t}")
                    for q in range(2):
                        pe.wait_ge(*is_drained(st, f"pT{t}{q}"))
                    for h in range(XH):
                        for m in range(2):
                            mm = pe.matmul(bk[:, h * P:(h + 1) * P], cpT[:, 2 * h + m], Vm[:, m, h * P:(h + 1) * P],
                                           start=(m == 0), stop=(m == 1))
                    mm.then_inc(FULL(st, f"PV{t}"), 1)
                    pe.wait_ge(*is_free(st, f"oT{t}"))
                    bk = bank_of(st, f"oT{t}")
                    pe.wait_ge(*is_drained(st, f"PV{t}"))
                    for h in range(XH):
                        mm = tp(bk[:, h * P:(h + 1) * P], Ox[:, h * P:(h + 1) * P])
                    mm.then_inc(FULL(st, f"oT{t}"), 1)
                pe.wait_ge(*is_free(st, "SS"))
                ss = bank_of(st, "SS")
                for b in range(DEC_B):
                    pe.wait_ge(kvb_in[b % 4], 16 * (4 * l + b // 4 + 1))
                    for m in range(2):
                        pe.wait_ge(*is_free(st, f"K{b}{m}"))
                        bk = bank_of(st, f"K{b}{m}")
                        for h in range(XH):
                            mm = tp(bk[:, h * P:(h + 1) * P], KVb[:, b % 4, m, h * P:(h + 1) * P])
                        mm.then_inc(FULL(st, f"K{b}{m}"), 1)
                    for m in range(2):
                        pe.wait_ge(*is_drained(st, f"K{b}{m}"))
                    for h in range(XH):
                        for m in range(2):
                            o = m * 256 + b * 32 + h * 8
                            mm = pe.matmul(ss[:, o:o + 8], ckT[:, h, m * P:(m + 1) * P],
                                           cqT[:, h, SEQ + b * 8:SEQ + b * 8 + 8], start=True, stop=True)
                mm.then_inc(FULL(st, "SS"), 1)
                pe.wait_ge(*is_free(st, "SR"))
                bk = bank_of(st, "SR")
                pe.wait_ge(*is_drained(st, "SS"))
                for half in range(2):
                    for m in range(2):
                        mm = tp(bk[:, half * 256 + m * P:half * 256 + (m + 1) * P], Sb[:, m * 256 + half * P:m * 256 + (half + 1) * P])
                mm.then_inc(FULL(st, "SR"), 1)
                pe.wait_ge(*is_free(st, "PR"))
                bk = bank_of(st, "PR")
                pe.wait_ge(cross_sp, l + 1)
                for m in range(2):
                    for half in range(2):
                        mm = tp(bk[:, m * 256 + half * P:m * 256 + (half + 1) * P], Px[:, half, m * P:(m + 1) * P])
                mm.then_inc(FULL(st, "PR"), 1)
                pe.wait_ge(*is_free(st, "OS"))
                bk = bank_of(st, "OS")
                pe.wait_ge(*is_drained(st, "PR"))
                pr = cpT.rearrange("p a b -> p (a b)")
                for b in range(DEC_B):
                    pe.wait_ge(kvb_in[b % 4], 16 * (4 * l + 2 + b // 4 + 1))
                    for h in range(XH):
                        for m in range(2):
                            o = m * 256 + b * 32 + h * 8
                            mm = pe.matmul(bk[:, h * NS + b * 8:h * NS + b * 8 + 8], KVb[:, b % 4, m, h * P:(h + 1) * P],
                                           pr[:, o:o + 8], start=(m == 0), stop=(m == 1))
                    if b < DEC_B - 1:
                        mm.then_inc(vb_used, 1)
                mm.then_inc(FULL(st, "OS"), 1)
                pe.wait_ge(*is_drained(st, "OS"))
                pe.wait_ge(*is_drained(st, f"oT{NT - 1}"))
                for n in range(4):
                    gemm(Lin(plan.groups[st + "o"]), st + "o", n, groups=2, g0=2 * n)

            cross(0)
            norm("n1", ALL, 14)
            xt_done("n1", 18)
            base = plan.groups["ret"]
            gemm(Lin(base), "retA", "acc")

            def retention_step(stage, h, i, name):
                kind = name[0]
                if kind == "W":
                    b, m = int(name[1]), int(name[2])
                    if m == 0:
                        pe.wait_ge(state_in[b % 4], 32 * h + (16 * (b // 4) + 16))
                        for k in range(2):
                            mm = pe.matmul(bank[5][0:NS, :], qz[:, k, b], Wst[:, b % 4, k], start=False, stop=(b == 7 and k == 1))
                        if b == 7:
                            mm.then_inc(FULL(stage, "OI"), 1)
                    pe.wait_ge(*is_free(stage, name, i))
                    bk = bank_of(stage, name)
                    pe.wait_ge(kz_ready, 8 * h + (b + 1))
                    mm = pe.matmul(bk[:, :], kzb[0:NS, b % 2, m * P:(m + 1) * P], V[0:NS, NT], start=True, stop=True)
                    mm.then_inc(FULL(stage, name), 1)
                    return
                pe.wait_ge(*is_free(stage, name, i))
                bk = bank_of(stage, name)
                if kind == "T":
                    c = int(name[1])
                    r = rows(c)
                    if c == NT:
                        wait_apart()
                    for n in range(4):
                        mm = tp(bk[:, n * r:(n + 1) * r], QK[0:r, c, n * P:(n + 1) * P], r)
                elif kind == "S":
                    c = int(name[2])
                    r = rows(c)
                    pe.wait_ge(*is_drained(stage, f"T{c}", i))
                    for k in range(2):
                        mm = pe.matmul(bk[0:r, 0:r], qkT[:, 2 + k, c * P:c * P + r], qkT[:, k, c * P:c * P + r],
                                       start=(k == 0), stop=(k == 1))
                elif name == "OI":
                    pe.wait_ge(*is_drained(stage, ("B", NT), i))
                    pe.wait_ge(*is_drained(stage, "ST4", i))
                    pe.wait_ge(qz_ready, h + 1)
                    wait_apart()
                    pe.matmul(bk[0:NS, :], STm[0:NS, NT, 0:NS], V[0:NS, NT], start=True, stop=False)
                    return
                elif kind == "O":
                    c = int(name[1])
                    pe.wait_ge(*is_drained(stage, ("B", c), i))
                    mm = pe.matmul(bk[:, :], STm[:, c], V[:, c], start=True, stop=(c == 0))
                    if c:
                        pe.wait_ge(*is_drained(stage, f"U{c - 1}1", i))
                        for k in range(2):
                            mm = pe.matmul(bk[:, :], qkT[:, k, c * P:(c + 1) * P], rstate[:, k], start=False, stop=(k == 1))
                elif kind == "U":
                    c, m = int(name[1]), int(name[2])
                    pe.wait_ge(kdec_ready, 4 * h + (c + 1))
                    mm = pe.matmul(bk[:, :], kdec[:, c % 2, m * P:(m + 1) * P], V[:, c], start=True, stop=True)
                else:
                    half, q = int(name[1]), int(name[2])
                    pe.wait_ge(gated, 5 * h + 10 + (2 * q + 2 if q < 2 else 5))
                    if q < 2:
                        for k in range(2):
                            for n in range(2):
                                t = 2 * q + n
                                mm = tp(bk[:, k * 256 + n * P:k * 256 + (n + 1) * P], ON[:, t, (2 * half + k) * P:(2 * half + k + 1) * P])
                    else:
                        wait_apart()
                        for k in range(2):
                            mm = tp(bk[:, k * NS:(k + 1) * NS], ON[0:NS, NT, (2 * half + k) * P:(2 * half + k + 1) * P], NS)
                mm.then_inc(FULL(stage, name), 1)

            def retention_steps(points, stage, h, i, step):
                for point, name in points:
                    if point == step:
                        retention_step(stage, h, i, name)

            with pe.Fori(0, RH - 1) as h:
                for t in ALL:
                    pe.wait_ge(*is_free("ret", ("B", t), h))
                gemm(Lin(base + GPC, 3 * GPC, h), "ret", "B", h, between=lambda step: retention_steps(RB_POINTS, "ret", h, h, step))
                gemm(Lin(base + 2 * GPC, 3 * GPC, h), "ret", "C", h, between=lambda step: retention_steps(RC_POINTS, "ret", h, h, step))
                gemm(Lin(base + 3 * GPC, 3 * GPC, h), "ret", "A", h, between=lambda step: retention_steps(RA_POINTS, "ret", h, h, step))
            h = RH - 1
            for t in ALL:
                pe.wait_ge(*is_free("retZ", ("B", t)))
            L = base + GPC + 3 * GPC * h
            gemm(Lin(L), "retZ", "B", between=lambda step: retention_steps(RB_POINTS, "retZ", h, 0, step))
            gemm(Lin(L + GPC), "retZ", "C", between=lambda step: retention_steps(RC_POINTS, "retZ", h, 0, step))

            def mixed_steps(half, step):
                if step % PT == 0:
                    pe.wait_ge(mix_ready, GPC * half + step // PT + 1)
                if half == 0:
                    retention_steps(RZ_POINTS, "retZ", RH - 1, 0, step)

            for half in range(2):
                L = plan.groups["rout"] + 4 * GPC * half
                gemm(Lin(L), "rout", "acc", 4 * half, between=lambda step: mixed_steps(half, step), parts=(xl, xh))
                with pe.Fori(1, 4) as i:
                    gemm(Lin(L, GPC, i), "rout", "acc", i + 4 * half, parts=(xl, xh))
            cross(1)

        @block.scalar
        def _(act):
            def hi(L, g):
                if L.k == 0 and L.c + g >= plan.total:
                    return
                s = (L.c + g) % RING
                act.wait_ge(raw_loaded[s], 16 * (L.quarter(g) + 1))
                head, inside = divmod(L.c + g - plan.groups["ret"], 3 * GPC)
                if 0 <= head < RH and inside < GPC:
                    act.wait_ge(keys_loaded[s], Lin(32 * head + 16 * (inside // RING + 1), 32 if L.k else 0, L.i).at())
                if not (L.k == 0 and L.c + g < RING):
                    act.wait_ge(w_used, L.at(g - RING + 1))
                act.activation(whi[:, s], raw[:, s], ACT.Copy).then_inc(hi_ready, 1)

            def chunk(L, groups=GPC, g0=0, between=None, evac=None):
                for g in range(groups):
                    if between:
                        between(range(PT * g, PT * (g + 1)))
                    if evac and g == groups - 1:
                        evac()
                    hi(L, g0 + g + RING)

            def copy(dst, src, **kw):
                return act.activation(dst, src, ACT.Copy, **kw)

            def xt_hi(stage, n, t, q):
                act.wait_ge(*is_full(stage, ("xt", n)))
                bk = bank_of(stage, ("xt", n))
                if t < NT:
                    dst = xh[:, 4 * q:4 * q + 4, t * P:(t + 1) * P]
                    src = bk[:, :].rearrange("p (k n) -> p k n", n=P)
                else:
                    dst = xs[:, 8 * q:8 * q + 8, 0:NS]
                    src = bk[:, :].rearrange("p (k n) -> p k n", n=NS)
                copy(dst, src).then_inc(xt_hi_ready, 1)

            def xt_all(stage, tiles):
                n = 0
                for t in tiles:
                    for q in range(4 if t < NT else 2):
                        xt_hi(stage, n, t, q)
                        n += 1

            def squares(src, tiles):
                for t in tiles:
                    r = rows(t)
                    act.drain()
                    act.activation(junk[0:r, :], src[0:r, t], ACT.Square, accum_out=stat[0:r, t:t + 1]).then_inc(squares_done, 1)

            def sqrt(n, cols):
                act.wait_ge(var_ready, n + 1)
                act.activation(stat[:, 16:16 + cols], stat[:, 8:8 + cols], ACT.Sqrt).then_inc(std_ready, 1)

            def load_gain(g, xn_before):
                if xn_before:
                    act.wait_ge(xn_ready, xn_before)
                act.dma_start(gbc, g.partition_broadcast(P)).then_inc(g_in, 16)

            def load_x(scratch):
                for t in range(NT):
                    src = x_scratch[t * P:(t + 1) * P, :] if scratch else I.x_prompt[0, t * P:(t + 1) * P, :]
                    act.dma_start(X[:, t], src).then_inc(x_in, 16)
                src = x_scratch[SEQ:SEQ + NS, :] if scratch else I.x_sample.rearrange("b t d -> (b t) d")
                act.dma_start(X[0:NS, NT], src).then_inc(x_in, 16)

            act.dma_start(cst[:, :], consts).then_inc(consts_in, 16)
            for m in range(2):
                act.dma_start(memX[:, m], I.mem_prompt[0, m * P:(m + 1) * P, :]).then_inc(mem_in, 16)
            load_gain(I.norm_mem[0], 0)
            load_x(False)
            for s in range(RING):
                hi(Lin(0), s)
            act.wait_ge(mem_in, 32)
            act.wait_ge(stat_zero, 1)
            squares(memX, [0, 1])
            sqrt(plan.st["mem"], 2)
            n = 0
            for l in range(2):
                if l == 1:
                    load_gain(I.norm_mem[1], 2)
                for m in range(2):
                    for q in range(4):
                        xt_hi("mem", n, 2 * l + m, q)
                        n += 1
            load_gain(I.norm_mix[0], 4)
            act.wait_ge(x_in, 80)
            squares(X, ALL)

            def mem_evac(ch):
                l = ch // 2
                if ch >= 2:
                    act.wait_ge(mem_stored[ch % 2], 32)
                for m in range(2):
                    t = 2 * l + m
                    if m == 0:
                        act.wait_ge(*is_full("mem", (ch, t)))
                        bk = bank_of("mem", (ch, t))
                    else:
                        act.wait_ge(w_used, plan.groups["mem"] + GPC * (ch + 1))
                        bk = bank[t]
                    copy(memKV[:, ch % 2, m], bk[:, :]).then_inc(FREE("mem", (ch, t)), 1)
                act.drain()
                out = (O.mem_k_prompt, O.mem_v_prompt)[ch % 2]
                for m in range(2):
                    act.dma_start(out[l, 0, m * P:(m + 1) * P].rearrange("m h d -> m (h d)"), memKV[:, ch % 2, m]).then_inc(mem_stored[ch % 2], 16)

            for ch in range(4):
                chunk(Lin(plan.groups["mem"] + GPC * ch), evac=lambda: mem_evac(ch))
            sqrt(plan.st["n0"], 5)
            xt_all("n0", ALL)

            act.wait_ge(xn_ready, 9)
            act.wait_ge(ws_zeroed, 1)
            for dst, src in ((wraw, I.w_spatial[0].rearrange("g i j -> i g j")), (sinkb, I.attn_sinks[0].partition_broadcast(P)),
                             (bs, I.b_spatial[0].rearrange("g i -> i g"))):
                act.dma_start(dst, src, allow_slow_non_contiguous=True).then_inc(small_in, 16)
            for b in range(DEC_B):
                r = slice(b * DEC_T, (b + 1) * DEC_T)
                for g in range(BG):
                    act.dma_start(wsTs[r, g, r], I.w_spatial[0, g, 0:DEC_T, 0:DEC_T].rearrange("t j -> j t"),
                                  allow_slow_non_contiguous=True).then_inc(small_in, 16)
                act.dma_start(bss[r, :], I.b_spatial[0, :, 0:DEC_T].rearrange("g t -> t g"),
                              allow_slow_non_contiguous=True).then_inc(small_in, 16)
            for hd in range(AH):
                act.dma_start(sinkr[hd * DEC_T:(hd + 1) * DEC_T, :], I.attn_sinks[0, hd:hd + 1].partition_broadcast(DEC_T)).then_inc(small_in, 16)

            base = plan.groups["even"]

            def kvq_evac(ch):
                for t in range(NT):
                    act.wait_ge(*is_full("kvq", (ch, t)))
                    bk = bank_of("kvq", (ch, t))
                    if ch == 0:
                        ins = copy(KV[:, t], bk[:, 0:256])
                    else:
                        ins = copy(Z[:, t, (ch - 1) * CW:ch * CW], bk[:, :], scale=AD ** -0.5)
                    ins.then_inc(FREE("kvq", (ch, t)), 1)

            for ch in range(3):
                chunk(Lin(base + GPC * ch), evac=lambda: kvq_evac(ch))
            act.wait_ge(*is_full("epre", "kT"))
            bk = bank_of("epre", "kT")
            copy(kT[:, 0:SEQ], bk[:, :]).then_inc(FREE("epre", "kT"), 1)
            act.wait_ge(*is_full("epre", "kTs"))
            bk = bank_of("epre", "kTs")
            copy(kTs[:, WIN:WIN + NS], bk[:, 0:NS]).then_inc(FREE("epre", "kTs"), 1)
            act.wait_ge(*is_full("epre", "qTs"))
            bk = bank_of("epre", "qTs")
            copy(qTs.rearrange("p b (g t) -> p g b t", t=DEC_T), bk[:, :].rearrange("p (g b t) -> p g b t", g=AG, t=DEC_T))\
                .then_inc(FREE("epre", "qTs"), 1)
            act.wait_ge(*is_full("epre", "wsT"))
            bk = bank_of("epre", "wsT")
            copy(wsT, bk[:, :].rearrange("p (g n) -> p g n", n=P)).then_inc(FREE("epre", "wsT"), 1)
            act.wait_ge(*is_drained("kvq", (0, NT)))
            act.drain()
            for out, cache, o in ((O.win_k_sample, I.cache_win_k, 0), (O.win_v_sample, I.cache_win_v, P)):
                act.dma_start(out[0, :, 0:WIN - DEC_T].rearrange("b w k d -> b (w k d)"),
                              cache[0, :, DEC_T:WIN].rearrange("b w k d -> b (w k d)")).then_inc(outs_done, 16)
                for b in range(DEC_B):
                    act.dma_start(out[0, b, WIN - DEC_T:WIN].rearrange("w k d -> w (k d)"), KV[b * DEC_T:(b + 1) * DEC_T, NT, o:o + P])\
                        .then_inc(outs_done, 16)
            for out, o in ((O.win_k_prompt, 0), (O.win_v_prompt, P)):
                act.dma_start(out[0, 0].rearrange("w k d -> w (k d)"), KV[:, NT - 1, o:o + P]).then_inc(outs_done, 16)
            act.dma_start(lng, I.norm_v_g[0].partition_broadcast(P)).then_inc(ln_in, 16)
            act.dma_start(lnb, I.norm_v_b[0].partition_broadcast(P)).then_inc(ln_in, 16)

            def window_step(stage, j, i, name):
                kind = name.rstrip("0123")
                b = int(name[-1]) if kind in ("QK", "pT", "PV") else 0
                if kind == "QK":
                    act.drain()
                    act.wait_ge(neg_ready, 4 * j + (b + 1))
                    ks = 0 if b else P
                    for kv in range(2):
                        ins = act.activation(S[:, kv, ks:257], S[:, kv, ks:257], ACT.Exp, bias=stat[:, 24 + kv:25 + kv],
                                             accum_out=stat[:, 26 + kv:27 + kv])
                    ins.then_inc(p_ready, 1)
                elif kind == "Ss":
                    act.wait_ge(sneg_ready, j + 1)
                    act.activation(Ss[:, 0:193], Ss[:, 0:193], ACT.Exp, bias=stat[:, 28:29], accum_out=stat[:, 29:30])\
                        .then_inc(sexp_done, 1)
                elif kind != "PV":
                    act.wait_ge(*is_full(stage, name, i))
                    bk = bank_of(stage, name)
                    if kind == "qT":
                        ins = copy(qT, bk[:, :])
                    elif kind == "Kb":
                        ins = copy(kTs[:, 0:P], bk[:, 0:P])
                    elif kind == "pT":
                        src = bk[:, :].rearrange("p (a n) -> p a n", n=P)
                        ins = copy(pT, src) if b else copy(pT[:, 1:4:2], src[:, 1:4:2])
                    elif kind == "pTs":
                        copy(pTs[:, 0:P], bk[:, 0:P])
                        ins = copy(pTs[0:NS, P:2 * P], bk[0:NS, P:2 * P])
                    else:
                        ins = copy(oTs.rearrange("p g (b t) -> p g b t", t=DEC_T)[:, :, j], bk[:, 0:NS].rearrange("p (g t) -> p g t", t=DEC_T))
                    ins.then_inc(FREE(stage, name), 1)

            def window_steps(stage, j, i, steps):
                for point, name in E_POINTS:
                    if point in steps:
                        window_step(stage, j, i, name)

            def gate_evac(stage, tag, i, n, buf, sbuf):
                for t in range(NT):
                    act.wait_ge(*is_full(stage, (tag, t), i))
                    bk = bank_of(stage, (tag, t))
                    if t >= 2:
                        act.wait_ge(gated, 5 * n + (t - 1))
                    act.activation(buf[:, t % 2], bk[:, :], ACT.Silu).then_inc(FREE(stage, (tag, t)), 1)
                act.wait_ge(*is_drained(stage, (tag, NT), i))
                act.activation(sbuf[0:NS, :], sbuf[0:NS, :], ACT.Silu).then_inc(sil_ready, 1)

            def pair_evac(stage, pair, i):
                if pair == 3:
                    return gate_evac(stage, "acc", i, i, sil, sils)
                if pair == 2:
                    return
                for t in range(NT):
                    act.wait_ge(*is_full(stage, ("acc", t), i))
                    bk = bank_of(stage, ("acc", t))
                    if pair == 0:
                        ins = copy(Z[:, t, bass.ds(AW + CW * i, CW)], bk[:, :])
                    else:
                        ins = act.activation(SG[:, t, bass.ds(CW * i, CW)], bk[:, :], ACT.Silu)
                    ins.then_inc(FREE(stage, ("acc", t)), 1)
                if pair == 1:
                    act.wait_ge(*is_drained(stage, ("acc", NT), i))
                    g = SG[0:NS, NT, bass.ds(CW * i, CW)]
                    act.activation(g, g, ACT.Silu).then_inc(sg_ready, 1)

            for pair in range(4):
                stage = f"pair{pair}"
                with act.Fori(0, 2) as i:
                    j = 2 * pair + i
                    for dst, src in ((Kraw, I.cache_win_k), (Vraw, I.cache_win_v)):
                        act.dma_start(dst, src[0].rearrange("b w k d -> b w (k d)")[j]).then_inc(kb_in, 16)
                    chunk(Lin(base + GPC * (3 + 2 * pair), GPC, i),
                          between=lambda steps: window_steps(stage, j, i, steps),
                          evac=lambda: pair_evac(stage, pair, i))
                if pair == 0:
                    sqrt(plan.st["ln"], 5)
                    act.wait_ge(vn_ready, 5)
                    act.dma_start(O.chunk_v[0].rearrange("b t n -> (b t) n"), Z[0:NS, NT, AW:D]).then_inc(vn_out, 16)
                    for t in ALL:
                        r = rows(t)
                        for q in range(2):
                            act.wait_ge(*is_full("mixv", (t, q)))
                        if t == NT:
                            act.wait_ge(vn_out, 16)
                        for g in range(BG):
                            bias = bs[:, g:g + 1] if t < NT else bss[0:r, g:g + 1]
                            ins = act.activation(Z[0:r, t, AW + 256 * g:AW + 256 * g + 256],
                                                 bank_of("mixv", (t, g // 2))[0:r, (g % 2) * 256:(g % 2) * 256 + 256], ACT.Identity, bias=bias)
                            if g % 2:
                                ins.then_inc(FREE("mixv", (t, g // 2)), 1)
            xt_all("zt", ALL)
            act.wait_ge(outs_done, 16 * 20)
            load_x(False)
            with act.Fori(0, 4) as i:
                chunk(Lin(plan.groups["eout"], GPC, i))

            def cross(l):
                st = f"x{l}"
                load_gain(I.norm_cross[l], 9 + 10 * l)
                act.wait_ge(x_done, 1 + 2 * l)
                squares(X, ALL)
                for n in range(2):
                    act.wait_ge(mem_stored[n], 16 * 4)
                act.dma_start(KVb[:, 0], O.mem_k_prompt[l, 0].rearrange("(m p) h d -> p m (h d)", p=P)).then_inc(cross_in, 16)
                sqrt(plan.st[st], 5)
                xt_all(st, ALL)
                act.dma_start(Vm, O.mem_v_prompt[l, 0].rearrange("(m p) h d -> p m (h d)", p=P)).then_inc(cross_in, 16)

                def load_b(cache, b):
                    act.dma_start(KVb[:, b % 4], cache[l, b].rearrange("(m p) h d -> p m (h d)", p=P)).then_inc(kvb_in[b % 4], 16)

                def q_evac():
                    for t in range(NT):
                        act.wait_ge(*is_full(st, ("acc", t)))
                        bk = bank_of(st, ("acc", t))
                        copy(qc[:, t], bk[:, :]).then_inc(FREE(st, ("acc", t)), 1)

                chunk(Lin(plan.groups[st + "q"]), evac=q_evac)
                for m in range(2):
                    act.wait_ge(*is_full(st, f"kT{m}"))
                    bk = bank_of(st, f"kT{m}")
                    copy(ckT[:, :, m * P:(m + 1) * P], bk[:, :].rearrange("p (h n) -> p h n", n=P)).then_inc(FREE(st, f"kT{m}"), 1)
                for b in range(4):
                    load_b(I.cache_mem_k, b)
                for t in ALL:
                    r = rows(t)
                    act.wait_ge(*is_full(st, f"qT{t}"))
                    bk = bank_of(st, f"qT{t}")
                    copy(cqT[:, :, t * P:t * P + r], bk[:, 0:XH * r].rearrange("p (h n) -> p h n", n=r)).then_inc(FREE(st, f"qT{t}"), 1)
                for t in range(NT):
                    act.wait_ge(cneg, 5 * l + t + 1)
                    for q in range(2):
                        act.wait_ge(*was_full(st, f"pT{t}{q}"))
                    for h in range(XH):
                        bk = bank[2 * (t % 2) + h // 2]
                        ins = act.activation(Px[:, h], bk[:, (h % 2) * MEM:(h % 2 + 1) * MEM], ACT.Exp, scale=XD ** -0.5,
                                             bias=stat[:, 56 + 4 * (t % 2) + h:57 + 4 * (t % 2) + h],
                                             accum_out=stat[:, 48 + 4 * (t % 2) + h:49 + 4 * (t % 2) + h])
                        if h % 2:
                            ins.then_inc(FREE(st, f"S{t}{h // 2}"), 1)
                    act.wait_ge(*is_full(st, f"pT{t}0"))
                    bk = bank_of(st, f"pT{t}0")
                    copy(cpT[:, 0:4], bk[:, :].rearrange("p (a n) -> p a n", n=P)).then_inc(FREE(st, f"pT{t}0"), 1)
                    act.wait_ge(*is_full(st, f"oT{t}"))
                    bk = bank_of(st, f"oT{t}")
                    copy(xh[:, 0:XH, t * P:(t + 1) * P], bk[:, :].rearrange("p (h n) -> p h n", n=P)).then_inc(xt_hi_ready, 1)
                for b in range(DEC_B):
                    act.wait_ge(*is_full(st, f"K{b}0"))
                    bk = bank_of(st, f"K{b}0")
                    copy(ckT[:, :, 0:P], bk[:, :].rearrange("p (h n) -> p h n", n=P)).then_inc(FREE(st, f"K{b}0"), 1)
                    act.wait_ge(*is_full(st, f"K{b}1"))
                    load_b(I.cache_mem_k, b + 4) if b < 4 else load_b(I.cache_mem_v, b - 4)
                act.wait_ge(*is_full(st, "SS"))
                bk = bank_of(st, "SS")
                copy(Sb, bk[:, :]).then_inc(FREE(st, "SS"), 1)
                act.wait_ge(cneg, 5 * l + 5)
                bk = bank[5]
                for half in range(2):
                    ins = act.activation(Px[:, half], bk[:, half * MEM:(half + 1) * MEM], ACT.Exp, scale=XD ** -0.5,
                                         bias=stat[:, 56 + half:57 + half], accum_out=stat[:, 48 + half:49 + half])
                ins.then_inc(FREE(st, "SR"), 1)
                act.wait_ge(*is_full(st, "PR"))
                bk = bank_of(st, "PR")
                copy(cpT.rearrange("p a b -> p (a b)")[:, 0:512], bk[:, :]).then_inc(FREE(st, "PR"), 1)
                for b in range(4, DEC_B):
                    act.wait_ge(vb_used, 7 * l + b - 3)
                    load_b(I.cache_mem_v, b)
                act.wait_ge(*is_full(st, "OS"))
                bk = bank_of(st, "OS")
                copy(xs[:, 0:XH, 0:NS], bk[:, 0:XH * NS].rearrange("p (h n) -> p h n", n=NS)).then_inc(xt_hi_ready, 1)
                chunk(Lin(plan.groups[st + "o"]))

            cross(0)
            load_gain(I.norm_mix[1], 14)
            act.wait_ge(x_done, 2)
            for t in ALL:
                r = rows(t)
                act.dma_start(x_scratch[t * P:t * P + r, :], X[0:r, t]).then_inc(x_saved, 16)
            squares(X, ALL)
            sqrt(plan.st["n1"], 5)
            xt_all("n1", ALL)
            act.wait_ge(xn_ready, 19)
            act.wait_ge(x_saved, 80)
            act.dma_start(zm.rearrange("p b n -> p (b n)"), zmask_d).then_inc(zm_in, 16)

            def qk_evac(stage, i):
                for t in range(NT):
                    act.wait_ge(*is_full(stage, (("A" if stage != "retA" else "acc"), t), i))
                    bk = bank_of(stage, (("A" if stage != "retA" else "acc"), t))
                    copy(QK[:, t], bk[:, :]).then_inc(FREE(stage, (("A" if stage != "retA" else "acc"), t)), 1)

            def v_evac(stage, i):
                for t in range(NT):
                    act.wait_ge(*is_full(stage, ("B", t), i))
                    bk = bank_of(stage, ("B", t))
                    copy(V[:, t], bk[:, :]).then_inc(FREE(stage, ("B", t)), 1)

            def load_state(h, b):
                src = I.state_ret[0].rearrange("b h (k p) e -> b h p k e", p=P)[b, h]
                act.dma_start(Wst[:, b % 4], src).then_inc(state_in[b % 4], 16)

            def head_start(stage, h, i):
                _, n, _ = use(stage, "ST0", i)
                act.wait_ge(free[6], n)
                act.dma_start(rdec, rdec_d[h]).then_inc(rd_in, 16)

            def values_step(stage, h, i, name):
                if name[0] == "T":
                    c = int(name[1])
                    r = rows(c)
                    act.wait_ge(*is_full(stage, name, i))
                    bk = bank_of(stage, name)
                    copy(qkT[:, :, c * P:c * P + r], bk[:, 0:4 * r].rearrange("p (a n) -> p a n", n=r)).then_inc(FREE(stage, name), 1)

            def gates_step(stage, h, i, name):
                if name[0] == "O" and name[1] != "I":
                    act.wait_ge(var_ready, plan.st["gn"] + 1 + 5 * h + int(name[1]))
                    act.activation(stat[:, 66:67], stat[:, 65:66], ACT.Sqrt).then_inc(std_ready, 1)
                elif name[0] == "W" and name[2] == "1":
                    b = int(name[1])
                    act.wait_ge(*is_drained(stage, f"W{b}1", i))
                    dst = O.ret_state_sample[0].rearrange("b h (k p) e -> b h p k e", p=P)[b, h]
                    act.dma_start(dst, Wst[:, b % 4]).then_inc(state_out[b % 4], 16)
                    if 1 <= b < 5:
                        act.wait_ge(state_out[(b - 1) % 4], 32 * h + 16)
                        load_state(h, b + 3)
                elif name == "U31":
                    act.wait_ge(*is_drained(stage, "U31", i))
                    dst = O.ret_state_prompt[0, 0].rearrange("h (k p) e -> h p k e", p=P)[h]
                    act.dma_start(dst, rstate).then_inc(rstate_out, 16)

            def c_evac(stage, h, i):
                act.wait_ge(var_ready, plan.st["gn"] + 5 + 5 * h)
                act.activation(stat[0:NS, 66:67], stat[0:NS, 65:66], ACT.Sqrt).then_inc(std_ready, 1)
                gate_evac(stage, "C", i, 2 + h, sg, sgs)

            def mixed_step(stage, h, i, name):
                half, q = int(name[1]), int(name[2])
                if q == 0 and half:
                    act.wait_ge(mt_out, 32 * h + 16)
                act.wait_ge(*is_full(stage, name, i))
                bk = bank_of(stage, name)
                if q < 2:
                    dst, src = mt[:, :, q * 256:q * 256 + 256], bk[:, :].rearrange("p (k n) -> p k n", k=2)
                else:
                    dst, src = mt[:, :, SEQ:SEQ + NS], bk[:, 0:2 * NS].rearrange("p (k n) -> p k n", k=2)
                copy(dst, src).then_inc(FREE(stage, name), 1)
                if q == 2:
                    act.drain()
                    act.dma_start(mix_scratch[bass.ds(4 * h + 2 * half, 2)].rearrange("k p n -> p k n"), mt).then_inc(mt_out, 16)

            def load_mix(half, g):
                k = slice(GK * g, GK * g + GK)
                src = mix_scratch[KT * half + GK * g:KT * half + GK * g + GK].rearrange("k p n -> p k n")
                act.dma_start(xh[:, k, :].bitcast(F32), src[:, :, 0:SEQ]).then_inc(mix_in[g], 16)
                act.dma_start(xs[:, k, NS:2 * NS].bitcast(F32), src[:, :, SEQ:SEQ + NS]).then_inc(mix_in[g], 16)

            def split_mix(half, g):
                k = slice(GK * g, GK * g + GK)
                act.wait_ge(mix_in[g], 32 * (half + 1))
                copy(xl[:, k, :], xh[:, k, :].bitcast(F32))
                copy(xs[:, k, 0:NS], xs[:, k, NS:2 * NS].bitcast(F32)).then_inc(mix_hi, 1)

            base = plan.groups["ret"]
            chunk(Lin(base), evac=lambda: qk_evac("retA", 0))

            def retention_steps(step, points, stage, h, i, steps):
                for point, name in points:
                    if point in steps:
                        step(stage, h, i, name)

            for b in range(4):
                load_state(0, b)
            with act.Fori(0, RH - 1) as h:
                head_start("ret", h, h)
                chunk(Lin(base + GPC, 3 * GPC, h), between=lambda steps: retention_steps(values_step, RB_POINTS, "ret", h, h, steps), evac=lambda: v_evac("ret", h))
                chunk(Lin(base + 2 * GPC, 3 * GPC, h), between=lambda steps: retention_steps(gates_step, RC_DRAINS, "ret", h, h, steps), evac=lambda: c_evac("ret", h, h))
                chunk(Lin(base + 3 * GPC, 3 * GPC, h), between=lambda steps: retention_steps(mixed_step, RA_POINTS, "ret", h, h, steps), evac=lambda: qk_evac("ret", h))
                act.wait_ge(mt_out, 32 * h + 32)
                for b in range(4):
                    act.wait_ge(state_out[b], 32 * h + 32)
                    load_state(h + 1, b)
            h = RH - 1
            head_start("retZ", h, 0)
            chunk(Lin(base + GPC + 3 * GPC * h), between=lambda steps: retention_steps(values_step, RB_POINTS, "retZ", h, 0, steps), evac=lambda: v_evac("retZ", 0))
            L = Lin(base + 2 * GPC + 3 * GPC * h)
            for g in range(GPC):
                retention_steps(gates_step, RC_DRAINS, "retZ", h, 0, range(PT * g, PT * (g + 1)))
                if g == GPC - 1:
                    c_evac("retZ", h, 0)
                hi(L, g + RING)
                load_mix(0, g)
            for g in range(GPC):
                split_mix(0, g)
            for g in range(GPC):
                retention_steps(mixed_step, RZ_POINTS, "retZ", h, 0, range(PT * g, PT * (g + 1)))
                if g == 4:
                    act.wait_ge(mt_out, 16 * 2 * RH)
                    act.wait_ge(rstate_out, 16 * RH)
                    for slot in range(4):
                        act.wait_ge(state_out[slot], 32 * RH)
                    load_x(True)
                hi(Lin(plan.groups["rout"]), g + RING)
            base = plan.groups["rout"]
            with act.Fori(1, 3) as i:
                chunk(Lin(base, GPC, i))
            for g in range(GPC):
                hi(Lin(base + 3 * GPC), g + RING)
                load_mix(1, g)
                if g >= 2:
                    split_mix(1, g - 2)
            for g in (GPC - 2, GPC - 1):
                split_mix(1, g)
            with act.Fori(0, 4) as i:
                chunk(Lin(base + 4 * GPC, GPC, i))
            cross(1)
            load_gain(I.norm_final, 24)
            act.wait_ge(x_done, 4)
            squares(X, ALL)
            sqrt(plan.st["fin"], 5)

        @block.vector
        def _(v):
            def do(ins):
                v.drain()
                return ins

            def newton(dst, var, std, tmp):
                do(v.reciprocal(dst, std))
                do(v.tensor_tensor(tmp, dst, dst, ALU.mult))
                do(v.scalar_tensor_tensor(tmp, tmp, -0.5, var, ALU.mult, ALU.mult))
                do(v.tensor_scalar(tmp, tmp, 1.5, None, ALU.add))
                do(v.tensor_tensor(dst, dst, tmp, ALU.mult))

            def rms_scales(n, squares, cols):
                v.wait_ge(squares_done, squares)
                do(v.tensor_scalar(stat[:, 8:8 + cols], stat[:, 0:cols], 1.0 / D, EPS, ALU.mult, ALU.add).then_inc(var_ready, 1))
                v.wait_ge(std_ready, n + 1)
                newton(stat[:, 32:32 + cols], stat[:, 8:8 + cols], stat[:, 16:16 + cols], stat[:, 40:40 + cols])

            def xn_tile(src, t, n):
                r = rows(t)
                do(v.scalar_tensor_tensor(xn[0:r, n % 2], src[0:r, t], stat[0:r, 32 + t:33 + t], gbc[0:r, :], ALU.mult, ALU.mult)
                   .then_inc(xn_ready, 1))

            def xt_lo(stage, n, t, q):
                v.wait_ge(xt_hi_ready, plan.hi[stage] + n + 1)
                bk = bank[plan.where[stage, ("xt", n)][0]]
                if t < NT:
                    d = (slice(0, P), slice(4 * q, 4 * q + 4), slice(t * P, (t + 1) * P))
                    do(v.tensor_tensor(xl[d], bk[:, :].rearrange("p (k n) -> p k n", n=P), xh[d].bitcast(F32), ALU.subtract)
                       .then_inc(FREE(stage, ("xt", n)), 1))
                else:
                    k = slice(8 * q, 8 * q + 8)
                    do(v.tensor_tensor(xs[:, k, NS:2 * NS], bk[:, :].rearrange("p (k n) -> p k n", n=NS), xs[:, k, 0:NS].bitcast(F32),
                                       ALU.subtract).then_inc(FREE(stage, ("xt", n)), 1))

            def xt_tile(stage, n0, t):
                for q in range(4 if t < NT else 2):
                    xt_lo(stage, n0 + q, t, q)

            def norm(stage, tiles, src):
                xn_tile(src, tiles[0], 0)
                for n, t in enumerate(tiles):
                    if n + 1 < len(tiles):
                        xn_tile(src, tiles[n + 1], n + 1)
                    xt_tile(stage, 4 * n, t)

            def sample_sum(dst, bk, ins_sem, width=CW):
                do(v.tensor_copy(dst, bk[0:NS, 0:width]))
                do(v.tensor_tensor(dst, bk[NS:2 * NS, 0:width], dst, ALU.add).then_inc(ins_sem, 1))

            v.memset(stat[:, 0:88], 1.0).then_inc(stat_zero, 1)
            for b in range(8):
                v.memset(bn[:, b:b + 1], 0.0).then_inc(free[b], 1)
            v.drain()
            rms_scales(plan.st["mem"], 2, 2)
            v.wait_ge(g_in, 16)
            n = 0
            for l in range(2):
                if l == 1:
                    v.wait_ge(g_in, 32)
                for m in range(2):
                    xn_tile(memX, m, m)
                for m in range(2):
                    for q in range(4):
                        xt_lo("mem", 8 * l + 4 * m + q, 2 * l + m, q)
            rms_scales(plan.st["n0"], 7, 5)
            v.wait_ge(g_in, 48)
            norm("n0", ALL, X)

            do(v.memset(wsTs, 0.0).then_inc(ws_zeroed, 1))
            v.wait_ge(small_in, 16 * (3 + DEC_B * (BG + 1) + AH))
            for g in range(BG):
                do(v.tensor_tensor(wsTs[0:NS, g], wsTs[0:NS, g], C("smask", NS), ALU.mult))
            for g in range(BG):
                ins = v.tensor_tensor(wraw[:, g], wraw[:, g], C("tril"), ALU.mult)
            do(ins.then_inc(ws_ready, 1))
            base = plan.groups["even"]
            for ch in range(3):
                v.wait_ge(w_used, Lin(base + GPC * ch).at(GPC))
                f = FREE("kvq", (ch, NT))
                if ch == 0:
                    sample_sum(KV[0:NS, NT], bank[NT], f, 256)
                else:
                    z = Z[0:NS, NT, 0:AW].rearrange("p (g k d) -> p k g d", g=AG, k=2)[:, ch - 1]
                    do(v.tensor_copy(z, bank[NT][0:NS, :].rearrange("p (g d) -> p g d", d=AD)))
                    do(v.tensor_tensor(z, bank[NT][NS:2 * NS, :].rearrange("p (g d) -> p g d", d=AD), z, ALU.add))
                    do(v.tensor_scalar(z, z, AD ** -0.5, None, ALU.mult).then_inc(f, 1))
            for t in range(NT):
                v.wait_ge(*is_drained("kvq", (2, t)))
            v.wait_ge(*is_drained("epre", "qTs"))
            v.wait_ge(*is_drained("epre", "kT"))

            slope, dist = C("slope"), C("dist")

            def e_stage(stage, j, i):
                v.wait_ge(*was_full(stage, "qT", i))
                src = Z[:, 0:NT, 0:AW].rearrange("p t (k n) -> p t k n", k=2)[:, :, :, bass.ds(AD * j, AD)]
                v.tensor_copy(qst.rearrange("p t (k d) -> p t k d", k=2), src)
                do(v.tensor_copy(qs, qTs[:, j]).then_inc(q_staged, 1))

            def window_step(stage, j, i, name):
                kind = name.rstrip("0123")
                b = int(name[-1]) if kind in ("QK", "RD", "PV") else 0
                if kind == "QK":
                    v.wait_ge(*is_full(stage, name, i))
                    bk = bank_of(stage, name)
                    v.wait_ge(*was_full(stage, f"pT{b}", i))
                    ks = 0 if b else P
                    for kv in range(2):
                        ins = v.scalar_tensor_tensor(S[:, kv, ks:256], dist[:, ks:256], slope[:, bass.ds(AG * kv + j, 1)],
                                                     bk[:, kv * 256 + ks:kv * 256 + 256], ALU.mult, ALU.add)
                    ins.then_inc(FREE(stage, name), 1)
                    do(v.tensor_copy(S[:, :, 256:257], sinkb.rearrange("p (k g) -> p k g", k=2)[:, :, bass.ds(j, 1)]))
                    do(v.tensor_reduce(stat[:, 30:32], S[:, :, ks:257], AXX, ALU.max))
                    do(v.tensor_scalar(stat[:, 24:26], stat[:, 30:32], -1.0, None, ALU.mult).then_inc(neg_ready, 1))
                elif kind == "RD":
                    v.wait_ge(p_ready, 4 * j + (b + 1))
                    do(v.reciprocal(rden[:, b % 2], stat[:, 26:28]))
                elif kind == "PV":
                    v.wait_ge(*is_full(stage, name, i))
                    bk = bank_of(stage, name)
                    dst = Z[:, b, 0:AW].rearrange("p (k n) -> p k n", k=2)[:, :, bass.ds(AD * j, AD)]
                    do(v.tensor_tensor(dst, bk[:, 0:P].rearrange("p (k d) -> p k d", k=2),
                                       rden[:, b % 2].unsqueeze(2).to_broadcast([P, 2, AD]), ALU.mult).then_inc(FREE(stage, name), 1))
                elif kind == "Ss":
                    v.wait_ge(*is_full(stage, name, i))
                    bk = bank_of(stage, name)
                    v.tensor_tensor(Ss[:, 0:WIN], bk[:, 0:WIN], C("sbias"), ALU.add)
                    o = COFF["strip"][0] + 56
                    v.tensor_tensor(Ss[:, WIN:WIN + NS], bk[:, WIN:WIN + NS], cst[:, bass.ds(o - DEC_T * j, NS)], ALU.add)\
                        .then_inc(FREE(stage, name), 1)
                    do(v.tensor_copy(Ss[:, 192:193], sinkr))
                    do(v.tensor_reduce(stat[:, 37:38], Ss[:, 0:193], AXX, ALU.max))
                    do(v.tensor_scalar(stat[:, 28:29], stat[:, 37:38], -1.0, None, ALU.mult).then_inc(sneg_ready, 1))
                elif kind == "Sr":
                    v.wait_ge(sexp_done, j + 1)
                    do(v.reciprocal(stat[:, 38:39], stat[:, 29:30]))
                    do(v.tensor_scalar(Ss[:, 0:192], Ss[:, 0:192], stat[:, 38:39], None, ALU.mult).then_inc(sp_ready, 1))

            def gate_mul(stage, tag, i, n, L, dst, buf, sbuf):
                for t in range(NT):
                    v.wait_ge(*is_drained(stage, (tag, t), i))
                    d = dst(t)
                    do(v.tensor_tensor(d, d, buf[:, t % 2], ALU.mult).then_inc(gated, 1))
                v.wait_ge(w_used, L.at(GPC))
                sample_sum(sbuf[0:NS, :], bank[NT], FREE(stage, (tag, NT)))
                v.wait_ge(sil_ready, n + 1)
                d = dst(NT)
                do(v.tensor_tensor(d, d, sbuf[0:NS, :], ALU.mult).then_inc(gated, 1))

            for pair in range(4):
                stage = f"pair{pair}"
                if pair == 2:
                    for q in range(2):
                        v.wait_ge(*is_drained("mixv", (NT, q)))
                with v.Fori(0, 2) as i:
                    j = 2 * pair + i
                    e_stage(stage, j, i)
                    tasks = sorted([(p, n) for p, n in E_POINTS if n not in ("qT", "Kb")] + [(14, "Sr")] +
                                   [(12 + 8 * b, f"RD{b}") for b in range(NT)])
                    for _, n in tasks:
                        window_step(stage, j, i, n)
                    L = Lin(base + GPC * (3 + 2 * pair), GPC, i)
                    cols = bass.ds(AW + CW * i, CW)
                    if pair == 0:
                        v.wait_ge(w_used, L.at(GPC))
                        sample_sum(Z[0:NS, NT, cols], bank[NT], FREE(stage, ("acc", NT)))
                    elif pair == 1:
                        v.wait_ge(w_used, L.at(GPC))
                        sample_sum(SG[0:NS, NT, bass.ds(CW * i, CW)], bank[NT], FREE(stage, ("acc", NT)))
                    elif pair == 2:
                        for t in range(NT):
                            v.wait_ge(*is_full(stage, ("acc", t), i))
                            bk = bank_of(stage, ("acc", t))
                            do(v.tensor_tensor(Z[:, t, cols], bk[:, :], Z[:, t, cols], ALU.mult).then_inc(FREE(stage, ("acc", t)), 1))
                        v.wait_ge(w_used, L.at(GPC))
                        sample_sum(sils[0:NS, :], bank[NT], FREE(stage, ("acc", NT)))
                        do(v.tensor_tensor(Z[0:NS, NT, cols], Z[0:NS, NT, cols], sils[0:NS, :], ALU.mult))
                    else:
                        gate_mul(stage, "acc", i, i, L, lambda t: Z[0:rows(t), t, cols], sil, sils)
                if pair == 0:
                    for t in range(NT):
                        v.wait_ge(*is_drained(stage, ("acc", t), 1))
                    v.wait_ge(ln_in, 32)
                    for t in ALL:
                        r = rows(t)
                        for q in range(2):
                            v.bn_stats(bn[0:r, 6 * q:6 * q + 6], Z[0:r, t, AW + CW * q:AW + CW * (q + 1)])
                        v.drain()
                        do(v.bn_aggr(stat[0:r, 70 + 2 * t:72 + 2 * t], bn[0:r, :]))
                    var = stat[:, 70:80].rearrange("p (t a) -> p t a", a=2)[:, :, 1]
                    do(v.tensor_scalar(stat[:, 8:13], var, EPS, None, ALU.add).then_inc(var_ready, 1))
                    v.wait_ge(std_ready, plan.st["ln"] + 1)
                    newton(stat[:, 32:37], stat[:, 8:13], stat[:, 16:21], stat[:, 40:45])
                    for t in ALL:
                        r = rows(t)
                        z = Z[0:r, t, AW:D]
                        do(v.tensor_scalar(z, z, stat[0:r, 70 + 2 * t:71 + 2 * t], stat[0:r, 32 + t:33 + t], ALU.subtract, ALU.mult))
                        do(v.tensor_tensor(z, z, lng[0:r, :], ALU.mult))
                        do(v.tensor_tensor(z, z, lnb[0:r, :], ALU.add).then_inc(vn_ready, 1))
            v.wait_ge(sg_ready, 2)
            for t in range(NT):
                do(v.tensor_tensor(Z[:, t, 0:AW], Z[:, t, 0:AW], SG[:, t], ALU.mult).then_inc(z_ready, 1))
            zs = Z[0:NS, NT, 0:AW].rearrange("p (k g d) -> p g k d", k=2, d=AD)
            gs = SG[0:NS, NT].rearrange("p (k g d) -> p g k d", k=2, d=AD)
            for n in range(2):
                v.wait_ge(*is_full("epost", f"o{n}"))
                bk = bank_of("epost", f"o{n}")
                g = slice(4 * n, 4 * n + 4)
                do(v.tensor_tensor(zs[:, g], bk[0:NS, :].rearrange("p (g k d) -> p g k d", g=4, k=2), gs[:, g], ALU.mult)
                   .then_inc(FREE("epost", f"o{n}"), 1))
            do(v.tensor_copy(stat[0:NS, 88:89], stat[0:NS, 0:1]).then_inc(z_ready, 1))
            for t in ALL:
                xt_tile("zt", 4 * t, t)

            def residual(stage, tag, i, L, cols, groups, done=False):
                for t in range(NT):
                    v.wait_ge(*is_full(stage, (tag, t), i))
                    bk = bank_of(stage, (tag, t))
                    do(v.tensor_tensor(X[:, t, cols], bk[:, :], X[:, t, cols], ALU.add).then_inc(FREE(stage, (tag, t)), 1))
                v.wait_ge(w_used, L.at(groups))
                x = X[0:NS, NT, cols]
                do(v.tensor_tensor(x, bank[NT][0:NS, :], x, ALU.add))
                do(v.tensor_tensor(x, bank[NT][NS:2 * NS, :], x, ALU.add).then_inc(FREE(stage, (tag, NT)), 1))

            def x_complete():
                do(v.tensor_copy(stat[0:NS, 88:89], stat[0:NS, 0:1]).then_inc(x_done, 1))

            v.wait_ge(x_in, 160)
            with v.Fori(0, 4) as i:
                residual("eout", "acc", i, Lin(plan.groups["eout"], GPC, i), bass.ds(CW * i, CW), GPC)
            x_complete()

            def cross(l):
                st = f"x{l}"
                rms_scales(plan.st[st], 12 + 10 * l, 5)
                v.wait_ge(g_in, 64 + 32 * l)
                norm(st, ALL, X)
                v.wait_ge(w_used, Lin(plan.groups[st + "q"]).at(GPC))
                sample_sum(qc[0:NS, NT], bank[NT], FREE(st, ("acc", NT)))
                scale = XD ** -0.5

                def neg(t):
                    for q in range(2):
                        v.wait_ge(*is_full(st, f"S{t}{q}"))
                        bk = bank_of(st, f"S{t}{q}")
                        do(v.tensor_reduce(stat[:, 64 + 2 * q:66 + 2 * q], bk[:, :].rearrange("p (h n) -> p h n", n=MEM), AXX, ALU.max))
                    do(v.tensor_scalar(stat[:, 56 + 4 * (t % 2):60 + 4 * (t % 2)], stat[:, 64:68], -scale, None, ALU.mult).then_inc(cneg, 1))

                neg(0)
                for t in range(NT):
                    if t + 1 < NT:
                        neg(t + 1)
                    for q in range(2):
                        v.wait_ge(*is_drained(st, f"S{t}{q}"))
                    do(v.reciprocal(stat[:, 80:84], stat[:, 48 + 4 * (t % 2):52 + 4 * (t % 2)]))
                    v.wait_ge(*is_full(st, f"pT{t}1"))
                    bk = bank_of(st, f"pT{t}1")
                    do(v.tensor_copy(cpT[:, 4:8], bk[:, :].rearrange("p (a n) -> p a n", n=P)).then_inc(FREE(st, f"pT{t}1"), 1))
                    v.wait_ge(*is_full(st, f"PV{t}"))
                    bk = bank_of(st, f"PV{t}")
                    do(v.tensor_tensor(Ox.rearrange("p (h n) -> p h n", n=P), bk[:, :].rearrange("p (h n) -> p h n", n=P),
                                       stat[:, 80:84].unsqueeze(2).to_broadcast([P, XH, P]), ALU.mult).then_inc(FREE(st, f"PV{t}"), 1))
                    v.wait_ge(xt_hi_ready, plan.hi[st + "o"] + t + 1)
                    d = (slice(0, P), slice(0, XH), slice(t * P, (t + 1) * P))
                    do(v.tensor_tensor(xl[d], bank[4][:, :].rearrange("p (h n) -> p h n", n=P), xh[d].bitcast(F32), ALU.subtract)
                       .then_inc(FREE(st, f"oT{t}"), 1))
                for b in range(DEC_B):
                    v.wait_ge(*is_full(st, f"K{b}1"))
                    bk = bank_of(st, f"K{b}1")
                    do(v.tensor_copy(ckT[:, :, P:2 * P], bk[:, :].rearrange("p (h n) -> p h n", n=P)).then_inc(FREE(st, f"K{b}1"), 1))
                v.wait_ge(*is_full(st, "SR"))
                bk = bank_of(st, "SR")
                do(v.tensor_reduce(stat[:, 64:66], bk[:, :].rearrange("p (h n) -> p h n", n=MEM), AXX, ALU.max))
                do(v.tensor_scalar(stat[:, 56:58], stat[:, 64:66], -scale, None, ALU.mult).then_inc(cneg, 1))
                v.wait_ge(*is_drained(st, "SR"))
                do(v.reciprocal(stat[:, 80:82], stat[:, 48:50]))
                do(v.tensor_scalar(Px[:, 0], Px[:, 0], stat[:, 80:81], None, ALU.mult))
                do(v.tensor_scalar(Px[:, 1], Px[:, 1], stat[:, 81:82], None, ALU.mult).then_inc(cross_sp, 1))
                v.wait_ge(xt_hi_ready, plan.hi[st + "o"] + 5)
                do(v.tensor_tensor(xs[:, 0:XH, NS:2 * NS], bank[7][:, 0:XH * NS].rearrange("p (h n) -> p h n", n=NS),
                                   xs[:, 0:XH, 0:NS].bitcast(F32), ALU.subtract).then_inc(FREE(st, "OS"), 1))
                for n in range(4):
                    residual(st + "o", n, 0, Lin(plan.groups[st + "o"] + 2 * n), slice(CW * n, CW * (n + 1)), 2)
                x_complete()

            cross(0)
            rms_scales(plan.st["n1"], 17, 5)
            v.wait_ge(g_in, 80)
            norm("n1", ALL, X)
            v.wait_ge(x_saved, 80)
            v.wait_ge(zm_in, 16)
            base = plan.groups["ret"]
            v.wait_ge(w_used, Lin(base).at(GPC))
            sample_sum(QK[0:NS, NT], bank[NT], FREE("retA", ("acc", NT)))
            qd, qd2, kd, kz, gp = C("qd"), C("qd2"), C("kd"), C("kz", NS), C("gp")

            def values_step(stage, h, i, name):
                if name[0] == "S":
                    c = int(name[2])
                    r = rows(c)
                    if c == 0:
                        v.wait_ge(rd_in, 16 * h + 16)
                    v.wait_ge(*is_full(stage, name, i))
                    bk = bank_of(stage, name)
                    dec = rdec[:, 0:P] if c < NT else rdec[0:NS, P:P + NS]
                    do(v.tensor_tensor(STm[0:r, c, 0:r], bk[0:r, 0:r], dec, ALU.mult).then_inc(FREE(stage, name), 1))
                elif name == "T4":
                    v.wait_ge(*is_drained(stage, name, i))
                    for k in range(2):
                        ins = v.tensor_tensor(qz[:, k], qkT[:, k, SEQ:SEQ + NS].unsqueeze(1).to_broadcast([P, DEC_B, NS]), zm, ALU.mult)
                    do(ins.then_inc(qz_ready, 1))

            def decayed_keys(h, c):
                do(v.tensor_scalar(kdec[:, c % 2], QK[:, c, RK:2 * RK], kd[:, bass.ds(h, 1)], None, ALU.mult).then_inc(kdec_ready, 1))

            def batch_keys(h, b):
                do(v.tensor_scalar(kzb[0:NS, b % 2], QK[0:NS, NT, RK:2 * RK], kz[:, bass.ds(DEC_B * h + b, 1)], None, ALU.mult)
                   .then_inc(kz_ready, 1))

            def group_norm(h, c, bk, sem_free):
                r = rows(c)
                col = bass.ds(h, 1) if c < NT else bass.ds(h + RH, 1)
                do(v.bn_stats(bn[0:r, 0:6], bk[0:r, :]))
                do(v.bn_aggr(stat[0:r, 82:84], bn[0:r, 0:6]))
                do(v.tensor_scalar(stat[0:r, 65:66], stat[0:r, 83:84], qd2[0:r, col], EPS, ALU.mult, ALU.add).then_inc(var_ready, 1))
                v.wait_ge(std_ready, plan.st["gn"] + 1 + 5 * h + c)
                newton(stat[0:r, 84:85], stat[0:r, 65:66], stat[0:r, 66:67], stat[0:r, 85:86])
                do(v.tensor_scalar(stat[0:r, 84:85], stat[0:r, 84:85], qd[0:r, col], None, ALU.mult))
                do(v.tensor_scalar(ON[0:r, c], bk[0:r, :], stat[0:r, 82:83], stat[0:r, 84:85], ALU.subtract, ALU.mult).then_inc(sem_free, 1))

            def gates_step(stage, h, i, name):
                if name[0] == "O":
                    if name[1] == "I":
                        return
                    c = int(name[1])
                    v.wait_ge(*is_full(stage, name, i))
                    group_norm(h, c, bank_of(stage, name), FREE(stage, name))
                elif name[0] == "U":
                    c, m = int(name[1]), int(name[2])
                    v.wait_ge(*is_full(stage, name, i))
                    bk = bank_of(stage, name)
                    if c == 0:
                        do(v.tensor_copy(rstate[:, m], bk[:, :]).then_inc(FREE(stage, name), 1))
                    else:
                        do(v.scalar_tensor_tensor(rstate[:, m], rstate[:, m], gp[:, bass.ds(h, 1)], bk[:, :], ALU.mult, ALU.add)
                           .then_inc(FREE(stage, name), 1))
                    if m == 1 and c + 2 < NT:
                        decayed_keys(h, c + 2)
                else:
                    b, m = int(name[1]), int(name[2])
                    v.wait_ge(*is_full(stage, name, i))
                    bk = bank_of(stage, name)
                    do(v.scalar_tensor_tensor(Wst[:, b % 4, m], Wst[:, b % 4, m], gp[:, bass.ds(h + RH, 1)], bk[:, :], ALU.mult, ALU.add)
                       .then_inc(FREE(stage, name), 1))
                    if m == 1 and b + 2 < DEC_B:
                        batch_keys(h, b + 2)

            def head(stage, h, i, L):
                for _, n in RB_POINTS:
                    values_step(stage, h, i, n)
                decayed_keys(h, 0)
                decayed_keys(h, 1)
                batch_keys(h, 0)
                batch_keys(h, 1)
                v.wait_ge(w_used, L.at(GPC))
                sample_sum(V[0:NS, NT], bank[NT], FREE(stage, ("B", NT)))
                for _, n in RC_DRAINS:
                    gates_step(stage, h, i, n)
                v.wait_ge(*is_full(stage, "OI", i))
                group_norm(h, NT, bank_of(stage, "OI"), FREE(stage, "OI"))
                gate_mul(stage, "C", i, 2 + h, Lin(L.c + GPC, L.k, L.i), lambda t: ON[0:rows(t), t], sg, sgs)

            with v.Fori(0, RH - 1) as h:
                for t in range(NT):
                    v.wait_ge(*is_free("ret", ("B", t), h))
                head("ret", h, h, Lin(base + GPC, 3 * GPC, h))
                v.wait_ge(w_used, Lin(base + 3 * GPC, 3 * GPC, h).at(GPC))
                sample_sum(QK[0:NS, NT], bank[NT], FREE("ret", ("A", NT)))
                v.wait_ge(rstate_out, 16 * h + 16)
            h = RH - 1
            for t in range(NT):
                v.wait_ge(*is_free("retZ", ("B", t)))
            head("retZ", h, 0, Lin(base + GPC + 3 * GPC * h))
            def split_mix(half, g):
                k = slice(GK * g, GK * g + GK)
                v.wait_ge(mix_hi, GPC * half + g + 1)
                v.tensor_tensor(xh[:, k, :], xh[:, k, :].bitcast(F32), xl[:, k, :].bitcast(F32), ALU.subtract)
                do(v.tensor_tensor(xs[:, k, NS:2 * NS], xs[:, k, NS:2 * NS].bitcast(F32), xs[:, k, 0:NS].bitcast(F32), ALU.subtract)
                   .then_inc(mix_ready, 1))

            for g in range(GPC):
                split_mix(0, g)
            v.wait_ge(x_in, 240)
            base = plan.groups["rout"]
            with v.Fori(0, 3) as i:
                residual("rout", "acc", i, Lin(base, GPC, i), bass.ds(CW * i, CW), GPC)
            for g in range(GPC - 2):
                split_mix(1, g)
            residual("rout", "acc", 3, Lin(base + 3 * GPC), slice(3 * CW, 4 * CW), GPC)
            for g in (GPC - 2, GPC - 1):
                split_mix(1, g)
            with v.Fori(0, 4) as i:
                residual("rout", "acc", i + 4, Lin(base + 4 * GPC, GPC, i), bass.ds(CW * i, CW), GPC)
            x_complete()
            cross(1)
            rms_scales(plan.st["fin"], 27, 5)
            v.wait_ge(g_in, 112)
            for n, t in enumerate(ALL):
                if n >= 2:
                    v.wait_ge(y_out[n % 2], 16 * (n // 2))
                xn_tile(X, t, n)


_INS = ["x_prompt", "x_sample", "cache_win_k", "cache_win_v", "state_ret", "cache_mem_k", "cache_mem_v", "mem_prompt",
        "norm_mix", "w_in_even", "attn_sinks", "w_spatial", "b_spatial", "norm_v_g", "norm_v_b", "w_out_even",
        "w_in_ret", "w_out_ret", "norm_cross", "norm_mem", "w_xq", "w_xk", "w_xv", "w_xo", "norm_final"]
_OUTS = [("y_prompt", (1, SEQ, D)), ("y_sample", (DEC_B, DEC_T, D)),
         ("win_k_prompt", (1, 1, WIN, 2, AD)), ("win_v_prompt", (1, 1, WIN, 2, AD)),
         ("ret_state_prompt", (1, 1, RH, RK, RV)),
         ("mem_k_prompt", (2, 1, MEM, XH, XD)), ("mem_v_prompt", (2, 1, MEM, XH, XD)),
         ("win_k_sample", (1, DEC_B, WIN, 2, AD)), ("win_v_sample", (1, DEC_B, WIN, 2, AD)),
         ("ret_state_sample", (1, DEC_B, RH, RK, RV)), ("chunk_v", (1, DEC_B, DEC_T, BW))]


def kernel(**inputs):
    import numpy as _np
    import concourse.bacc as _bacc
    from concourse.bass_utils import run_bass_kernel_spmd as _run

    nc = _bacc.Bacc("TRN2", target_bir_lowering=False, num_devices=1, dynamic_dma_scratch_size=1024)
    arrays, I, O = {}, Bag(), Bag()
    given = {n: _np.ascontiguousarray(inputs[n]) for n in _INS}
    I.x_prompt, I.x_sample, I.cache_win_k, I.cache_win_v, I.state_ret, I.cache_mem_k, I.cache_mem_v, I.mem_prompt, \
        I.norm_mix, I.w_in_even, I.attn_sinks, I.w_spatial, I.b_spatial, I.norm_v_g, I.norm_v_b, I.w_out_even, \
        I.w_in_ret, I.w_out_ret, I.norm_cross, I.norm_mem, I.w_xq, I.w_xk, I.w_xv, I.w_xo, I.norm_final = [
            nc.dram_tensor(f"in_{n}", given[n].shape, F32, kind="ExternalInput").ap() for n in _INS]
    for n in _INS:
        arrays[f"in_{n}"] = given[n]
    c, rdec, zmask = shape_constants()
    aps = []
    for name, a in (("consts", c), ("ret_decay", rdec), ("batch_mask", zmask)):
        arrays[name] = a
        aps.append(nc.dram_tensor(name, a.shape, F32, kind="ExternalInput").ap())
    O.y_prompt, O.y_sample, O.win_k_prompt, O.win_v_prompt, O.ret_state_prompt, O.mem_k_prompt, O.mem_v_prompt, \
        O.win_k_sample, O.win_v_sample, O.ret_state_sample, O.chunk_v = [
            nc.dram_tensor(f"out_{n}", shape, F32, kind="ExternalOutput").ap() for n, shape in _OUTS]
    x_scratch = nc.dram_tensor("x_scratch", (SEQ + NS, D), F32).ap()
    mix_scratch = nc.dram_tensor("mix_scratch", (2 * KT, P, SEQ + NS), F32).ap()
    build(nc, I, O, *aps, x_scratch, mix_scratch)
    r = _run(nc, [arrays], core_ids=[0])
    return tuple(r.results[0][f"out_{n}"] for n, _ in _OUTS)
```

```python
from contextlib import ExitStack

import numpy as np

import concourse.bass as bass
from concourse import mybir

F32 = mybir.dt.float32
F32R = mybir.dt.float32r
ALU = mybir.AluOpType
ACT = mybir.ActivationFunctionType
AXX = mybir.AxisListType.X

P = 128
D = 2048
KT = D // P
SEQ = 512
DEC_B, DEC_T = 8, 8
NS = DEC_B * DEC_T
NT = SEQ // P
AH, AD, AG = 16, 64, 8
AW = AH * AD
WIN = 128
BW = D - AW
BG = 4
EVEN_IN = 2 * AW + 2 * 128 + 3 * BW
RH, RK, RV = 8, 256, 512
XH, XD, MEM = 4, 128, 256
XW = XH * XD
EPS = 1e-6
CW = 512
GK = 2
GPC = KT // GK
RING = 4
PT = NT + 1
MASKED = -1e33

CONSTS = dict(ident=128, dist=256, slope=16, sbias=128, strip=120, tril=128, smask=64, qd=16, qd2=16, kd=8, kz=64, gp=16)
COFF = {}
_o = 0
for _n, _w in CONSTS.items():
    COFF[_n] = (_o, _w)
    _o += _w
NCONST = _o


def shape_constants():
    c = np.zeros((P, NCONST), np.float32)

    def put(name, a):
        o, w = COFF[name]
        c[:a.shape[0], o:o + w] = a.reshape(a.shape[0], w)

    i = np.arange(P)
    put("ident", np.eye(P))
    dist = i[:, None] + WIN - np.arange(2 * WIN)[None]
    put("dist", np.where((dist >= 0) & (dist < WIN), -dist.astype(np.float64), MASKED))
    slopes = np.exp2(-8.0 * (np.arange(AH) + 1.0) / AH)
    put("slope", np.tile(slopes, (P, 1)))
    row_t = i % DEC_T
    row_slope = slopes[(i // 64) * AG + (i % 64) // DEC_T][:, None]
    d = WIN + row_t[:, None] - np.arange(WIN)[None]
    put("sbias", np.where(d < WIN, -d * row_slope, MASKED))
    x = np.arange(120)[None] - 56
    dn = row_t[:, None] - x
    put("strip", np.where((x >= 0) & (x < DEC_T) & (dn >= 0), -dn * row_slope, MASKED))
    put("tril", (i[None] <= i[:, None]).astype(np.float64))
    s = np.arange(NS)
    same = (s[:, None] // DEC_T) == (s[None] // DEC_T)
    put("smask", (same & (s[:, None] % DEC_T <= s[None] % DEC_T)).astype(np.float64))
    g = 1.0 - np.exp2(-5.0 - np.arange(RH))
    qd = np.zeros((P, 16))
    qd[:, :8] = g[None] ** (i[:, None] + 1)
    qd[:, 8:] = g[None] ** (row_t[:, None] + 1)
    put("qd", qd)
    put("qd2", qd ** 2)
    put("kd", g[None] ** (P - 1 - i[:, None]) * RK ** -0.5)
    kz = np.zeros((NS, RH, DEC_B))
    kz[s, :, s // DEC_T] = g[None] ** (DEC_T - 1 - s[:, None] % DEC_T) * RK ** -0.5
    put("kz", np.concatenate([kz.reshape(NS, -1)] * 2))
    put("gp", np.tile(np.concatenate([g ** P, g ** DEC_T]), (P, 1)))
    rdec = np.zeros((RH, P, P + NS), np.float32)
    rdec[:, :, :P] = np.where(i[None, :, None] <= i[None, None], g[:, None, None] ** (-i[None, :, None] - 1.0), 0) * RK ** -0.5
    rdec[:, :NS, P:] = np.where((same & (s[:, None] % DEC_T <= s[None] % DEC_T))[None],
                                g[:, None, None] ** (-(s % DEC_T)[None, :, None] - 1.0), 0) * RK ** -0.5
    zmask = np.zeros((P, DEC_B, NS), np.float32)
    for b in range(DEC_B):
        zmask[:, b, b * DEC_T:(b + 1) * DEC_T] = 1.0
    return c, rdec, zmask.reshape(P, DEC_B * NS)


class Bag:
    pass


class Lin:

    def __init__(self, c, k=0, i=0):
        self.c, self.k, self.i = c, k, i

    def at(self, d=0):
        return self.c + d + (self.k * self.i if self.k else 0)

    def quarter(self, d=0):
        return (self.c + d) // RING + ((self.k // RING) * self.i if self.k else 0)


class BankPlan:

    def __init__(self):
        self.uses, self.fulls, self.where = [0] * 8, [0] * 8, {}

    def add(self, stage, names, trips=1):
        u, f = [0] * 8, [0] * 8
        mine = []
        for name, bank, signals in names:
            mine.append((name, bank, self.uses[bank] + u[bank], self.fulls[bank] + f[bank]))
            u[bank] += 1
            f[bank] += signals
        for name, bank, n, m in mine:
            self.where[stage, name] = (bank, n, u[bank], m, f[bank])
        for b in range(8):
            self.uses[b] += trips * u[b]
            self.fulls[b] += trips * f[b]


XT_BANKS = [5, 6, 7, 0, 1, 2]


def acc_uses(tag, tiles):
    return [((tag, t), t, t != tiles[-1]) for t in tiles]


ALL = list(range(NT + 1))

E_POINTS = [(4, "qT"), (6, "Kb"), (10, "Ss"), (17, "pTs"), (25, "PVs")] + \
    [(7 + 8 * b, f"QK{b}") for b in range(NT)] + [(11 + 8 * b, f"pT{b}") for b in range(NT)] + \
    [(13 + 8 * b, f"PV{b}") for b in range(NT)]
E_POINTS.sort()
LN_AFTER = ["QK1", "QK3"]
E_BANK = dict(qT=5, Kb=7, Ss=7, pTs=7, PVs=7, QK=5, pT=6, PV=7)
RB_POINTS = [(2 + 4 * c, f"T{c}") for c in range(NT)] + [(5 + 4 * c, f"ST{c}") for c in range(NT)] + [(18, "T4"), (22, "ST4")]
RC_POINTS = [(2, "OI")] + [(4 + 9 * c, f"O{c}") for c in range(NT)] + \
    [(5 + 9 * c, f"U{c}0") for c in range(NT)] + [(7 + 9 * c, f"U{c}1") for c in range(NT)] + \
    [(p, f"W{b}0") for b, p in enumerate((3, 8, 12, 17, 21, 26, 30, 35))] + \
    [(p + 1, f"W{b}1") for b, p in enumerate((3, 8, 12, 17, 21, 26, 30, 35))]
RC_DRAINS = [(p + 3 if n[0] == "O" else p, n) for p, n in RC_POINTS]
RA_POINTS = [(4, "M00"), (8, "M01"), (12, "M02"), (18, "M10"), (22, "M11"), (26, "M12")]
RZ_POINTS = [(2 + 3 * n, name) for n, (_, name) in enumerate(RA_POINTS)]
for _l in (RB_POINTS, RC_POINTS, RC_DRAINS, RA_POINTS):
    _l.sort()


def r_bank(name):
    return {"T": 5, "S": 6, "O": 6, "U": 7, "W": 7, "M": 5 + (name[-1] == "1")}[name[0]]


def make_plan():
    plan = BankPlan()
    plan.groups = {}
    plan.st = {}
    state = Bag()
    state.g, state.xt, state.st, state.hi = 0, 0, 0, 0

    def weights(stage, chunks):
        plan.groups[stage] = state.g
        state.g += GPC * chunks

    def xt(stage, batches, first=0):
        for n in range(first, first + batches):
            plan.add(stage, [(("xt", n), XT_BANKS[state.xt % len(XT_BANKS)], True)])
            state.xt += 1
        highs(stage, batches)

    plan.hi = {}

    def highs(stage, n):
        plan.hi.setdefault(stage, state.hi)
        state.hi += n

    def sqrt(stage, n):
        plan.st[stage] = state.st
        state.st += n

    sqrt("mem", 1)
    weights("mem", 4)
    for l in range(2):
        xt("mem", 8, 8 * l)
        for c in (2 * l, 2 * l + 1):
            plan.add("mem", acc_uses(c, [2 * l, 2 * l + 1]))
    sqrt("n0", 1)
    xt("n0", 18)
    weights("even", 11)
    plan.add("kvq", [(n, b, s) for c in range(3) for n, b, s in acc_uses(c, ALL)])
    plan.add("epre", [("kT", 5, True), ("kTs", 6, True), ("qTs", 7, True), ("wsT", 5, True)])
    for pair in range(4):
        plan.add(f"pair{pair}", [(n, E_BANK[n.rstrip("0123")], True) for _, n in E_POINTS] + acc_uses("acc", ALL), trips=2)
        if pair == 1:
            sqrt("ln", 5)
            plan.add("mixv", [((t, q), 5 + q, True) for t in ALL for q in range(2)])
    plan.add("epost", [("o0", 5, True), ("o1", 6, True)])
    xt("zt", 18)
    weights("eout", 4)
    plan.add("eout", acc_uses("acc", ALL), trips=4)
    for layer in range(2):
        s = f"x{layer}"
        sqrt(s, 1)
        xt(s, 18)
        weights(s + "q", 1)
        plan.add(s, acc_uses("acc", ALL))
        plan.add(s, [("kT0", 5, True), ("kT1", 6, True)] + [(f"qT{t}", 5 + t % 2, True) for t in ALL])
        order = [(f"S0{q}", q, True) for q in range(2)]
        for t in range(NT):
            if t + 1 < NT:
                order += [(f"S{t + 1}{q}", 2 * ((t + 1) % 2) + q, True) for q in range(2)]
            order += [(f"pT{t}0", 5, True), (f"pT{t}1", 6, True), (f"PV{t}", 7, True), (f"oT{t}", 4, True)]
        plan.add(s, order)
        plan.add(s, [(f"K{b}{m}", (5 + m if b % 2 == 0 else m), True) for b in range(DEC_B) for m in range(2)] + [("SS", 7, True)])
        plan.add(s, [("PR", 6, True), ("OS", 7, True), ("oS", 5, True)])
        highs(s + "o", 5)
        weights(s + "o", 1)
        for c in range(4):
            plan.add(s + "o", acc_uses(c, ALL))
        if layer == 0:
            sqrt("n1", 1)
            xt("n1", 18)
            weights("ret", 3 * RH)
            plan.add("retA", acc_uses("acc", ALL))
            body = [(n, r_bank(n), True) for _, n in RB_POINTS] + acc_uses("B", ALL) + \
                [("OI", 5, True)] + [(n, r_bank(n), True) for _, n in RC_POINTS if n != "OI"] + acc_uses("C", ALL) + \
                [(n, r_bank(n), True) for _, n in RA_POINTS]
            plan.add("ret", body + acc_uses("A", ALL), trips=RH - 1)
            plan.add("retZ", body)
            sqrt("gn", RH * 5)
            weights("rout", 8)
            plan.add("rout", acc_uses("acc", ALL), trips=8)
    sqrt("fin", 1)
    plan.total = state.g
    return plan


PLAN = make_plan()


def build(nc, I, O, consts, rdec_d, zmask_d, x_scratch, mix_scratch):
    plan = PLAN
    with ExitStack() as ctx:
        def sb(name, shape, dt=F32):
            return ctx.enter_context(nc.sbuf_tensor(name, shape, dt))

        def sem(name):
            return ctx.enter_context(nc.semaphore(name))

        xh = sb("xT_hi", [P, KT, SEQ], F32R)
        xl = sb("xT_lo", [P, KT, SEQ], F32R)
        xs = sb("xT_sample", [P, KT, 2 * NS], F32R)
        raw = sb("w_raw", [P, RING, GK, CW])
        whi = sb("w_hi", [P, RING, GK, CW], F32R)
        wlo = sb("w_lo", [P, RING, GK, CW], F32R)
        cst = sb("cst", [P, NCONST])
        stat = sb("stat", [P, 96])
        bn = sb("bn", [P, 12])
        sq = sb("squares", [P, NT + 1, 4])
        split = sb("ret_split", [P, 4 * RK + CW], F32R)
        R1 = sb("R1", [P, 10240])
        R2 = sb("R2", [P, 13440])
        bank = [ctx.enter_context(nc.psum_tensor(f"bank{b}", [P, 512], F32)) for b in range(8)]

        def C(name, rows=P):
            o, w = COFF[name]
            return cst[0:rows, o:o + w]

        ident = C("ident")

        class Carve:
            def __init__(self, tensor, at=0, size=None):
                self.t, self.at = tensor, at

            def take(self, *shape):
                n = int(np.prod(shape))
                a = self.t[:, self.at:self.at + n]
                self.at += n
                assert self.at <= self.t.shape[1], (self.at, self.t.shape)
                if len(shape) == 2:
                    a = a.rearrange("p (a b) -> p a b", b=shape[1])
                elif len(shape) == 3:
                    a = a.rearrange("p (a b c) -> p a b c", b=shape[1], c=shape[2])
                return a

        X = R2[:, 0:5 * D].rearrange("p (t n) -> p t n", n=D)
        Z = R1[:, 0:5 * D].rearrange("p (t n) -> p t n", n=D)
        xg = Z
        c = Carve(R2, 5 * D)
        gbc, _, diag = c.take(D), c.take(512), c.take(NT + 1, P)
        memX = R1[:, 0:2 * D].rearrange("p (t n) -> p t n", n=D)
        memG = R1[:, 2 * D:4 * D].rearrange("p (t n) -> p t n", n=D)
        memKV = R1[:, 4 * D:5 * D].rearrange("p (c m n) -> p c m n", c=2, m=2)
        c = Carve(R2)
        KV, SG = c.take(5, 256), c.take(5, AW)
        qst, qT, kT = c.take(NT, P), c.take(SEQ), c.take(SEQ + NS)
        S = c.take(2, 260)
        pT, qTs, oTs = c.take(4, P), c.take(DEC_B, 64), c.take(AG, NS)
        qs, kTs, Kraw, Vraw = c.take(64), c.take(WIN + NS), c.take(P), c.take(P)
        Ss, pTs = c.take(196), c.take(2 * P)
        wsT, wsTs = c.take(BG, P), c.take(BG, NS)
        bs, bss, sinkb, sinkr = c.take(BG), c.take(BG), c.take(AH), c.take(1)
        rden = c.take(2, 2)
        sil, sils = c.take(2, CW), c.take(CW)
        gate_area = SG.rearrange("p t n -> p (t n)")
        lng, lnb = SG[:, 0:2, CW:], SG[:, 2:4, CW:]
        wraw = gate_area[:, 0:BG * P].rearrange("p (g n) -> p g n", n=P)
        c = Carve(R1)
        qc, cqT, ckT, Vm = c.take(5, XW), c.take(XH, SEQ + NS), c.take(XH, MEM), c.take(2, XW)
        qz_at = c.at
        Px, cpT, Ox = c.take(XH, MEM), c.take(8, P), c.take(XW)
        kTb = [ckT, R1[:, qz_at + 8 * 4 * NS:qz_at + 8 * 4 * NS + XH * MEM].rearrange("p (h n) -> p h n", h=XH)]
        cpz = Px.rearrange("p h n -> p (h n)").rearrange("p (s a n) -> p s a n", s=2, a=8)
        cqz = R1[:, qz_at:qz_at + 8 * 4 * NS].rearrange("p (h b n) -> p h b n", h=XH, b=DEC_B)
        c = Carve(R2, 5 * D)
        KVb = c.take(3, 2, XW)
        Vb = [qc[:, 0:2], qc[:, 2:4], Vm, KVb[:, 0], KVb[:, 1], KVb[:, 2],
              ckT.rearrange("p h m -> p (h m)").rearrange("p (m n) -> p m n", m=2), qc[:, 0:2]]
        c = Carve(R1)
        QK, V, ON, sg = c.take(5, CW), c.take(5, CW), c.take(5, CW), c.take(2, CW)
        sgs = c.take(CW)
        c = Carve(R2)
        mt, qkT, STm = c.take(GK, SEQ + NS), c.take(4, SEQ + NS), c.take(5, P)
        kdec, rstate, Wst = c.take(2, RK), c.take(2, RV), c.take(4, 2, RV)
        qz, zm, rdec = c.take(2, DEC_B, NS), c.take(DEC_B, NS), c.take(P + NS)
        kzb = split[:, 0:4 * RK].rearrange("p (s n) -> p s n", s=2)
        Vx = split[:, 4 * RK:]

        raw_loaded = [sem(f"raw_loaded{s}") for s in range(RING)]
        keys_loaded = [sem(f"keys_loaded{s}") for s in range(RING)]
        hi_ready, lo_ready, w_used = sem("hi_ready"), sem("lo_ready"), sem("w_used")
        full = [sem(f"full{b}") for b in range(8)]
        free = [sem(f"free{b}") for b in range(8)]
        waited = sem("waited")
        consts_in, mem_in, x_in, g_in = sem("consts_in"), sem("mem_in"), sem("x_in"), sem("gain_in")
        squares_done, var_ready, std_ready = sem("squares_done"), sem("var_ready"), sem("std_ready")
        xn_ready, xt_hi_ready, stat_zero = sem("xn_ready"), sem("xt_hi_ready"), sem("stat_zero")
        outs_done, x_saved = sem("outs_done"), sem("x_saved")
        mem_stored = [sem(f"mem_stored{n}") for n in range(2)]
        y_out, y_act, y_vec = sem("y_out"), sem("y_act"), sem("y_vec")
        x_done = sem("x_done")
        q_staged, neg_ready, p_ready = sem("q_staged"), sem("neg_ready"), sem("p_ready")
        sneg_ready, sexp_done, sp_ready = sem("sneg_ready"), sem("sexp_done"), sem("sp_ready")
        kb_in, vn_ready, small_in, ln_in = sem("kb_in"), sem("vn_ready"), sem("small_in"), sem("ln_in")
        ws_zeroed, ws_ready, sg_ready = sem("ws_zeroed"), sem("ws_ready"), sem("sg_ready")
        vn_out, z_ready = sem("vn_out"), sem("z_ready")
        sil_ready, gated = sem("sil_ready"), sem("gated")
        kT_used = sem("sample_keys_used")
        cqz_ready, cpz_ready = sem("cross_queries_ready"), sem("cross_probs_ready")
        cneg, cross_in, cross_sp, vb_used = sem("cross_neg"), sem("cross_in"), sem("cross_sample_p"), sem("vb_used")
        k_in = [sem(f"keys_in{s}") for s in range(3)]
        v_in = [sem(f"values_in{b}") for b in range(DEC_B)]
        rd_in, zm_in, kdec_ready, kz_ready, qz_ready = sem("rd_in"), sem("zm_in"), sem("kdec_ready"), sem("kz_ready"), sem("qz_ready")
        state_in = [sem(f"state_in{s}") for s in range(4)]
        state_out = [sem(f"state_out{s}") for s in range(4)]
        mt_out, rstate_out = sem("mt_out"), sem("rstate_out")
        mix_in = [sem(f"mix_in{g}") for g in range(GPC)]
        mix_hi, mix_ready, vx_ready = sem("mix_hi"), sem("mix_ready"), sem("vx_ready")

        def is_free(stage, name, i=0):
            b, n, _ = use(stage, name, i)
            return free[b], n + 1

        def is_full(stage, name, i=0):
            b, _, m = use(stage, name, i)
            return full[b], m + 1

        def is_drained(stage, name, i=0):
            b, n, _ = use(stage, name, i)
            return free[b], n + 2

        def was_full(stage, name, i=0):
            b, _, m = use(stage, name, i)
            return full[b], m

        def use(stage, name, i):
            b, n, per, m, fper = plan.where[stage, name]
            if isinstance(i, int):
                return b, n + per * i, m + fper * i
            return b, Lin(n, per, i).at(), Lin(m, fper, i).at()

        def bank_of(stage, name):
            return bank[plan.where[stage, name][0]]

        def FULL(stage, name):
            return full[plan.where[stage, name][0]]

        def FREE(stage, name):
            return free[plan.where[stage, name][0]]

        def rows(t):
            return P if t < NT else NS

        block = ctx.enter_context(nc.Block())

        @block.sync
        def _(sp):
            def group(L, g, w, k0, col, width=CW):
                if not (L.k == 0 and L.c + g < RING):
                    sp.wait_ge(lo_ready, L.at(g - RING + 1))
                src = w.rearrange("(k p) n -> p k n", p=P)[:, k0:k0 + GK, bass.ds(col, width)]
                sp.dma_start(raw[:, g % RING, :, 0:width], src).then_inc(raw_loaded[g % RING], 16)

            def chunk(L, w, col, width=CW, k0=0):
                for g in range(GPC):
                    group(L, g, w, k0 + GK * g, col, width)

            for l in range(2):
                for n, w in enumerate((I.w_xk, I.w_xv)):
                    chunk(Lin(plan.groups["mem"] + GPC * (2 * l + n)), w[l], 0)
            base = plan.groups["even"]
            w = I.w_in_even[0]
            chunk(Lin(base), w, AW, 256)
            with sp.Fori(0, 2) as i:
                chunk(Lin(base + GPC, GPC, i), w, CW * i)
            for pair, col in enumerate((2304 + BW, 1280, 2304, 2304 + 2 * BW)):
                with sp.Fori(0, 2) as i:
                    chunk(Lin(base + GPC * (3 + 2 * pair), GPC, i), w, col + CW * i)
            with sp.Fori(0, 4) as i:
                chunk(Lin(plan.groups["eout"], GPC, i), I.w_out_even[0], CW * i)

            def cross(l):
                chunk(Lin(plan.groups[f"x{l}q"]), I.w_xq[l], 0)
                for n in range(4):
                    for g in range(2):
                        group(Lin(plan.groups[f"x{l}o"]), 2 * n + g, I.w_xo[l], GK * g, CW * n)

            cross(0)
            wr = I.w_in_ret[0]
            base = plan.groups["ret"]

            def chunk_a(L, h):
                for g in range(GPC):
                    sp.wait_ge(lo_ready, L.at(g - RING + 1))
                    for n, loaded in enumerate((raw_loaded, keys_loaded)):
                        src = wr.rearrange("(k p) n -> p k n", p=P)[:, GK * g:GK * g + GK, bass.ds(n * RH * RK + RK * h, RK)]
                        sp.dma_start(raw[:, g % RING, :, n * RK:(n + 1) * RK], src).then_inc(loaded[g % RING], 16)

            def head(h, L):
                chunk(L, wr, 2 * RH * RK + RV * h)
                chunk(Lin(L.c + GPC, L.k, L.i), wr, 2 * RH * RK + RH * RV + RV * h)

            chunk_a(Lin(base), 0)
            with sp.Fori(0, RH - 1) as h:
                head(h, Lin(base + GPC, 3 * GPC, h))
                chunk_a(Lin(base + 3 * GPC, 3 * GPC, h), h + 1)
            head(RH - 1, Lin(base + GPC + 3 * GPC * (RH - 1)))
            for half in range(2):
                with sp.Fori(0, 4) as i:
                    chunk(Lin(plan.groups["rout"] + 4 * GPC * half, GPC, i), I.w_out_ret[0], CW * i, k0=KT * half)
            cross(1)
            for t in ALL:
                if t % 2:
                    sp.wait_ge(y_act, t // 2 + 1)
                else:
                    sp.wait_ge(y_vec, t // 2 + 1)
                dst = O.y_prompt[0, t * P:(t + 1) * P, :] if t < NT else O.y_sample.rearrange("b t d -> (b t) d")
                sp.dma_start(dst, xg[0:rows(t), t]).then_inc(y_out, 16)
            for s, n in ((mem_stored[0], 4), (mem_stored[1], 4), (outs_done, 6), (vn_out, 1), (x_saved, 5), (rstate_out, RH), (mt_out, 2 * RH), (y_out, 5)):
                sp.wait_ge(s, 16 * n)
            for s in state_out:
                sp.wait_ge(s, 16 * 2 * RH)

        @block.gpsimd
        def _(pool):
            with pool.Fori(0, plan.total // RING) as i:
                for s in range(RING):
                    pool.wait_ge(hi_ready, RING * i + (s + 1))
                    pool.tensor_tensor(wlo[:, s], raw[:, s], whi[:, s].bitcast(F32), ALU.subtract).then_inc(lo_ready, 1)

        @block.tensor
        def _(pe):
            def gemm(L, stage, tag, i=0, tiles=ALL, width=CW, groups=GPC, g0=0, between=None, parts=(xh, xl)):
                th, tl = parts
                for g in range(groups):
                    slot = (g0 + g) % RING
                    pe.wait_ge(lo_ready, L.at(g0 + g + 1))
                    hi, lo = whi[:, slot], wlo[:, slot]
                    for n, t in enumerate(tiles):
                        if between:
                            between(PT * g + n)
                        if g == 0:
                            pe.wait_ge(*is_free(stage, (tag, t), i))
                        acc = bank[t][:, 0:width]
                        for kk in range(GK):
                            k = GK * g + kk
                            first, last = g == 0 and kk == 0, g == groups - 1 and kk == GK - 1
                            if t < NT:
                                tok = slice(t * P, (t + 1) * P)
                                pe.matmul(acc, th[:, k, tok], hi[:, kk, 0:width], start=first, stop=False)
                                pe.matmul(acc, th[:, k, tok], lo[:, kk, 0:width], start=False, stop=False)
                                mm = pe.matmul(acc, tl[:, k, tok], hi[:, kk, 0:width], start=False, stop=last)
                            else:
                                pe.matmul(acc, xs[:, k, :], hi[:, kk, 0:width], start=first, stop=False)
                                mm = pe.matmul(acc, xs[:, k, :], lo[:, kk, 0:width], start=False, stop=last)
                        if t == tiles[-1]:
                            mm.then_inc(w_used, 1)
                        elif g == groups - 1:
                            mm.then_inc(full[t], 1)

            def wait_apart():
                pe.nop().then_inc(waited, 1)

            def tp(out, in_, n=P):
                return pe.transpose(out, in_, cst[0:n, 0:n])

            def xt_tile(stage, t, at, src):
                per, m = (4, P) if t < NT else (8, NS)
                for q in range(KT // per):
                    pe.wait_ge(*is_free(stage, ("xt", at + q)))
                    bk = bank_of(stage, ("xt", at + q))
                    for k in range(per):
                        mm = tp(bk[:, k * m:(k + 1) * m], src[0:m, (q * per + k) * P:(q * per + k + 1) * P], m)
                    mm.then_inc(FULL(stage, ("xt", at + q)), 1)

            def norm_tile(stage, at, src, scale, m):
                per = 4 if m == P else 8
                for q in range(KT // per):
                    pe.wait_ge(*is_free(stage, ("xt", at + q)))
                    bk = bank_of(stage, ("xt", at + q))
                    for k in range(per):
                        mm = pe.matmul(bk[:, k * m:(k + 1) * m], src[0:m, (q * per + k) * P:(q * per + k + 1) * P], scale[0:m, 0:m],
                                       start=True, stop=True)
                    mm.then_inc(FULL(stage, ("xt", at + q)), 1)

            def norm(stage, first_xn):
                for t in ALL:
                    pe.wait_ge(xn_ready, first_xn + t + 1)
                    norm_tile(stage, 4 * t, xg[:, t], diag[:, t], rows(t))

            def xt_done(stage, batches):
                pe.wait_ge(*is_drained(stage, ("xt", batches - 1)))

            pe.wait_ge(consts_in, 16)
            for l in range(2):
                for m in range(2):
                    pe.wait_ge(xn_ready, 2 * l + m + 1)
                    norm_tile("mem", 8 * l + 4 * m, memG[:, m], diag[:, m], P)
                xt_done("mem", 8 * l + 8)
                for ch in (2 * l, 2 * l + 1):
                    gemm(Lin(plan.groups["mem"] + GPC * ch), "mem", ch, tiles=[2 * l, 2 * l + 1])
            norm("n0", 4)
            xt_done("n0", 18)
            base = plan.groups["even"]
            for ch in range(3):
                gemm(Lin(base + GPC * ch), "kvq", ch, width=256 if ch == 0 else CW)

            for t in ALL:
                pe.wait_ge(*is_drained("kvq", (0, t)))
            pe.wait_ge(*is_free("epre", "kT"))
            bk = bank_of("epre", "kT")
            for b in range(NT):
                mm = tp(bk[:, b * P:(b + 1) * P], KV[:, b, 0:P])
            mm.then_inc(FULL("epre", "kT"), 1)
            pe.wait_ge(*is_free("epre", "kTs"))
            bk = bank_of("epre", "kTs")
            tp(bk[:, 0:NS], KV[0:NS, NT, 0:P], NS).then_inc(FULL("epre", "kTs"), 1)
            pe.wait_ge(*is_free("epre", "qTs"))
            bk = bank_of("epre", "qTs")
            for ch in (1, 2):
                pe.wait_ge(*is_drained("kvq", (ch, NT)))
            for g in range(AG):
                mm = tp(bk[:, g * NS:(g + 1) * NS], Z[0:NS, NT, g * P:(g + 1) * P], NS)
            mm.then_inc(FULL("epre", "qTs"), 1)
            pe.wait_ge(ws_ready, 1)
            pe.wait_ge(*is_free("epre", "wsT"))
            bk = bank_of("epre", "wsT")
            for g in range(BG):
                mm = tp(bk[:, g * P:(g + 1) * P], wraw[:, g])
            mm.then_inc(FULL("epre", "wsT"), 1)

            def window_step(stage, j, i, name):
                pe.wait_ge(*is_free(stage, name, i))
                bk = bank_of(stage, name)
                kind = name.rstrip("0123")
                b = int(name[-1]) if kind in ("QK", "pT", "PV") else 0
                if kind == "qT":
                    pe.wait_ge(q_staged, j + 1)
                    for n in range(NT):
                        mm = tp(bk[:, n * P:(n + 1) * P], qst[:, n])
                elif kind == "Kb":
                    pe.wait_ge(kb_in, 32 * j + 32)
                    mm = tp(bk[:, 0:P], Kraw)
                elif kind == "Ss":
                    wait_apart()
                    for kv in range(2):
                        h = slice(64 * kv, 64 * kv + 64)
                        mm = pe.matmul(bk[h, 0:WIN + NS], qs[h, :], kTs[h, :], start=True, stop=True)
                elif kind == "QK":
                    ks = 0 if b else P
                    for kv in range(2):
                        if kv:
                            pe.drain()
                        h = slice(64 * kv, 64 * kv + 64)
                        mm = pe.matmul(bk[:, kv * 256 + ks:kv * 256 + 256], qT[h, b * P:(b + 1) * P],
                                       kT[h, (b - 1) * P + ks:(b + 1) * P], start=True, stop=True)
                elif kind == "pT":
                    pe.wait_ge(p_ready, 4 * j + (b + 1))
                    for kv in range(2):
                        for kb in range(0 if b else 1, 2):
                            mm = tp(bk[:, (2 * kv + kb) * P:(2 * kv + kb + 1) * P], S[:, kv, kb * P:(kb + 1) * P])
                elif kind == "PV":
                    pe.wait_ge(*is_drained(stage, f"pT{b}", i))
                    for kv in range(2):
                        for kb in range(0 if b else 1, 2):
                            mm = pe.matmul(bk[:, kv * 64:kv * 64 + 64], pT[:, 2 * kv + kb],
                                           KV[:, b - 1 + kb, P + kv * 64:P + kv * 64 + 64],
                                           start=(kb == (0 if b else 1)), stop=(kb == 1))
                elif kind == "pTs":
                    pe.wait_ge(sp_ready, j + 1)
                    tp(bk[:, 0:P], Ss[:, 0:P])
                    mm = tp(bk[0:NS, P:2 * P], Ss[:, P:P + NS])
                else:
                    for kv in range(2):
                        h = slice(64 * kv, 64 * kv + 64)
                        pe.matmul(bk[h, 0:64], Vraw[:, h], pTs[:, h], start=True, stop=False)
                        mm = pe.matmul(bk[h, 0:64], KV[0:NS, NT, P + 64 * kv:P + 64 * kv + 64],
                                       pTs[0:NS, P + 64 * kv:P + 64 * kv + 64], start=False, stop=True)
                mm.then_inc(FULL(stage, name), 1)

            def window_steps(stage, j, i, step):
                for point, name in E_POINTS:
                    if point == step:
                        window_step(stage, j, i, name)

            for pair in range(4):
                stage = f"pair{pair}"
                with pe.Fori(0, 2) as i:
                    gemm(Lin(base + GPC * (3 + 2 * pair), GPC, i), stage, "acc", i,
                         between=lambda step: window_steps(stage, 2 * pair + i, i, step))
                if pair == 1:
                    for t in ALL:
                        pe.wait_ge(vn_ready, t + 1)
                        for q in range(2):
                            pe.wait_ge(*is_free("mixv", (t, q)))
                            bk = bank_of("mixv", (t, q))
                            for g in (2 * q, 2 * q + 1):
                                lhs = wsT[:, g] if t < NT else wsTs[0:NS, g]
                                mm = pe.matmul(bk[0:rows(t), (g % 2) * 256:(g % 2) * 256 + 256], lhs,
                                               Z[0:rows(t), t, AW + 256 * g:AW + 256 * g + 256], start=True, stop=True)
                            mm.then_inc(FULL("mixv", (t, q)), 1)
            for n in range(2):
                pe.wait_ge(*is_free("epost", f"o{n}"))
                bk = bank_of("epost", f"o{n}")
                if n == 0:
                    pe.wait_ge(*is_drained("pair3", "PVs", 1))
                for g in range(4):
                    mm = tp(bk[0:NS, g * P:(g + 1) * P], oTs[:, 4 * n + g])
                mm.then_inc(FULL("epost", f"o{n}"), 1)
            for t in ALL:
                if t < NT:
                    pe.wait_ge(gated, 5 + t + 1)
                else:
                    pe.wait_ge(z_ready, 1)
                xt_tile("zt", t, 4 * t, Z[:, t])
            xt_done("zt", 18)
            with pe.Fori(0, 4) as i:
                gemm(Lin(plan.groups["eout"], GPC, i), "eout", "acc", i)

            def cross(l):
                st = f"x{l}"
                norm(st, 9 + 10 * l)
                xt_done(st, 18)
                gemm(Lin(plan.groups[st + "q"]), st, "acc")
                pe.wait_ge(cross_in, 32 * (l + 1))
                for m in range(2):
                    pe.wait_ge(*is_free(st, f"kT{m}"))
                    bk = bank_of(st, f"kT{m}")
                    for h in range(XH):
                        mm = tp(bk[:, h * P:(h + 1) * P], KVb[:, 0, m, h * P:(h + 1) * P])
                    mm.then_inc(FULL(st, f"kT{m}"), 1)
                for t in ALL:
                    r = rows(t)
                    pe.wait_ge(*is_free(st, f"qT{t}"))
                    bk = bank_of(st, f"qT{t}")
                    if t < NT:
                        pe.wait_ge(*is_drained(st, ("acc", t)))
                    else:
                        pe.wait_ge(*is_drained(st, ("acc", NT)))
                    for h in range(XH):
                        mm = tp(bk[:, h * r:(h + 1) * r], qc[0:r, t, h * P:(h + 1) * P], r)
                    mm.then_inc(FULL(st, f"qT{t}"), 1)
                for t in ALL:
                    pe.wait_ge(*is_drained(st, f"qT{t}"))

                def scores(t):
                    for q in range(2):
                        pe.wait_ge(*is_free(st, f"S{t}{q}"))
                        bk = bank_of(st, f"S{t}{q}")
                        for h in (2 * q, 2 * q + 1):
                            mm = pe.matmul(bk[:, (h % 2) * MEM:(h % 2 + 1) * MEM], cqT[:, h, t * P:(t + 1) * P],
                                           ckT[:, h], start=True, stop=True)
                        mm.then_inc(FULL(st, f"S{t}{q}"), 1)

                scores(0)
                for t in range(NT):
                    if t + 1 < NT:
                        scores(t + 1)
                    for q in range(2):
                        pe.wait_ge(*is_free(st, f"pT{t}{q}"))
                        bk = bank_of(st, f"pT{t}{q}")
                        pe.wait_ge(*is_drained(st, f"S{t}{q}"))
                        for h in (2 * q, 2 * q + 1):
                            for m in range(2):
                                mm = tp(bk[:, (2 * (h % 2) + m) * P:(2 * (h % 2) + m + 1) * P], Px[:, h, m * P:(m + 1) * P])
                        mm.then_inc(FULL(st, f"pT{t}{q}"), 1)
                    pe.wait_ge(*is_free(st, f"PV{t}"))
                    bk = bank_of(st, f"PV{t}")
                    for q in range(2):
                        pe.wait_ge(*is_drained(st, f"pT{t}{q}"))
                    for h in range(XH):
                        for m in range(2):
                            mm = pe.matmul(bk[:, h * P:(h + 1) * P], cpT[:, 2 * h + m], Vm[:, m, h * P:(h + 1) * P],
                                           start=(m == 0), stop=(m == 1))
                    mm.then_inc(FULL(st, f"PV{t}"), 1)
                    pe.wait_ge(*is_free(st, f"oT{t}"))
                    bk = bank_of(st, f"oT{t}")
                    pe.wait_ge(*is_drained(st, f"PV{t}"))
                    for h in range(XH):
                        mm = tp(bk[:, h * P:(h + 1) * P], Ox[:, h * P:(h + 1) * P])
                    mm.then_inc(FULL(st, f"oT{t}"), 1)
                pe.wait_ge(*is_free(st, "SS"))
                ss = bank_of(st, "SS")

                def keys(b):
                    pe.wait_ge(k_in[(b + 1) % 3], 16 * ((3 if (b + 1) % 3 else 2) * l + b // 3 + 1))
                    for m in range(2):
                        pe.wait_ge(*is_free(st, f"K{b}{m}"))
                        bk = bank_of(st, f"K{b}{m}")
                        for h in range(XH):
                            mm = tp(bk[:, h * P:(h + 1) * P], KVb[:, (b + 1) % 3, m, h * P:(h + 1) * P])
                        mm.then_inc(FULL(st, f"K{b}{m}"), 1)

                keys(0)
                for b in range(DEC_B):
                    if b + 1 < DEC_B:
                        keys(b + 1)
                    for m in range(2):
                        pe.wait_ge(*is_drained(st, f"K{b}{m}"))
                    if b == 0:
                        pe.wait_ge(cqz_ready, l + 1)
                    for h in range(XH):
                        mm = pe.matmul(ss[NS * (h // 2):NS * (h // 2) + NS, (h % 2) * MEM:(h % 2 + 1) * MEM], cqz[:, h, b], kTb[b % 2][:, h],
                                       start=(b == 0 and h % 2 == 0), stop=(b == DEC_B - 1 and h % 2 == 1))
                    if b < DEC_B - 2:
                        mm.then_inc(kT_used, 1)
                mm.then_inc(FULL(st, "SS"), 1)
                pe.wait_ge(*is_free(st, "PR"))
                bk = bank_of(st, "PR")
                pe.wait_ge(cross_sp, l + 1)
                for m in range(2):
                    for half in range(2):
                        mm = tp(bk[:, m * 256 + half * P:m * 256 + (half + 1) * P], Px[:, half, m * P:(m + 1) * P])
                mm.then_inc(FULL(st, "PR"), 1)
                pe.wait_ge(*is_free(st, "OS"))
                bk = bank_of(st, "OS")
                last = (DEC_B - 1, XH - 1, 1)
                for b in range(DEC_B):
                    pe.wait_ge(cpz_ready, DEC_B * l + b + 1)
                    pe.wait_ge(v_in[b], 16 * (l + 1))
                    for h in range(XH):
                        for m in range(2):
                            mm = pe.matmul(bk[0:NS, h * P:(h + 1) * P], cpz[:, b % 2, 4 * m + 2 * (h % 2) + h // 2],
                                           Vb[b][:, m, h * P:(h + 1) * P], start=((b, h, m) == (0, 0, 0)), stop=((b, h, m) == last))
                    if b < DEC_B - 1:
                        mm.then_inc(vb_used, 1)
                mm.then_inc(FULL(st, "OS"), 1)
                pe.wait_ge(*is_free(st, "oS"))
                bk = bank_of(st, "oS")
                pe.wait_ge(*is_drained(st, "OS"))
                for h in range(XH):
                    mm = tp(bk[:, h * NS:(h + 1) * NS], Ox[0:NS, h * P:(h + 1) * P], NS)
                mm.then_inc(FULL(st, "oS"), 1)
                pe.wait_ge(*is_drained(st, "oS"))
                pe.wait_ge(*is_drained(st, f"oT{NT - 1}"))
                for n in range(4):
                    gemm(Lin(plan.groups[st + "o"]), st + "o", n, groups=2, g0=2 * n)

            cross(0)
            norm("n1", 14)
            xt_done("n1", 18)
            base = plan.groups["ret"]
            gemm(Lin(base), "retA", "acc")

            def retention_step(stage, h, i, name):
                kind = name[0]
                if kind == "W":
                    b, m = int(name[1]), int(name[2])
                    if m == 0:
                        pe.wait_ge(state_in[b % 4], 32 * h + (16 * (b // 4) + 16))
                        for k in range(2):
                            mm = pe.matmul(bank[5][0:NS, :], qz[:, k, b], Wst[:, b % 4, k], start=False, stop=(b == 7 and k == 1))
                        if b == 7:
                            mm.then_inc(FULL(stage, "OI"), 1)
                    pe.wait_ge(*is_free(stage, name, i))
                    bk = bank_of(stage, name)
                    pe.wait_ge(kz_ready, 8 * h + (b + 1))
                    if b == 0 and m == 0:
                        pe.wait_ge(vx_ready, h + 1)
                    for part in range(2):
                        mm = pe.matmul(bk[:, :], kzb[:, b % 2, part * RK + m * P:part * RK + (m + 1) * P], Vx,
                                       start=(part == 0), stop=(part == 1))
                    mm.then_inc(FULL(stage, name), 1)
                    return
                pe.wait_ge(*is_free(stage, name, i))
                bk = bank_of(stage, name)
                if kind == "T":
                    c = int(name[1])
                    r = rows(c)
                    if c == NT:
                        wait_apart()
                    for n in range(4):
                        mm = tp(bk[:, n * r:(n + 1) * r], QK[0:r, c, n * P:(n + 1) * P], r)
                elif kind == "S":
                    c = int(name[2])
                    r = rows(c)
                    pe.wait_ge(*is_drained(stage, f"T{c}", i))
                    for k in range(2):
                        mm = pe.matmul(bk[0:r, 0:r], qkT[:, 2 + k, c * P:c * P + r], qkT[:, k, c * P:c * P + r],
                                       start=(k == 0), stop=(k == 1))
                elif name == "OI":
                    pe.wait_ge(*is_drained(stage, ("B", NT), i))
                    pe.wait_ge(*is_drained(stage, "ST4", i))
                    pe.wait_ge(qz_ready, h + 1)
                    wait_apart()
                    pe.matmul(bk[0:NS, :], STm[0:NS, NT, 0:NS], V[0:NS, NT], start=True, stop=False)
                    return
                elif kind == "O":
                    c = int(name[1])
                    pe.wait_ge(*is_drained(stage, ("B", c), i))
                    mm = pe.matmul(bk[:, :], STm[:, c], V[:, c], start=True, stop=(c == 0))
                    if c:
                        pe.wait_ge(*is_drained(stage, f"U{c - 1}1", i))
                        for k in range(2):
                            mm = pe.matmul(bk[:, :], qkT[:, k, c * P:(c + 1) * P], rstate[:, k], start=False, stop=(k == 1))
                elif kind == "U":
                    c, m = int(name[1]), int(name[2])
                    pe.wait_ge(kdec_ready, 4 * h + (c + 1))
                    mm = pe.matmul(bk[:, :], kdec[:, c % 2, m * P:(m + 1) * P], V[:, c], start=True, stop=True)
                else:
                    half, q = int(name[1]), int(name[2])
                    pe.wait_ge(gated, 5 * h + 10 + (2 * q + 2 if q < 2 else 5))
                    if q < 2:
                        for k in range(2):
                            for n in range(2):
                                t = 2 * q + n
                                mm = tp(bk[:, k * 256 + n * P:k * 256 + (n + 1) * P], ON[:, t, (2 * half + k) * P:(2 * half + k + 1) * P])
                    else:
                        wait_apart()
                        for k in range(2):
                            mm = tp(bk[:, k * NS:(k + 1) * NS], ON[0:NS, NT, (2 * half + k) * P:(2 * half + k + 1) * P], NS)
                mm.then_inc(FULL(stage, name), 1)

            def retention_steps(points, stage, h, i, step):
                for point, name in points:
                    if point == step:
                        retention_step(stage, h, i, name)

            with pe.Fori(0, RH - 1) as h:
                gemm(Lin(base + GPC, 3 * GPC, h), "ret", "B", h, between=lambda step: retention_steps(RB_POINTS, "ret", h, h, step))
                gemm(Lin(base + 2 * GPC, 3 * GPC, h), "ret", "C", h, between=lambda step: retention_steps(RC_POINTS, "ret", h, h, step))
                gemm(Lin(base + 3 * GPC, 3 * GPC, h), "ret", "A", h, between=lambda step: retention_steps(RA_POINTS, "ret", h, h, step))
            h = RH - 1
            L = base + GPC + 3 * GPC * h
            gemm(Lin(L), "retZ", "B", between=lambda step: retention_steps(RB_POINTS, "retZ", h, 0, step))
            gemm(Lin(L + GPC), "retZ", "C", between=lambda step: retention_steps(RC_POINTS, "retZ", h, 0, step))

            def mixed_steps(half, step):
                if step % PT == 0:
                    pe.wait_ge(mix_ready, GPC * half + step // PT + 1)
                if half == 0:
                    retention_steps(RZ_POINTS, "retZ", RH - 1, 0, step)

            for half in range(2):
                L = plan.groups["rout"] + 4 * GPC * half
                gemm(Lin(L), "rout", "acc", 4 * half, between=lambda step: mixed_steps(half, step), parts=(xl, xh))
                with pe.Fori(1, 4) as i:
                    gemm(Lin(L, GPC, i), "rout", "acc", i + 4 * half, parts=(xl, xh))
            cross(1)

        @block.scalar
        def _(act):
            def hi(L, g):
                if L.k == 0 and L.c + g >= plan.total:
                    return
                s = (L.c + g) % RING
                act.wait_ge(raw_loaded[s], 16 * (L.quarter(g) + 1))
                head, inside = divmod(L.c + g - plan.groups["ret"], 3 * GPC)
                if 0 <= head < RH and inside < GPC:
                    act.wait_ge(keys_loaded[s], Lin(32 * head + 16 * (inside // RING + 1), 32 if L.k else 0, L.i).at())
                if not (L.k == 0 and L.c + g < RING):
                    act.wait_ge(w_used, L.at(g - RING + 1))
                act.activation(whi[:, s], raw[:, s], ACT.Copy).then_inc(hi_ready, 1)

            def chunk(L, groups=GPC, g0=0, between=None, evac=None):
                for g in range(groups):
                    if between:
                        between(range(PT * g, PT * (g + 1)))
                    if evac and g == groups - 1:
                        evac()
                    hi(L, g0 + g + RING)

            def copy(dst, src, **kw):
                return act.activation(dst, src, ACT.Copy, **kw)

            def xt_hi(stage, n, t, q):
                act.wait_ge(*is_full(stage, ("xt", n)))
                bk = bank_of(stage, ("xt", n))
                if t < NT:
                    dst = xh[:, 4 * q:4 * q + 4, t * P:(t + 1) * P]
                    src = bk[:, :].rearrange("p (k n) -> p k n", n=P)
                else:
                    dst = xs[:, 8 * q:8 * q + 8, 0:NS]
                    src = bk[:, :].rearrange("p (k n) -> p k n", n=NS)
                copy(dst, src).then_inc(xt_hi_ready, 1)

            def xt_all(stage, tiles):
                n = 0
                for t in tiles:
                    for q in range(4 if t < NT else 2):
                        xt_hi(stage, n, t, q)
                        n += 1

            def squares(src, tiles, junk):
                for t in tiles:
                    r = rows(t)
                    act.drain()
                    act.activation(junk[0:r, :], src[0:r, t], ACT.Square, accum_out=sq[0:r, t, 0:1]).then_inc(squares_done, 1)

            def chunk_squares(stage, tag, i, n):
                for t in ALL:
                    r = rows(t)
                    act.wait_ge(*is_drained(stage, (tag, t), i))
                    act.activation(bank[7][0:r, :], X[0:r, t, bass.ds(CW * n, CW)], ACT.Square, accum_out=sq[0:r, t, bass.ds(n, 1)])\
                        .then_inc(squares_done, 1)
                    act.drain()

            def sqrt(n, cols):
                act.wait_ge(var_ready, n + 1)
                act.activation(stat[:, 16:16 + cols], stat[:, 8:8 + cols], ACT.Sqrt).then_inc(std_ready, 1)

            def load_gain(g, xn_before):
                if xn_before:
                    act.wait_ge(xn_ready, xn_before)
                act.dma_start(gbc, g.partition_broadcast(P)).then_inc(g_in, 16)

            def load_x(scratch):
                for t in range(NT):
                    src = x_scratch[t * P:(t + 1) * P, :] if scratch else I.x_prompt[0, t * P:(t + 1) * P, :]
                    act.dma_start(X[:, t], src).then_inc(x_in, 16)
                src = x_scratch[SEQ:SEQ + NS, :] if scratch else I.x_sample.rearrange("b t d -> (b t) d")
                act.dma_start(X[0:NS, NT], src).then_inc(x_in, 16)

            act.dma_start(cst[:, :], consts).then_inc(consts_in, 16)
            for m in range(2):
                act.dma_start(memX[:, m], I.mem_prompt[0, m * P:(m + 1) * P, :]).then_inc(mem_in, 16)
            load_gain(I.norm_mem[0], 0)
            act.wait_ge(mem_in, 32)
            act.wait_ge(stat_zero, 1)
            squares(memX, [0, 1], Z[:, NT])
            load_x(False)
            sqrt(plan.st["mem"], 2)
            for s in range(RING):
                hi(Lin(0), s)

            def mem_evac(ch):
                l = ch // 2
                if ch >= 2:
                    act.wait_ge(mem_stored[ch % 2], 32)
                for m in range(2):
                    t = 2 * l + m
                    if m == 0:
                        act.wait_ge(*is_full("mem", (ch, t)))
                        bk = bank_of("mem", (ch, t))
                    else:
                        act.wait_ge(w_used, plan.groups["mem"] + GPC * (ch + 1))
                        bk = bank[t]
                    copy(memKV[:, ch % 2, m], bk[:, :]).then_inc(FREE("mem", (ch, t)), 1)
                act.drain()
                out = (O.mem_k_prompt, O.mem_v_prompt)[ch % 2]
                for m in range(2):
                    act.dma_start(out[l, 0, m * P:(m + 1) * P].rearrange("m h d -> m (h d)"), memKV[:, ch % 2, m]).then_inc(mem_stored[ch % 2], 16)

            for l in range(2):
                for m in range(2):
                    for q in range(4):
                        xt_hi("mem", 8 * l + 4 * m + q, 2 * l + m, q)
                load_gain((I.norm_mem[1], I.norm_mix[0])[l], 2 * l + 2)
                for ch in (2 * l, 2 * l + 1):
                    chunk(Lin(plan.groups["mem"] + GPC * ch), evac=lambda: mem_evac(ch))
                    if ch == 2:
                        act.wait_ge(x_in, 80)
                        squares(X, ALL, Z[:, 0])
                        sqrt(plan.st["n0"], 5)
            xt_all("n0", ALL)

            act.wait_ge(xn_ready, 9)
            act.wait_ge(ws_zeroed, 1)

            def small_loads(n):
                if n == 0:
                    for dst, src in ((wraw, I.w_spatial[0].rearrange("g i j -> i g j")), (sinkb, I.attn_sinks[0].partition_broadcast(P)),
                                     (bs, I.b_spatial[0].rearrange("g i -> i g"))):
                        act.dma_start(dst, src, allow_slow_non_contiguous=True).then_inc(small_in, 16)
                elif n < 16 and n % 2 == 0:
                    for hd in (n, n + 1):
                        act.dma_start(sinkr[hd * DEC_T:(hd + 1) * DEC_T, :], I.attn_sinks[0, hd:hd + 1].partition_broadcast(DEC_T))\
                            .then_inc(small_in, 16)
                elif n >= GPC * 2:
                    b = n - GPC * 2
                    r = slice(b * DEC_T, (b + 1) * DEC_T)
                    for g in range(BG):
                        act.dma_start(wsTs[r, g, r], I.w_spatial[0, g, 0:DEC_T, 0:DEC_T].rearrange("t j -> j t"),
                                      allow_slow_non_contiguous=True).then_inc(small_in, 16)
                    act.dma_start(bss[r, :], I.b_spatial[0, :, 0:DEC_T].rearrange("g t -> t g"),
                                  allow_slow_non_contiguous=True).then_inc(small_in, 16)
                if n == 1:
                    for hd in range(2):
                        act.dma_start(sinkr[hd * DEC_T:(hd + 1) * DEC_T, :], I.attn_sinks[0, hd:hd + 1].partition_broadcast(DEC_T))\
                            .then_inc(small_in, 16)

            base = plan.groups["even"]

            def kvq_evac(ch):
                for t in range(NT):
                    act.wait_ge(*is_full("kvq", (ch, t)))
                    bk = bank_of("kvq", (ch, t))
                    if ch == 0:
                        ins = copy(KV[:, t], bk[:, 0:256])
                    else:
                        ins = copy(Z[:, t, (ch - 1) * CW:ch * CW], bk[:, :], scale=AD ** -0.5)
                    ins.then_inc(FREE("kvq", (ch, t)), 1)

            for ch in range(3):
                chunk(Lin(base + GPC * ch), between=lambda steps: small_loads(GPC * ch + steps[0] // PT), evac=lambda: kvq_evac(ch))
            act.wait_ge(*is_full("epre", "kT"))
            bk = bank_of("epre", "kT")
            copy(kT[:, 0:SEQ], bk[:, :]).then_inc(FREE("epre", "kT"), 1)
            act.wait_ge(*is_full("epre", "kTs"))
            bk = bank_of("epre", "kTs")
            copy(kTs[:, WIN:WIN + NS], bk[:, 0:NS]).then_inc(FREE("epre", "kTs"), 1)
            act.wait_ge(*is_full("epre", "qTs"))
            bk = bank_of("epre", "qTs")
            copy(qTs.rearrange("p b (g t) -> p g b t", t=DEC_T), bk[:, :].rearrange("p (g b t) -> p g b t", g=AG, t=DEC_T))\
                .then_inc(FREE("epre", "qTs"), 1)
            act.wait_ge(*is_full("epre", "wsT"))
            bk = bank_of("epre", "wsT")
            copy(wsT, bk[:, :].rearrange("p (g n) -> p g n", n=P)).then_inc(FREE("epre", "wsT"), 1)
            act.wait_ge(*is_drained("kvq", (0, NT)))
            act.drain()
            for out, cache, o in ((O.win_k_sample, I.cache_win_k, 0), (O.win_v_sample, I.cache_win_v, P)):
                act.dma_start(out[0, :, 0:WIN - DEC_T].rearrange("b w k d -> b (w k d)"),
                              cache[0, :, DEC_T:WIN].rearrange("b w k d -> b (w k d)")).then_inc(outs_done, 16)
                act.dma_start(out[0, :, WIN - DEC_T:WIN].rearrange("b w k d -> b w (k d)"), KV[0:NS, NT, o:o + P]).then_inc(outs_done, 16)
            for out, o in ((O.win_k_prompt, 0), (O.win_v_prompt, P)):
                act.dma_start(out[0, 0].rearrange("w k d -> w (k d)"), KV[:, NT - 1, o:o + P]).then_inc(outs_done, 16)
            act.dma_start(lng, I.norm_v_g[0].partition_broadcast(P).rearrange("p (a n) -> p a n", a=2)).then_inc(ln_in, 16)
            act.dma_start(lnb, I.norm_v_b[0].partition_broadcast(P).rearrange("p (a n) -> p a n", a=2)).then_inc(ln_in, 16)

            def window_step(stage, j, i, name):
                kind = name.rstrip("0123")
                b = int(name[-1]) if kind in ("QK", "pT", "PV") else 0
                if kind == "QK":
                    act.drain()
                    act.wait_ge(neg_ready, 4 * j + (b + 1))
                    ks = 0 if b else P
                    for kv in range(2):
                        ins = act.activation(S[:, kv, ks:257], S[:, kv, ks:257], ACT.Exp, bias=stat[:, 24 + kv:25 + kv],
                                             accum_out=stat[:, 26 + kv:27 + kv])
                    ins.then_inc(p_ready, 1)
                elif kind == "Ss":
                    act.wait_ge(sneg_ready, j + 1)
                    act.activation(Ss[:, 0:193], Ss[:, 0:193], ACT.Exp, bias=stat[:, 28:29], accum_out=stat[:, 29:30])\
                        .then_inc(sexp_done, 1)
                elif kind != "PV":
                    act.wait_ge(*is_full(stage, name, i))
                    bk = bank_of(stage, name)
                    if kind == "qT":
                        ins = copy(qT, bk[:, :])
                    elif kind == "Kb":
                        ins = copy(kTs[:, 0:P], bk[:, 0:P])
                    elif kind == "pT":
                        src = bk[:, :].rearrange("p (a n) -> p a n", n=P)
                        ins = copy(pT, src) if b else copy(pT[:, 1:4:2], src[:, 1:4:2])
                    elif kind == "pTs":
                        copy(pTs[:, 0:P], bk[:, 0:P])
                        ins = copy(pTs[0:NS, P:2 * P], bk[0:NS, P:2 * P])
                    else:
                        ins = copy(oTs.rearrange("p g (b t) -> p g b t", t=DEC_T)[:, :, j], bk[:, 0:NS].rearrange("p (g t) -> p g t", t=DEC_T))
                    ins.then_inc(FREE(stage, name), 1)

            def window_steps(stage, j, i, steps):
                for point, name in E_POINTS:
                    if point in steps:
                        window_step(stage, j, i, name)
                        if stage == "pair1" and name in LN_AFTER:
                            norm_sqrt(2 * i + (LN_AFTER.index(name) + 1))

            def gate_evac(stage, tag, i, n, buf, sbuf):
                for t in range(NT):
                    act.wait_ge(*is_full(stage, (tag, t), i))
                    bk = bank_of(stage, (tag, t))
                    if t >= 2:
                        act.wait_ge(gated, 5 * n + (t - 1))
                    act.activation(buf[:, t % 2], bk[:, :], ACT.Silu).then_inc(FREE(stage, (tag, t)), 1)
                act.wait_ge(*is_drained(stage, (tag, NT), i))
                act.activation(sbuf[0:NS, :], sbuf[0:NS, :], ACT.Silu).then_inc(sil_ready, 1)

            def norm_sqrt(n):
                act.wait_ge(var_ready, plan.st["ln"] + n + 1)
                act.activation(stat[:, 36:37], stat[:, 35:36], ACT.Sqrt).then_inc(std_ready, 1)

            def pair_evac(stage, pair, i):
                if pair == 3:
                    return gate_evac(stage, "acc", i, i, sil, sils)
                if pair == 2:
                    return
                for t in range(NT):
                    act.wait_ge(*is_full(stage, ("acc", t), i))
                    bk = bank_of(stage, ("acc", t))
                    if pair == 1 and t == 0:
                        act.wait_ge(vn_ready, 2 * i + 3)
                    if pair == 0:
                        ins = copy(Z[:, t, bass.ds(AW + CW * i, CW)], bk[:, :])
                    else:
                        ins = act.activation(SG[:, t, bass.ds(CW * i, CW)], bk[:, :], ACT.Silu)
                    ins.then_inc(FREE(stage, ("acc", t)), 1)
                if pair == 1:
                    act.wait_ge(*is_drained(stage, ("acc", NT), i))
                    g = SG[0:NS, NT, bass.ds(CW * i, CW)]
                    act.activation(g, g, ACT.Silu).then_inc(sg_ready, 1)

            for pair in range(4):
                stage = f"pair{pair}"
                with act.Fori(0, 2) as i:
                    j = 2 * pair + i
                    for dst, src in ((Kraw, I.cache_win_k), (Vraw, I.cache_win_v)):
                        act.dma_start(dst, src[0].rearrange("b w k d -> b w (k d)")[j]).then_inc(kb_in, 16)
                    chunk(Lin(base + GPC * (3 + 2 * pair), GPC, i),
                          between=lambda steps: window_steps(stage, j, i, steps),
                          evac=lambda: pair_evac(stage, pair, i))
                if pair == 0:
                    norm_sqrt(0)
                if pair == 1:
                    act.wait_ge(vn_ready, 5)
                    act.dma_start(O.chunk_v[0].rearrange("b t n -> (b t) n"), Z[0:NS, NT, AW:D]).then_inc(vn_out, 16)
                    for t in ALL:
                        r = rows(t)
                        for q in range(2):
                            act.wait_ge(*is_full("mixv", (t, q)))
                        if t == NT:
                            act.wait_ge(vn_out, 16)
                        for g in range(BG):
                            bias = bs[:, g:g + 1] if t < NT else bss[0:r, g:g + 1]
                            ins = act.activation(Z[0:r, t, AW + 256 * g:AW + 256 * g + 256],
                                                 bank_of("mixv", (t, g // 2))[0:r, (g % 2) * 256:(g % 2) * 256 + 256], ACT.Identity, bias=bias)
                            if g % 2:
                                ins.then_inc(FREE("mixv", (t, g // 2)), 1)
            xt_all("zt", ALL)
            act.wait_ge(outs_done, 16 * 6)
            load_x(False)
            load_gain(I.norm_cross[0], 9)
            with act.Fori(0, 4) as i:
                chunk(Lin(plan.groups["eout"], GPC, i))
                chunk_squares("eout", "acc", i, i)

            def cross(l):
                st = f"x{l}"
                sqrt(plan.st[st], 5)
                for n in range(2):
                    act.wait_ge(mem_stored[n], 16 * 4)
                act.wait_ge(xn_ready, 9 + 10 * l + 1)
                act.dma_start(KVb[:, 0], O.mem_k_prompt[l, 0].rearrange("(m p) h d -> p m (h d)", p=P)).then_inc(cross_in, 16)

                def load_k(b):
                    s = (b + 1) % 3
                    act.dma_start(KVb[:, s], I.cache_mem_k[l, b].rearrange("(m p) h d -> p m (h d)", p=P)).then_inc(k_in[s], 16)

                def load_v(b):
                    act.dma_start(Vb[b], I.cache_mem_v[l, b].rearrange("(m p) h d -> p m (h d)", p=P)).then_inc(v_in[b], 16)

                load_k(0)
                xt_all(st, ALL)
                load_k(1)
                act.dma_start(Vm, O.mem_v_prompt[l, 0].rearrange("(m p) h d -> p m (h d)", p=P)).then_inc(cross_in, 16)

                def q_evac():
                    for t in range(NT):
                        act.wait_ge(*is_full(st, ("acc", t)))
                        bk = bank_of(st, ("acc", t))
                        copy(qc[:, t], bk[:, :]).then_inc(FREE(st, ("acc", t)), 1)

                chunk(Lin(plan.groups[st + "q"]), evac=q_evac)
                for m in range(2):
                    act.wait_ge(*is_full(st, f"kT{m}"))
                    bk = bank_of(st, f"kT{m}")
                    copy(ckT[:, :, m * P:(m + 1) * P], bk[:, :].rearrange("p (h n) -> p h n", n=P)).then_inc(FREE(st, f"kT{m}"), 1)
                load_k(2)
                for t in ALL:
                    r = rows(t)
                    act.wait_ge(*is_full(st, f"qT{t}"))
                    bk = bank_of(st, f"qT{t}")
                    copy(cqT[:, :, t * P:t * P + r], bk[:, 0:XH * r].rearrange("p (h n) -> p h n", n=r)).then_inc(FREE(st, f"qT{t}"), 1)
                load_v(0)
                load_v(1)
                for t in range(NT):
                    act.wait_ge(cneg, 5 * l + t + 1)
                    for q in range(2):
                        act.wait_ge(*was_full(st, f"pT{t}{q}"))
                    for h in range(XH):
                        bk = bank[2 * (t % 2) + h // 2]
                        ins = act.activation(Px[:, h], bk[:, (h % 2) * MEM:(h % 2 + 1) * MEM], ACT.Exp, scale=XD ** -0.5,
                                             bias=stat[:, 56 + 4 * (t % 2) + h:57 + 4 * (t % 2) + h],
                                             accum_out=stat[:, 48 + 4 * (t % 2) + h:49 + 4 * (t % 2) + h])
                        if h % 2:
                            ins.then_inc(FREE(st, f"S{t}{h // 2}"), 1)
                    act.wait_ge(*is_full(st, f"pT{t}0"))
                    bk = bank_of(st, f"pT{t}0")
                    copy(cpT[:, 0:4], bk[:, :].rearrange("p (a n) -> p a n", n=P)).then_inc(FREE(st, f"pT{t}0"), 1)
                    act.wait_ge(*is_full(st, f"oT{t}"))
                    bk = bank_of(st, f"oT{t}")
                    copy(xh[:, 0:XH, t * P:(t + 1) * P], bk[:, :].rearrange("p (h n) -> p h n", n=P)).then_inc(xt_hi_ready, 1)
                for b in range(DEC_B):
                    act.wait_ge(*is_full(st, f"K{b}0"))
                    bk = bank_of(st, f"K{b}0")
                    if b >= 2:
                        act.wait_ge(kT_used, 6 * l + b - 1)
                    copy(kTb[b % 2][:, :, 0:P], bk[:, :].rearrange("p (h n) -> p h n", n=P)).then_inc(FREE(st, f"K{b}0"), 1)
                    act.wait_ge(*is_full(st, f"K{b}1"))
                    if b + 3 < DEC_B:
                        load_k(b + 3)
                    else:
                        load_v(b - 2)
                    if b == 0:
                        load_v(2)
                act.wait_ge(*is_full(st, "SS"))
                load_v(6)
                act.wait_ge(cneg, 5 * l + 5)
                for half in range(2):
                    ins = act.activation(Px[:, half], bank_of(st, "SS")[:, half * MEM:(half + 1) * MEM], ACT.Exp, scale=XD ** -0.5,
                                         bias=stat[:, 56 + half:57 + half], accum_out=stat[:, 48 + half:49 + half])
                ins.then_inc(FREE(st, "SS"), 1)
                act.wait_ge(vb_used, 7 * l + 1)
                load_v(7)
                act.wait_ge(*is_full(st, "OS"))
                copy(Ox[0:NS, :], bank_of(st, "OS")[0:NS, :]).then_inc(FREE(st, "OS"), 1)
                act.wait_ge(*is_full(st, "oS"))
                copy(xs[:, 0:XH, 0:NS], bank_of(st, "oS")[:, 0:XH * NS].rearrange("p (h n) -> p h n", n=NS)).then_inc(xt_hi_ready, 1)
                load_gain((I.norm_mix[1], I.norm_final)[l], 9 + 10 * l + 5)
                for n in range(4):
                    chunk(Lin(plan.groups[st + "o"]), groups=2, g0=2 * n)
                    chunk_squares(st + "o", n, 0, n)

            cross(0)
            sqrt(plan.st["n1"], 5)
            act.wait_ge(x_done, 2)
            for t in ALL:
                r = rows(t)
                act.dma_start(x_scratch[t * P:t * P + r, :], X[0:r, t]).then_inc(x_saved, 16)
            xt_all("n1", ALL)
            act.wait_ge(xn_ready, 19)
            act.wait_ge(x_saved, 80)
            act.dma_start(zm.rearrange("p b n -> p (b n)"), zmask_d).then_inc(zm_in, 16)

            def qk_evac(stage, i):
                for t in range(NT):
                    act.wait_ge(*is_full(stage, (("A" if stage != "retA" else "acc"), t), i))
                    bk = bank_of(stage, (("A" if stage != "retA" else "acc"), t))
                    copy(QK[:, t], bk[:, :]).then_inc(FREE(stage, (("A" if stage != "retA" else "acc"), t)), 1)

            def v_evac(stage, i):
                for t in range(NT):
                    act.wait_ge(*is_full(stage, ("B", t), i))
                    bk = bank_of(stage, ("B", t))
                    copy(V[:, t], bk[:, :]).then_inc(FREE(stage, ("B", t)), 1)

            def load_state(h, b):
                src = I.state_ret[0].rearrange("b h (k p) e -> b h p k e", p=P)[b, h]
                act.dma_start(Wst[:, b % 4], src).then_inc(state_in[b % 4], 16)

            def head_start(stage, h, i):
                _, n, _ = use(stage, "ST0", i)
                act.wait_ge(free[6], n)
                act.dma_start(rdec, rdec_d[h]).then_inc(rd_in, 16)

            def values_step(stage, h, i, name):
                if name[0] == "T":
                    c = int(name[1])
                    r = rows(c)
                    act.wait_ge(*is_full(stage, name, i))
                    bk = bank_of(stage, name)
                    copy(qkT[:, :, c * P:c * P + r], bk[:, 0:4 * r].rearrange("p (a n) -> p a n", n=r)).then_inc(FREE(stage, name), 1)

            def gates_step(stage, h, i, name):
                if name[0] == "O" and name[1] != "I":
                    act.wait_ge(var_ready, plan.st["gn"] + 1 + 5 * h + int(name[1]))
                    act.activation(stat[:, 66:67], stat[:, 65:66], ACT.Sqrt).then_inc(std_ready, 1)
                elif name[0] == "W" and name[2] == "1":
                    b = int(name[1])
                    act.wait_ge(*is_drained(stage, f"W{b}1", i))
                    dst = O.ret_state_sample[0].rearrange("b h (k p) e -> b h p k e", p=P)[b, h]
                    act.dma_start(dst, Wst[:, b % 4]).then_inc(state_out[b % 4], 16)
                    if 1 <= b < 5:
                        act.wait_ge(state_out[(b - 1) % 4], 32 * h + 16)
                        load_state(h, b + 3)
                elif name == "U31":
                    act.wait_ge(*is_drained(stage, "U31", i))
                    dst = O.ret_state_prompt[0, 0].rearrange("h (k p) e -> h p k e", p=P)[h]
                    act.dma_start(dst, rstate).then_inc(rstate_out, 16)

            def c_evac(stage, h, i):
                act.wait_ge(var_ready, plan.st["gn"] + 5 + 5 * h)
                act.activation(stat[0:NS, 66:67], stat[0:NS, 65:66], ACT.Sqrt).then_inc(std_ready, 1)
                gate_evac(stage, "C", i, 2 + h, sg, sgs)

            def mixed_step(stage, h, i, name):
                half, q = int(name[1]), int(name[2])
                if q == 0 and half:
                    act.wait_ge(mt_out, 32 * h + 16)
                act.wait_ge(*is_full(stage, name, i))
                bk = bank_of(stage, name)
                if q < 2:
                    dst, src = mt[:, :, q * 256:q * 256 + 256], bk[:, :].rearrange("p (k n) -> p k n", k=2)
                else:
                    dst, src = mt[:, :, SEQ:SEQ + NS], bk[:, 0:2 * NS].rearrange("p (k n) -> p k n", k=2)
                copy(dst, src).then_inc(FREE(stage, name), 1)
                if q == 2:
                    act.drain()
                    act.dma_start(mix_scratch[bass.ds(4 * h + 2 * half, 2)].rearrange("k p n -> p k n"), mt).then_inc(mt_out, 16)

            def load_mix(half, g):
                k = slice(GK * g, GK * g + GK)
                src = mix_scratch[KT * half + GK * g:KT * half + GK * g + GK].rearrange("k p n -> p k n")
                act.dma_start(xh[:, k, :].bitcast(F32), src[:, :, 0:SEQ]).then_inc(mix_in[g], 16)
                act.dma_start(xs[:, k, NS:2 * NS].bitcast(F32), src[:, :, SEQ:SEQ + NS]).then_inc(mix_in[g], 16)

            def split_mix(half, g):
                k = slice(GK * g, GK * g + GK)
                act.wait_ge(mix_in[g], 32 * (half + 1))
                copy(xl[:, k, :], xh[:, k, :].bitcast(F32))
                copy(xs[:, k, 0:NS], xs[:, k, NS:2 * NS].bitcast(F32)).then_inc(mix_hi, 1)

            base = plan.groups["ret"]
            chunk(Lin(base), evac=lambda: qk_evac("retA", 0))

            def retention_steps(step, points, stage, h, i, steps):
                for point, name in points:
                    if point in steps:
                        step(stage, h, i, name)

            for b in range(4):
                load_state(0, b)
            with act.Fori(0, RH - 1) as h:
                head_start("ret", h, h)
                chunk(Lin(base + GPC, 3 * GPC, h), between=lambda steps: retention_steps(values_step, RB_POINTS, "ret", h, h, steps), evac=lambda: v_evac("ret", h))
                chunk(Lin(base + 2 * GPC, 3 * GPC, h), between=lambda steps: retention_steps(gates_step, RC_DRAINS, "ret", h, h, steps), evac=lambda: c_evac("ret", h, h))
                chunk(Lin(base + 3 * GPC, 3 * GPC, h), between=lambda steps: retention_steps(mixed_step, RA_POINTS, "ret", h, h, steps), evac=lambda: qk_evac("ret", h))
                act.wait_ge(mt_out, 32 * h + 32)
                for b in range(4):
                    act.wait_ge(state_out[b], 32 * h + 32)
                    load_state(h + 1, b)
            h = RH - 1
            head_start("retZ", h, 0)
            chunk(Lin(base + GPC + 3 * GPC * h), between=lambda steps: retention_steps(values_step, RB_POINTS, "retZ", h, 0, steps), evac=lambda: v_evac("retZ", 0))
            L = Lin(base + 2 * GPC + 3 * GPC * h)
            for g in range(GPC):
                retention_steps(gates_step, RC_DRAINS, "retZ", h, 0, range(PT * g, PT * (g + 1)))
                if g == GPC - 1:
                    c_evac("retZ", h, 0)
                hi(L, g + RING)
                load_mix(0, g)
                if 2 <= g < GPC - 1:
                    split_mix(0, g - 2)
            for g in range(GPC - 3, GPC):
                split_mix(0, g)
            for g in range(GPC):
                retention_steps(mixed_step, RZ_POINTS, "retZ", h, 0, range(PT * g, PT * (g + 1)))
                if g == 4:
                    act.wait_ge(mt_out, 16 * 2 * RH)
                    act.wait_ge(rstate_out, 16 * RH)
                    for slot in range(4):
                        act.wait_ge(state_out[slot], 32 * RH)
                    load_x(True)
                    load_gain(I.norm_cross[1], 19)
                hi(Lin(plan.groups["rout"]), g + RING)
            base = plan.groups["rout"]
            with act.Fori(1, 3) as i:
                chunk(Lin(base, GPC, i))
            for g in range(GPC):
                hi(Lin(base + 3 * GPC), g + RING)
                load_mix(1, g)
                if g >= 2:
                    split_mix(1, g - 2)
            for g in (GPC - 2, GPC - 1):
                split_mix(1, g)
            with act.Fori(0, 4) as i:
                chunk(Lin(base + 4 * GPC, GPC, i))
                chunk_squares("rout", "acc", i + 4, i)
            cross(1)
            sqrt(plan.st["fin"], 5)
            act.wait_ge(xn_ready, 25)
            for t in (1, 3):
                copy(xg[:, t], xg[:, t], scale=stat[:, 32 + t:33 + t]).then_inc(y_act, 1)

        @block.vector
        def _(v):
            def do(ins):
                v.drain()
                return ins

            def newton(dst, var, std, tmp):
                do(v.reciprocal(dst, std))
                do(v.tensor_tensor(tmp, dst, dst, ALU.mult))
                do(v.scalar_tensor_tensor(tmp, tmp, -0.5, var, ALU.mult, ALU.mult))
                do(v.tensor_scalar(tmp, tmp, 1.5, None, ALU.add))
                do(v.tensor_tensor(dst, dst, tmp, ALU.mult))

            def rms_scales(n, squares, cols):
                v.wait_ge(squares_done, squares)
                do(v.tensor_reduce(stat[:, 0:cols], sq[:, 0:cols], AXX, ALU.add))
                do(v.tensor_scalar(stat[:, 8:8 + cols], stat[:, 0:cols], 1.0 / D, EPS, ALU.mult, ALU.add).then_inc(var_ready, 1))
                v.wait_ge(std_ready, n + 1)
                newton(stat[:, 32:32 + cols], stat[:, 8:8 + cols], stat[:, 16:16 + cols], stat[:, 40:40 + cols])

            def scale_tile(t):
                return v.tensor_scalar(diag[:, t], ident, stat[:, 32 + t:33 + t], None, ALU.mult)

            def xt_lo(stage, n, t, q):
                v.wait_ge(xt_hi_ready, plan.hi[stage] + n + 1)
                bk = bank_of(stage, ("xt", n))
                if t < NT:
                    d = (slice(0, P), slice(4 * q, 4 * q + 4), slice(t * P, (t + 1) * P))
                    v.tensor_tensor(xl[d], bk[:, :].rearrange("p (k n) -> p k n", n=P), xh[d].bitcast(F32), ALU.subtract)\
                        .then_inc(FREE(stage, ("xt", n)), 1)
                else:
                    k = slice(8 * q, 8 * q + 8)
                    v.tensor_tensor(xs[:, k, NS:2 * NS], bk[:, :].rearrange("p (k n) -> p k n", n=NS), xs[:, k, 0:NS].bitcast(F32),
                                    ALU.subtract).then_inc(FREE(stage, ("xt", n)), 1)

            def xt_tile(stage, n0, t):
                for q in range(4 if t < NT else 2):
                    xt_lo(stage, n0 + q, t, q)

            def norm(stage):
                for t in ALL:
                    scale_tile(t).then_inc(xn_ready, 1)
                v.drain()
                for t in ALL:
                    xt_tile(stage, 4 * t, t)

            def sample_sum(dst, bk, ins_sem, width=CW):
                do(v.tensor_copy(dst, bk[0:NS, 0:width]))
                do(v.tensor_tensor(dst, bk[NS:2 * NS, 0:width], dst, ALU.add).then_inc(ins_sem, 1))

            v.memset(sq[:, :, :], 0.0)
            v.memset(stat[:, 0:88], 1.0).then_inc(stat_zero, 1)
            for b in range(8):
                v.memset(bn[:, b:b + 1], 0.0).then_inc(free[b], 1)
            v.drain()
            rms_scales(plan.st["mem"], 2, 2)
            v.wait_ge(g_in, 16)
            for m in range(2):
                do(scale_tile(m))
            for l in range(2):
                if l == 1:
                    v.wait_ge(g_in, 32)
                for m in range(2):
                    if l == 1:
                        v.wait_ge(*is_full("mem", ("xt", 4 * m + 3)))
                    do(v.tensor_tensor(memG[:, m], memX[:, m], gbc, ALU.mult).then_inc(xn_ready, 1))
                for m in range(2):
                    for q in range(4):
                        xt_lo("mem", 8 * l + 4 * m + q, 2 * l + m, q)
            rms_scales(plan.st["n0"], 7, 5)
            v.wait_ge(g_in, 48)
            for t in range(NT):
                do(v.tensor_tensor(xg[:, t], X[:, t], gbc, ALU.mult))
            for t in range(NT):
                scale_tile(t).then_inc(xn_ready, 1)
            v.drain()
            for t in ALL:
                if t == 2:
                    for n in range(2):
                        v.wait_ge(mem_stored[n], 64)
                    v.tensor_tensor(xg[0:NS, NT], X[0:NS, NT], gbc[0:NS], ALU.mult)
                    do(scale_tile(NT))
                    do(v.tensor_copy(stat[0:NS, 88:89], stat[0:NS, 0:1]).then_inc(xn_ready, 1))
                xt_tile("n0", 4 * t, t)

            do(v.memset(wsTs, 0.0).then_inc(ws_zeroed, 1))
            base = plan.groups["even"]
            for ch in range(3):
                v.wait_ge(w_used, Lin(base + GPC * ch).at(GPC))
                f = FREE("kvq", (ch, NT))
                if ch == 0:
                    sample_sum(KV[0:NS, NT], bank[NT], f, 256)
                else:
                    z = Z[0:NS, NT, 0:AW].rearrange("p (g k d) -> p k g d", g=AG, k=2)[:, ch - 1]
                    do(v.tensor_copy(z, bank[NT][0:NS, :].rearrange("p (g d) -> p g d", d=AD)))
                    do(v.tensor_tensor(z, bank[NT][NS:2 * NS, :].rearrange("p (g d) -> p g d", d=AD), z, ALU.add))
                    do(v.tensor_scalar(z, z, AD ** -0.5, None, ALU.mult).then_inc(f, 1))
            v.wait_ge(small_in, 16 * (3 + DEC_B * (BG + 1) + AH))
            for g in range(BG):
                ins = v.tensor_tensor(wraw[:, g], wraw[:, g], C("tril"), ALU.mult)
            do(ins.then_inc(ws_ready, 1))
            for g in range(BG):
                do(v.tensor_tensor(wsTs[0:NS, g], wsTs[0:NS, g], C("smask", NS), ALU.mult))
            for t in range(NT):
                v.wait_ge(*is_drained("kvq", (2, t)))
            v.wait_ge(*is_drained("epre", "qTs"))
            v.wait_ge(*is_drained("epre", "kT"))

            slope, dist = C("slope"), C("dist")

            def e_stage(stage, j, i):
                v.wait_ge(*was_full(stage, "qT", i))
                src = Z[:, 0:NT, 0:AW].rearrange("p t (k n) -> p t k n", k=2)[:, :, :, bass.ds(AD * j, AD)]
                v.tensor_copy(qst.rearrange("p t (k d) -> p t k d", k=2), src)
                do(v.tensor_copy(qs, qTs[:, j]).then_inc(q_staged, 1))

            def window_step(stage, j, i, name):
                kind = name.rstrip("0123")
                b = int(name[-1]) if kind in ("QK", "RD", "PV") else 0
                if kind == "QK":
                    v.wait_ge(*is_full(stage, name, i))
                    bk = bank_of(stage, name)
                    v.wait_ge(*was_full(stage, f"pT{b}", i))
                    ks = 0 if b else P
                    for kv in range(2):
                        ins = v.scalar_tensor_tensor(S[:, kv, ks:256], dist[:, ks:256], slope[:, bass.ds(AG * kv + j, 1)],
                                                     bk[:, kv * 256 + ks:kv * 256 + 256], ALU.mult, ALU.add)
                    ins.then_inc(FREE(stage, name), 1)
                    do(v.tensor_copy(S[:, :, 256:257], sinkb.rearrange("p (k g) -> p k g", k=2)[:, :, bass.ds(j, 1)]))
                    do(v.tensor_reduce(stat[:, 30:32], S[:, :, ks:257], AXX, ALU.max))
                    do(v.tensor_scalar(stat[:, 24:26], stat[:, 30:32], -1.0, None, ALU.mult).then_inc(neg_ready, 1))
                elif kind == "LN":
                    n = int(name[-1])
                    layer_norm(2 * i + (n + 1), 2 * i + n, P)
                elif kind == "RD":
                    v.wait_ge(p_ready, 4 * j + (b + 1))
                    do(v.reciprocal(rden[:, b % 2], stat[:, 26:28]))
                elif kind == "PV":
                    v.wait_ge(*is_full(stage, name, i))
                    bk = bank_of(stage, name)
                    at = bass.ds(AD * j, AD)
                    dst = Z[:, b, 0:AW].rearrange("p (k n) -> p k n", k=2)[:, :, at]
                    if stage in ("pair0", "pair1"):
                        do(v.tensor_tensor(dst, bk[:, 0:P].rearrange("p (k d) -> p k d", k=2),
                                           rden[:, b % 2].unsqueeze(2).to_broadcast([P, 2, AD]), ALU.mult).then_inc(FREE(stage, name), 1))
                    else:
                        gate = SG[:, b].rearrange("p (k n) -> p k n", k=2)[:, :, at]
                        for kv in range(2):
                            ins = v.scalar_tensor_tensor(dst[:, kv], bk[:, kv * AD:(kv + 1) * AD], rden[:, b % 2, kv:kv + 1],
                                                         gate[:, kv], ALU.mult, ALU.mult)
                        ins.then_inc(FREE(stage, name), 1)
                        v.drain()
                elif kind == "Ss":
                    v.wait_ge(*is_full(stage, name, i))
                    bk = bank_of(stage, name)
                    v.tensor_tensor(Ss[:, 0:WIN], bk[:, 0:WIN], C("sbias"), ALU.add)
                    o = COFF["strip"][0] + 56
                    v.tensor_tensor(Ss[:, WIN:WIN + NS], bk[:, WIN:WIN + NS], cst[:, bass.ds(o - DEC_T * j, NS)], ALU.add)\
                        .then_inc(FREE(stage, name), 1)
                    do(v.tensor_copy(Ss[:, 192:193], sinkr))
                    do(v.tensor_reduce(stat[:, 37:38], Ss[:, 0:193], AXX, ALU.max))
                    do(v.tensor_scalar(stat[:, 28:29], stat[:, 37:38], -1.0, None, ALU.mult).then_inc(sneg_ready, 1))
                elif kind == "Sr":
                    v.wait_ge(sexp_done, j + 1)
                    do(v.reciprocal(stat[:, 38:39], stat[:, 29:30]))
                    do(v.tensor_scalar(Ss[:, 0:192], Ss[:, 0:192], stat[:, 38:39], None, ALU.mult).then_inc(sp_ready, 1))

            def layer_norm(n, t, r):
                z = Z[0:r, bass.ds(t, 1), AW:D].rearrange("p a (b n) -> p (a b) n", b=2) if not isinstance(t, int) else \
                    Z[0:r, t, AW:D].rearrange("p (b n) -> p b n", b=2)
                for q in range(2):
                    v.bn_stats(bn[0:r, 6 * q:6 * q + 6], z[:, q])
                v.drain()
                do(v.bn_aggr(stat[0:r, 70:72], bn[0:r, :]))
                do(v.tensor_scalar(stat[0:r, 35:36], stat[0:r, 71:72], EPS, None, ALU.add).then_inc(var_ready, 1))
                v.wait_ge(std_ready, plan.st["ln"] + 1 + n)
                newton(stat[0:r, 34:35], stat[0:r, 35:36], stat[0:r, 36:37], stat[0:r, 32:33])
                do(v.tensor_scalar(z, z, stat[0:r, 70:71], stat[0:r, 34:35], ALU.subtract, ALU.mult))
                do(v.tensor_tensor(z, z, lng[0:r], ALU.mult))
                do(v.tensor_tensor(z, z, lnb[0:r], ALU.add).then_inc(vn_ready, 1))

            def gate_mul(stage, tag, i, n, L, dst, buf, sbuf):
                for t in range(NT):
                    v.wait_ge(*is_drained(stage, (tag, t), i))
                    d = dst(t)
                    do(v.tensor_tensor(d, d, buf[:, t % 2], ALU.mult).then_inc(gated, 1))
                v.wait_ge(w_used, L.at(GPC))
                sample_sum(sbuf[0:NS, :], bank[NT], FREE(stage, (tag, NT)))
                v.wait_ge(sil_ready, n + 1)
                d = dst(NT)
                do(v.tensor_tensor(d, d, sbuf[0:NS, :], ALU.mult).then_inc(gated, 1))

            for pair in range(4):
                stage = f"pair{pair}"
                if pair == 2:
                    for q in range(2):
                        v.wait_ge(*is_drained("mixv", (NT, q)))
                    for t in range(NT):
                        v.wait_ge(*is_drained("pair1", ("acc", t), 1))
                        first = (slice(0, P), slice(0, 2), slice(0, 4 * AD))
                        z, gate = (a.rearrange("p (k n) -> p k n", k=2)[first] for a in (Z[:, t, 0:AW], SG[:, t]))
                        v.tensor_tensor(z, z, gate, ALU.mult)
                    v.drain()
                with v.Fori(0, 2) as i:
                    j = 2 * pair + i
                    e_stage(stage, j, i)
                    tasks = sorted([(p, n) for p, n in E_POINTS if n not in ("qT", "Kb")] + [(14, "Sr")] +
                                   [(12 + 8 * b, f"RD{b}") for b in range(NT)])
                    if pair == 1:
                        tasks = sorted(tasks + [(p + 0.5, f"LN{LN_AFTER.index(n)}") for p, n in tasks if n in LN_AFTER])
                    for _, n in tasks:
                        window_step(stage, j, i, n)
                    L = Lin(base + GPC * (3 + 2 * pair), GPC, i)
                    cols = bass.ds(AW + CW * i, CW)
                    if pair == 0:
                        v.wait_ge(w_used, L.at(GPC))
                        sample_sum(Z[0:NS, NT, cols], bank[NT], FREE(stage, ("acc", NT)))
                    elif pair == 1:
                        v.wait_ge(w_used, L.at(GPC))
                        sample_sum(SG[0:NS, NT, bass.ds(CW * i, CW)], bank[NT], FREE(stage, ("acc", NT)))
                    elif pair == 2:
                        for t in range(NT):
                            v.wait_ge(*is_full(stage, ("acc", t), i))
                            bk = bank_of(stage, ("acc", t))
                            do(v.tensor_tensor(Z[:, t, cols], bk[:, :], Z[:, t, cols], ALU.mult).then_inc(FREE(stage, ("acc", t)), 1))
                        v.wait_ge(w_used, L.at(GPC))
                        sample_sum(sils[0:NS, :], bank[NT], FREE(stage, ("acc", NT)))
                        do(v.tensor_tensor(Z[0:NS, NT, cols], Z[0:NS, NT, cols], sils[0:NS, :], ALU.mult))
                    else:
                        gate_mul(stage, "acc", i, i, L, lambda t: Z[0:rows(t), t, cols], sil, sils)
                if pair == 0:
                    for t in range(NT):
                        v.wait_ge(*is_drained(stage, ("acc", t), 1))
                    v.wait_ge(ln_in, 32)
                    layer_norm(0, NT, NS)
            v.wait_ge(sg_ready, 2)
            zs = Z[0:NS, NT, 0:AW].rearrange("p (k g d) -> p g k d", k=2, d=AD)
            gs = SG[0:NS, NT].rearrange("p (k g d) -> p g k d", k=2, d=AD)
            for n in range(2):
                v.wait_ge(*is_full("epost", f"o{n}"))
                bk = bank_of("epost", f"o{n}")
                g = slice(4 * n, 4 * n + 4)
                do(v.tensor_tensor(zs[:, g], bk[0:NS, :].rearrange("p (g k d) -> p g k d", g=4, k=2), gs[:, g], ALU.mult)
                   .then_inc(FREE("epost", f"o{n}"), 1))
            do(v.tensor_copy(stat[0:NS, 88:89], stat[0:NS, 0:1]).then_inc(z_ready, 1))
            for t in ALL:
                xt_tile("zt", 4 * t, t)

            def residual(stage, tag, i, L, cols, groups, gained=False):
                for t in ALL:
                    r = rows(t)
                    x = X[0:r, t, cols]
                    if t < NT:
                        v.wait_ge(*is_full(stage, (tag, t), i))
                    else:
                        v.wait_ge(w_used, L.at(groups))
                        do(v.tensor_tensor(x, bank[NT][NS:2 * NS, :], x, ALU.add))
                    do(v.tensor_tensor(x, bank[t][0:r, :], x, ALU.add).then_inc(FREE(stage, (tag, t)), 1))
                    if gained:
                        do(v.tensor_tensor(xg[0:r, t, cols], x, gbc[0:r, cols], ALU.mult))

            def x_complete():
                do(v.tensor_copy(stat[0:NS, 88:89], stat[0:NS, 0:1]).then_inc(x_done, 1))

            v.wait_ge(x_in, 160)
            v.wait_ge(g_in, 64)
            with v.Fori(0, 4) as i:
                residual("eout", "acc", i, Lin(plan.groups["eout"], GPC, i), bass.ds(CW * i, CW), GPC, True)
            x_complete()

            def cross(l):
                st = f"x{l}"
                rms_scales(plan.st[st], 27 + 40 * l, 5)
                norm(st)
                v.wait_ge(w_used, Lin(plan.groups[st + "q"]).at(GPC))
                sample_sum(qc[0:NS, NT], bank[NT], FREE(st, ("acc", NT)))
                scale = XD ** -0.5

                def neg(t):
                    for q in range(2):
                        v.wait_ge(*is_full(st, f"S{t}{q}"))
                        bk = bank_of(st, f"S{t}{q}")
                        do(v.tensor_reduce(stat[:, 64 + 2 * q:66 + 2 * q], bk[:, :].rearrange("p (h n) -> p h n", n=MEM), AXX, ALU.max))
                    do(v.tensor_scalar(stat[:, 56 + 4 * (t % 2):60 + 4 * (t % 2)], stat[:, 64:68], -scale, None, ALU.mult).then_inc(cneg, 1))

                neg(0)
                for t in range(NT):
                    if t + 1 < NT:
                        neg(t + 1)
                    for q in range(2):
                        v.wait_ge(*is_drained(st, f"S{t}{q}"))
                    do(v.reciprocal(stat[:, 80:84], stat[:, 48 + 4 * (t % 2):52 + 4 * (t % 2)]))
                    v.wait_ge(*is_full(st, f"pT{t}1"))
                    bk = bank_of(st, f"pT{t}1")
                    do(v.tensor_copy(cpT[:, 4:8], bk[:, :].rearrange("p (a n) -> p a n", n=P)).then_inc(FREE(st, f"pT{t}1"), 1))
                    v.wait_ge(*is_full(st, f"PV{t}"))
                    bk = bank_of(st, f"PV{t}")
                    do(v.tensor_tensor(Ox.rearrange("p (h n) -> p h n", n=P), bk[:, :].rearrange("p (h n) -> p h n", n=P),
                                       stat[:, 80:84].unsqueeze(2).to_broadcast([P, XH, P]), ALU.mult).then_inc(FREE(st, f"PV{t}"), 1))
                    v.wait_ge(xt_hi_ready, plan.hi[st + "o"] + t + 1)
                    d = (slice(0, P), slice(0, XH), slice(t * P, (t + 1) * P))
                    do(v.tensor_tensor(xl[d], bank[4][:, :].rearrange("p (h n) -> p h n", n=P), xh[d].bitcast(F32), ALU.subtract)
                       .then_inc(FREE(st, f"oT{t}"), 1))
                do(v.memset(cqz, 0.0))
                v.wait_ge(*is_drained(st, f"qT{NT}"))
                for b in range(DEC_B):
                    at = slice(b * DEC_T, (b + 1) * DEC_T)
                    ins = v.tensor_copy(cqz[:, :, b, at], cqT[:, :, SEQ + b * DEC_T:SEQ + (b + 1) * DEC_T])
                do(ins.then_inc(cqz_ready, 1))
                for b in range(DEC_B):
                    v.wait_ge(*is_full(st, f"K{b}1"))
                    bk = bank_of(st, f"K{b}1")
                    if b >= 2:
                        v.wait_ge(kT_used, 6 * l + b - 1)
                    do(v.tensor_copy(kTb[b % 2][:, :, P:2 * P], bk[:, :].rearrange("p (h n) -> p h n", n=P)).then_inc(FREE(st, f"K{b}1"), 1))
                v.wait_ge(*is_full(st, "SS"))
                bk = bank_of(st, "SS")
                do(v.tensor_reduce(stat[:, 64:66], bk[:, :].rearrange("p (h n) -> p h n", n=MEM), AXX, ALU.max))
                do(v.tensor_scalar(stat[:, 56:58], stat[:, 64:66], -scale, None, ALU.mult).then_inc(cneg, 1))
                v.wait_ge(*is_drained(st, "SS"))
                do(v.reciprocal(stat[:, 80:82], stat[:, 48:50]))
                do(v.tensor_scalar(Px[:, 0], Px[:, 0], stat[:, 80:81], None, ALU.mult))
                do(v.tensor_scalar(Px[:, 1], Px[:, 1], stat[:, 81:82], None, ALU.mult).then_inc(cross_sp, 1))
                v.wait_ge(*is_full(st, "PR"))
                pr = bank_of(st, "PR")[:, :].rearrange("p (a n) -> p a n", n=NS)
                do(v.memset(cpz, 0.0))
                for b in range(DEC_B):
                    at = slice(b * DEC_T, (b + 1) * DEC_T)
                    if b >= 2:
                        v.wait_ge(vb_used, 7 * l + b - 1)
                        v.memset(cpz[:, b % 2, :, at.start - 2 * DEC_T:at.stop - 2 * DEC_T], 0.0)
                    v.tensor_copy(cpz[:, b % 2, :, at], pr[:, :, at]).then_inc(cpz_ready, 1)
                do(v.tensor_copy(stat[:, 88:89], stat[:, 0:1]).then_inc(FREE(st, "PR"), 1))
                v.wait_ge(xt_hi_ready, plan.hi[st + "o"] + 5)
                do(v.tensor_tensor(xs[:, 0:XH, NS:2 * NS], bank_of(st, "oS")[:, 0:XH * NS].rearrange("p (h n) -> p h n", n=NS),
                                   xs[:, 0:XH, 0:NS].bitcast(F32), ALU.subtract).then_inc(FREE(st, "oS"), 1))
                v.wait_ge(g_in, 80 + 32 * l)
                for n in range(4):
                    residual(st + "o", n, 0, Lin(plan.groups[st + "o"] + 2 * n), slice(CW * n, CW * (n + 1)), 2, True)
                x_complete()

            cross(0)
            rms_scales(plan.st["n1"], 47, 5)
            norm("n1")
            v.wait_ge(x_saved, 80)
            v.wait_ge(zm_in, 16)
            base = plan.groups["ret"]
            v.wait_ge(w_used, Lin(base).at(GPC))
            sample_sum(QK[0:NS, NT], bank[NT], FREE("retA", ("acc", NT)))
            qd, qd2, kd, kz, gp = C("qd"), C("qd2"), C("kd"), C("kz"), C("gp")

            def double_keys():
                v.tensor_copy(QK[NS:2 * NS, NT, RK:2 * RK], QK[0:NS, NT, RK:2 * RK])
                v.drain()

            def values_step(stage, h, i, name):
                if name[0] == "S":
                    c = int(name[2])
                    r = rows(c)
                    if c == 0:
                        v.wait_ge(rd_in, 16 * h + 16)
                    v.wait_ge(*is_full(stage, name, i))
                    bk = bank_of(stage, name)
                    dec = rdec[:, 0:P] if c < NT else rdec[0:NS, P:P + NS]
                    do(v.tensor_tensor(STm[0:r, c, 0:r], bk[0:r, 0:r], dec, ALU.mult).then_inc(FREE(stage, name), 1))
                elif name == "T4":
                    v.wait_ge(*is_drained(stage, name, i))
                    for k in range(2):
                        ins = v.tensor_tensor(qz[:, k], qkT[:, k, SEQ:SEQ + NS].unsqueeze(1).to_broadcast([P, DEC_B, NS]), zm, ALU.mult)
                    do(ins.then_inc(qz_ready, 1))

            def decayed_keys(h, c):
                do(v.tensor_scalar(kdec[:, c % 2], QK[:, c, RK:2 * RK], kd[:, bass.ds(h, 1)], None, ALU.mult).then_inc(kdec_ready, 1))

            def batch_keys(h, b):
                keys, col = QK[:, NT, RK:2 * RK], kz[:, bass.ds(DEC_B * h + b, 1)]
                do(v.tensor_scalar(kzb[:, b % 2, 0:RK], keys, col, None, ALU.mult))
                do(v.scalar_tensor_tensor(kzb[:, b % 2, RK:2 * RK], keys, col, kzb[:, b % 2, 0:RK].bitcast(F32), ALU.mult, ALU.subtract)
                   .then_inc(kz_ready, 1))

            def group_norm(h, c, bk, sem_free):
                r = rows(c)
                col = bass.ds(h, 1) if c < NT else bass.ds(h + RH, 1)
                do(v.bn_stats(bn[0:r, 0:6], bk[0:r, :]))
                do(v.bn_aggr(stat[0:r, 82:84], bn[0:r, 0:6]))
                do(v.tensor_scalar(stat[0:r, 65:66], stat[0:r, 83:84], qd2[0:r, col], EPS, ALU.mult, ALU.add).then_inc(var_ready, 1))
                v.wait_ge(std_ready, plan.st["gn"] + 1 + 5 * h + c)
                newton(stat[0:r, 84:85], stat[0:r, 65:66], stat[0:r, 66:67], stat[0:r, 85:86])
                do(v.tensor_scalar(stat[0:r, 84:85], stat[0:r, 84:85], qd[0:r, col], None, ALU.mult))
                do(v.tensor_scalar(ON[0:r, c], bk[0:r, :], stat[0:r, 82:83], stat[0:r, 84:85], ALU.subtract, ALU.mult).then_inc(sem_free, 1))

            def gates_step(stage, h, i, name):
                if name[0] == "O":
                    if name[1] == "I":
                        return
                    c = int(name[1])
                    v.wait_ge(*is_full(stage, name, i))
                    group_norm(h, c, bank_of(stage, name), FREE(stage, name))
                elif name[0] == "U":
                    c, m = int(name[1]), int(name[2])
                    v.wait_ge(*is_full(stage, name, i))
                    bk = bank_of(stage, name)
                    if c == 0:
                        do(v.tensor_copy(rstate[:, m], bk[:, :]).then_inc(FREE(stage, name), 1))
                    else:
                        do(v.scalar_tensor_tensor(rstate[:, m], rstate[:, m], gp[:, bass.ds(h, 1)], bk[:, :], ALU.mult, ALU.add)
                           .then_inc(FREE(stage, name), 1))
                    if m == 1 and c + 2 < NT:
                        decayed_keys(h, c + 2)
                else:
                    b, m = int(name[1]), int(name[2])
                    v.wait_ge(*is_full(stage, name, i))
                    bk = bank_of(stage, name)
                    do(v.scalar_tensor_tensor(Wst[:, b % 4, m], Wst[:, b % 4, m], gp[:, bass.ds(h + RH, 1)], bk[:, :], ALU.mult, ALU.add)
                       .then_inc(FREE(stage, name), 1))
                    if m == 1 and b + 2 < DEC_B:
                        batch_keys(h, b + 2)

            def split_mix(half, g):
                k = slice(GK * g, GK * g + GK)
                v.wait_ge(mix_hi, GPC * half + g + 1)
                v.tensor_tensor(xh[:, k, :], xh[:, k, :].bitcast(F32), xl[:, k, :].bitcast(F32), ALU.subtract)
                do(v.tensor_tensor(xs[:, k, NS:2 * NS], xs[:, k, NS:2 * NS].bitcast(F32), xs[:, k, 0:NS].bitcast(F32), ALU.subtract)
                   .then_inc(mix_ready, 1))

            def head(stage, h, i, L):
                for _, n in RB_POINTS:
                    values_step(stage, h, i, n)
                decayed_keys(h, 0)
                decayed_keys(h, 1)
                batch_keys(h, 0)
                batch_keys(h, 1)
                v.wait_ge(w_used, L.at(GPC))
                sample_sum(V[0:NS, NT], bank[NT], FREE(stage, ("B", NT)))
                do(v.tensor_copy(Vx[0:NS], V[0:NS, NT]))
                do(v.tensor_tensor(Vx[NS:2 * NS], V[0:NS, NT], Vx[0:NS].bitcast(F32), ALU.subtract).then_inc(vx_ready, 1))
                for _, n in RC_DRAINS:
                    gates_step(stage, h, i, n)
                if stage == "retZ":
                    for g in range(GPC - 3):
                        split_mix(0, g)
                v.wait_ge(*is_full(stage, "OI", i))
                group_norm(h, NT, bank_of(stage, "OI"), FREE(stage, "OI"))
                gate_mul(stage, "C", i, 2 + h, Lin(L.c + GPC, L.k, L.i), lambda t: ON[0:rows(t), t], sg, sgs)

            double_keys()
            with v.Fori(0, RH - 1) as h:
                for t in range(NT):
                    v.wait_ge(*is_free("ret", ("B", t), h))
                head("ret", h, h, Lin(base + GPC, 3 * GPC, h))
                v.wait_ge(w_used, Lin(base + 3 * GPC, 3 * GPC, h).at(GPC))
                sample_sum(QK[0:NS, NT], bank[NT], FREE("ret", ("A", NT)))
                double_keys()
                v.wait_ge(rstate_out, 16 * h + 16)
            h = RH - 1
            for t in range(NT):
                v.wait_ge(*is_free("retZ", ("B", t)))
            head("retZ", h, 0, Lin(base + GPC + 3 * GPC * h))
            for g in range(GPC - 3, GPC):
                split_mix(0, g)
            v.wait_ge(x_in, 240)
            base = plan.groups["rout"]
            with v.Fori(0, 3) as i:
                residual("rout", "acc", i, Lin(base, GPC, i), bass.ds(CW * i, CW), GPC)
            for g in range(GPC - 2):
                split_mix(1, g)
            residual("rout", "acc", 3, Lin(base + 3 * GPC), slice(3 * CW, 4 * CW), GPC)
            for g in (GPC - 2, GPC - 1):
                split_mix(1, g)
            v.wait_ge(g_in, 96)
            with v.Fori(0, 4) as i:
                residual("rout", "acc", i + 4, Lin(base + 4 * GPC, GPC, i), bass.ds(CW * i, CW), GPC, True)
            x_complete()
            cross(1)
            rms_scales(plan.st["fin"], 87, 5)
            do(v.tensor_copy(stat[0:NS, 88:89], stat[0:NS, 0:1]).then_inc(xn_ready, 1))
            for t in (0, 2, 4):
                r = rows(t)
                do(v.tensor_scalar(xg[0:r, t], xg[0:r, t], stat[0:r, 32 + t:33 + t], None, ALU.mult).then_inc(y_vec, 1))


_INS = ["x_prompt", "x_sample", "cache_win_k", "cache_win_v", "state_ret", "cache_mem_k", "cache_mem_v", "mem_prompt",
        "norm_mix", "w_in_even", "attn_sinks", "w_spatial", "b_spatial", "norm_v_g", "norm_v_b", "w_out_even",
        "w_in_ret", "w_out_ret", "norm_cross", "norm_mem", "w_xq", "w_xk", "w_xv", "w_xo", "norm_final"]
_OUTS = [("y_prompt", (1, SEQ, D)), ("y_sample", (DEC_B, DEC_T, D)),
         ("win_k_prompt", (1, 1, WIN, 2, AD)), ("win_v_prompt", (1, 1, WIN, 2, AD)),
         ("ret_state_prompt", (1, 1, RH, RK, RV)),
         ("mem_k_prompt", (2, 1, MEM, XH, XD)), ("mem_v_prompt", (2, 1, MEM, XH, XD)),
         ("win_k_sample", (1, DEC_B, WIN, 2, AD)), ("win_v_sample", (1, DEC_B, WIN, 2, AD)),
         ("ret_state_sample", (1, DEC_B, RH, RK, RV)), ("chunk_v", (1, DEC_B, DEC_T, BW))]


def kernel(**inputs):
    import numpy as _np
    import concourse.bacc as _bacc
    from concourse.bass_utils import run_bass_kernel_spmd as _run

    nc = _bacc.Bacc("TRN2", target_bir_lowering=False, num_devices=1, dynamic_dma_scratch_size=1024)
    arrays, I, O = {}, Bag(), Bag()
    given = {n: _np.ascontiguousarray(inputs[n]) for n in _INS}
    I.x_prompt, I.x_sample, I.cache_win_k, I.cache_win_v, I.state_ret, I.cache_mem_k, I.cache_mem_v, I.mem_prompt, \
        I.norm_mix, I.w_in_even, I.attn_sinks, I.w_spatial, I.b_spatial, I.norm_v_g, I.norm_v_b, I.w_out_even, \
        I.w_in_ret, I.w_out_ret, I.norm_cross, I.norm_mem, I.w_xq, I.w_xk, I.w_xv, I.w_xo, I.norm_final = [
            nc.dram_tensor(f"in_{n}", given[n].shape, F32, kind="ExternalInput").ap() for n in _INS]
    for n in _INS:
        arrays[f"in_{n}"] = given[n]
    c, rdec, zmask = shape_constants()
    aps = []
    for name, a in (("consts", c), ("ret_decay", rdec), ("batch_mask", zmask)):
        arrays[name] = a
        aps.append(nc.dram_tensor(name, a.shape, F32, kind="ExternalInput").ap())
    O.y_prompt, O.y_sample, O.win_k_prompt, O.win_v_prompt, O.ret_state_prompt, O.mem_k_prompt, O.mem_v_prompt, \
        O.win_k_sample, O.win_v_sample, O.ret_state_sample, O.chunk_v = [
            nc.dram_tensor(f"out_{n}", shape, F32, kind="ExternalOutput").ap() for n, shape in _OUTS]
    x_scratch = nc.dram_tensor("x_scratch", (SEQ + NS, D), F32).ap()
    mix_scratch = nc.dram_tensor("mix_scratch", (2 * KT, P, SEQ + NS), F32).ap()
    build(nc, I, O, *aps, x_scratch, mix_scratch)
    r = _run(nc, [arrays], core_ids=[0])
    return tuple(r.results[0][f"out_{n}"] for n, _ in _OUTS)
```
